# Optimizing a Trainium2 kernel written in Bass

```python
import jax
import jax.numpy as jnp
from jax import lax
import numpy as np
import math
import jax, jax.numpy as jnp

D_MODEL = 1024
BATCH = 1
SEQ = 256
DEPTH = 2

HEAD_DIM = 64
N_HEADS = D_MODEL // HEAD_DIM
SB_HEADS = N_HEADS // 2
NSA_HEADS = N_HEADS - SB_HEADS
NSA_KV_GROUPS = 2
FOX_HEADS = N_HEADS
CMP_LEN = 32
CMP_STRIDE = 16
SEL_LEN = 64
SEL_TOP = 16
WINDOW = 512
N_BRANCH = 3
Q_BLOCK = 128
ROPE_THETA = 500000.0
ROT_DIM = HEAD_DIM // 4
D_FF = 256 * ((8 * D_MODEL // 3 + 255) // 256)
CONV_WIDTH = 3
NORM_EPS = 1e-6
N_EVEN = (DEPTH + 1) // 2
N_ODD = DEPTH // 2
SB_W = SB_HEADS * HEAD_DIM
NSA_QW = NSA_HEADS * HEAD_DIM
NSA_KVW = NSA_KV_GROUPS * HEAD_DIM
EVEN_SPLITS = (SB_W, SB_W, SB_W, NSA_QW) + (NSA_KVW,) * 6 + (NSA_HEADS * N_BRANCH,)
EVEN_IN = sum(EVEN_SPLITS)
FOX_W = FOX_HEADS * HEAD_DIM
ODD_SPLITS = (FOX_W, FOX_W, FOX_W, FOX_HEADS)
ODD_IN = sum(ODD_SPLITS)


def rmsnorm(x, g):
    x32 = x.astype(jnp.float32)
    y = x32 * lax.rsqrt(jnp.mean(x32 * x32, axis=-1, keepdims=True) + NORM_EPS)
    return y.astype(x.dtype) * g

def split_cols(h, sizes):
    offs = np.cumsum(sizes)[:-1].tolist()
    return jnp.split(h, offs, axis=-1)

def partial_rope(x, pos):
    half = ROT_DIM // 2
    inv_freq = ROPE_THETA ** (-(jnp.arange(half, dtype=jnp.float32) * 2.0 / ROT_DIM))
    ang = pos[:, None] * inv_freq[None, :]
    cos = jnp.cos(ang)[None, :, None, :].astype(x.dtype)
    sin = jnp.sin(ang)[None, :, None, :].astype(x.dtype)
    x1 = x[..., :half]
    x2 = x[..., half:ROT_DIM]
    return jnp.concatenate([x1 * cos - x2 * sin, x1 * sin + x2 * cos, x[..., ROT_DIM:]], axis=-1)

def masked_softmax(s, mask):
    s = jnp.where(mask, s, -jnp.inf)
    m = jnp.max(s, axis=-1, keepdims=True)
    m = jnp.where(jnp.isfinite(m), m, 0.0)
    e = jnp.where(mask, jnp.exp(s - m), 0.0)
    d = jnp.sum(e, axis=-1, keepdims=True)
    return e / jnp.where(d > 0, d, 1.0)

def sweep_query_blocks(fn, seq):
    out = lax.map(fn, jnp.arange(seq // Q_BLOCK))
    nb, bsz, q, nh, dh = out.shape
    return jnp.moveaxis(out, 0, 1).reshape(bsz, nb * q, nh, dh)

def stick_breaking_attention(q, k, v):
    bsz, seq, nh, dh = q.shape
    scale = dh ** -0.5
    kpos = jnp.arange(seq)

    def block(i):
        q0 = i * Q_BLOCK
        qb = lax.dynamic_slice_in_dim(q, q0, Q_BLOCK, axis=1)
        tpos = q0 + jnp.arange(Q_BLOCK)
        z = jnp.einsum('bqhd,bshd->bhqs', qb, k, preferred_element_type=jnp.float32) * scale
        mask = kpos[None, :] < tpos[:, None]
        log_keep = jnp.where(mask, jax.nn.log_sigmoid(-z), 0.0)
        after = lax.cumsum(log_keep, axis=3, reverse=True) - log_keep
        a = jnp.where(mask, jnp.exp(jax.nn.log_sigmoid(z) + after), 0.0)
        return jnp.einsum('bhqs,bshd->bqhd', a.astype(v.dtype), v)

    return sweep_query_blocks(block, seq)

def forgetting_attention(q, k, v, log_f):
    bsz, seq, nh, dh = q.shape
    scale = dh ** -0.5
    kpos = jnp.arange(seq)
    cum = jnp.transpose(jnp.cumsum(log_f, axis=1), (0, 2, 1))

    def block(i):
        q0 = i * Q_BLOCK
        qb = lax.dynamic_slice_in_dim(q, q0, Q_BLOCK, axis=1)
        cq = lax.dynamic_slice_in_dim(cum, q0, Q_BLOCK, axis=2)
        tpos = q0 + jnp.arange(Q_BLOCK)
        s = jnp.einsum('bqhd,bshd->bhqs', qb, k, preferred_element_type=jnp.float32) * scale
        s = s + (cq[..., :, None] - cum[..., None, :])
        p = masked_softmax(s, kpos[None, :] <= tpos[:, None])
        return jnp.einsum('bhqs,bshd->bqhd', p.astype(v.dtype), v)

    return sweep_query_blocks(block, seq)

def nsa_attention(q, k_cmp, v_cmp, k_slc, v_slc, k_win, v_win, gates, pos_k, pos_v, w_ck, w_cv):
    bsz, seq, nh, dh = q.shape
    ng = k_cmp.shape[2]
    rep = nh // ng
    scale = dh ** -0.5
    n_cmp = (seq - CMP_LEN) // CMP_STRIDE + 1
    c_start = jnp.arange(n_cmp) * CMP_STRIDE
    cidx = c_start[:, None] + jnp.arange(CMP_LEN)[None, :]

    def compress(t, pe, w):
        blocks = t[:, cidx] + pe[None, None, :, None, :]
        blocks = jnp.moveaxis(blocks, 3, 2).reshape(bsz, n_cmp, ng, CMP_LEN * dh)
        return blocks @ w

    cmp_end = c_start + CMP_LEN - 1
    kc = partial_rope(compress(k_cmp, pos_k, w_ck), cmp_end.astype(jnp.float32))
    vc = compress(v_cmp, pos_v, w_cv)
    n_sel = seq // SEL_LEN
    top = min(SEL_TOP, n_sel)
    ks = k_slc.reshape(bsz, n_sel, SEL_LEN, ng, dh).transpose(0, 3, 1, 2, 4)
    vs = v_slc.reshape(bsz, n_sel, SEL_LEN, ng, dh).transpose(0, 3, 1, 2, 4)
    sel_start = jnp.arange(n_sel) * SEL_LEN
    overlap = (c_start[:, None] < sel_start[None, :] + SEL_LEN) & (c_start[:, None] + CMP_LEN > sel_start[None, :])
    cmp_to_sel = overlap.astype(jnp.float32)
    blk = jnp.arange(n_sel)
    bi = jnp.arange(bsz)[:, None, None, None]
    gi = jnp.arange(ng)[None, :, None, None]
    kw = jnp.pad(k_win, ((0, 0), (WINDOW, 0), (0, 0), (0, 0)))
    vw = jnp.pad(v_win, ((0, 0), (WINDOW, 0), (0, 0), (0, 0)))

    def block(i):
        q0 = i * Q_BLOCK
        tpos = q0 + jnp.arange(Q_BLOCK)
        qb = lax.dynamic_slice_in_dim(q, q0, Q_BLOCK, axis=1).reshape(bsz, Q_BLOCK, ng, rep, dh)
        sc = jnp.einsum('bqgrd,bcgd->bgrqc', qb, kc, preferred_element_type=jnp.float32) * scale
        pc = masked_softmax(sc, cmp_end[None, :] <= tpos[:, None])
        o_cmp = jnp.einsum('bgrqc,bcgd->bqgrd', pc.astype(vc.dtype), vc)
        imp = jnp.einsum('bgrqc,cn->bgqn', pc, cmp_to_sel)
        cur = tpos // SEL_LEN
        causal = blk[None, :] <= cur[:, None]
        forced = (blk[None, :] == 0) | (blk[None, :] == cur[:, None]) | (blk[None, :] == cur[:, None] - 1)
        score = jnp.where(causal, jnp.where(forced, jnp.inf, imp), -jnp.inf)
        top_val, top_idx = lax.top_k(score, top)
        sel_ok = top_val > -jnp.inf
        kg = ks[bi, gi, top_idx]
        vg = vs[bi, gi, top_idx]
        kpos = top_idx[..., None] * SEL_LEN + jnp.arange(SEL_LEN)
        smask = sel_ok[..., None] & (kpos <= tpos[None, None, :, None, None])
        ss = jnp.einsum('bqgrd,bgqnld->bgrqnl', qb, kg, preferred_element_type=jnp.float32) * scale
        ps = masked_softmax(ss.reshape(bsz, ng, rep, Q_BLOCK, top * SEL_LEN),
                            smask.reshape(bsz, ng, 1, Q_BLOCK, top * SEL_LEN))
        ps = ps.reshape(bsz, ng, rep, Q_BLOCK, top, SEL_LEN)
        o_slc = jnp.einsum('bgrqnl,bgqnld->bqgrd', ps.astype(vg.dtype), vg)
        kwb = lax.dynamic_slice_in_dim(kw, q0, Q_BLOCK + WINDOW, axis=1)
        vwb = lax.dynamic_slice_in_dim(vw, q0, Q_BLOCK + WINDOW, axis=1)
        wpos = q0 - WINDOW + jnp.arange(Q_BLOCK + WINDOW)
        wmask = (wpos[None, :] >= 0) & (wpos[None, :] <= tpos[:, None]) & (wpos[None, :] > tpos[:, None] - WINDOW)
        sw = jnp.einsum('bqgrd,bkgd->bgrqk', qb, kwb, preferred_element_type=jnp.float32) * scale
        pw = masked_softmax(sw, wmask)
        o_win = jnp.einsum('bgrqk,bkgd->bqgrd', pw.astype(vwb.dtype), vwb)
        gb = lax.dynamic_slice_in_dim(gates, q0, Q_BLOCK, axis=1).reshape(bsz, Q_BLOCK, ng, rep, N_BRANCH)
        o = gb[..., 0:1] * o_cmp + gb[..., 1:2] * o_slc + gb[..., 2:3] * o_win
        return o.reshape(bsz, Q_BLOCK, nh, dh)

    return sweep_query_blocks(block, seq)

def even_mixer(h, w_in, pos_k, pos_v, w_ck, w_cv, w_out):
    bsz, seq, _ = h.shape
    sq, sk, sv, nq, kc, vc, ksl, vsl, kwn, vwn, g = split_cols(h @ w_in, EVEN_SPLITS)
    pos = jnp.arange(seq, dtype=jnp.float32)

    def heads(t):
        return t.reshape(bsz, seq, -1, HEAD_DIM)

    o_sb = stick_breaking_attention(heads(sq), heads(sk), heads(sv))
    o_nsa = nsa_attention(partial_rope(heads(nq), pos), heads(kc), heads(vc),
                          partial_rope(heads(ksl), pos), heads(vsl),
                          partial_rope(heads(kwn), pos), heads(vwn),
                          jax.nn.sigmoid(g.reshape(bsz, seq, NSA_HEADS, N_BRANCH)),
                          pos_k, pos_v, w_ck, w_cv)
    o = jnp.concatenate([o_sb.reshape(bsz, seq, SB_W), o_nsa.reshape(bsz, seq, NSA_QW)], axis=-1)
    return o @ w_out

def odd_mixer(h, w_in, b_f, w_out):
    bsz, seq, _ = h.shape
    q, k, v, f = split_cols(h @ w_in, ODD_SPLITS)
    log_f = jax.nn.log_sigmoid((f + b_f).astype(jnp.float32))
    o = forgetting_attention(q.reshape(bsz, seq, FOX_HEADS, HEAD_DIM),
                             k.reshape(bsz, seq, FOX_HEADS, HEAD_DIM),
                             v.reshape(bsz, seq, FOX_HEADS, HEAD_DIM), log_f)
    return o.reshape(bsz, seq, FOX_W) @ w_out

def conv_glu_ffn(h, w_in, conv_w, conv_b, w_out):
    a, b = jnp.split(h @ w_in, 2, axis=-1)
    taps = conv_w[:, None, :]
    a = lax.conv_general_dilated(a, taps, window_strides=(1,), padding=[(CONV_WIDTH - 1, 0)],
                                 dimension_numbers=('NWC', 'WIO', 'NWC'),
                                 feature_group_count=a.shape[-1]) + conv_b
    return (jax.nn.silu(a) * b) @ w_out

def first_inputs(seed: int = 0) -> dict:
    key = jax.random.key(seed)
    k = jax.random.split(key, 17)

    def nrm(kk, shape, scale):
        return jax.random.normal(kk, shape, jnp.float32) * scale

    d = D_MODEL
    lc = CMP_LEN * HEAD_DIM
    return {
        'x': nrm(k[0], (BATCH, SEQ, d), 1.0),
        'attn_norm': 1.0 + nrm(k[1], (DEPTH, d), 0.02),
        'ffn_norm': 1.0 + nrm(k[2], (DEPTH, d), 0.02),
        'ev_w_in': nrm(k[3], (N_EVEN, d, EVEN_IN), d ** -0.5),
        'ev_cmp_pos_k': nrm(k[4], (N_EVEN, CMP_LEN, HEAD_DIM), 0.2),
        'ev_cmp_pos_v': nrm(k[5], (N_EVEN, CMP_LEN, HEAD_DIM), 0.2),
        'ev_cmp_w_k': nrm(k[6], (N_EVEN, lc, HEAD_DIM), lc ** -0.5),
        'ev_cmp_w_v': nrm(k[7], (N_EVEN, lc, HEAD_DIM), lc ** -0.5),
        'ev_w_out': nrm(k[8], (N_EVEN, SB_W + NSA_QW, d), (SB_W + NSA_QW) ** -0.5),
        'od_w_in': nrm(k[9], (N_ODD, d, ODD_IN), d ** -0.5),
        'od_b_f': 2.0 + nrm(k[10], (N_ODD, FOX_HEADS), 0.5),
        'od_w_out': nrm(k[11], (N_ODD, FOX_W, d), FOX_W ** -0.5),
        'ffn_w_in': nrm(k[12], (DEPTH, d, 2 * D_FF), d ** -0.5),
        'ffn_conv_w': nrm(k[13], (DEPTH, CONV_WIDTH, D_FF), CONV_WIDTH ** -0.5),
        'ffn_conv_b': nrm(k[14], (DEPTH, D_FF), 0.02),
        'ffn_w_out': nrm(k[15], (DEPTH, D_FF, d), D_FF ** -0.5),
        'final_norm': 1.0 + nrm(k[16], (d,), 0.02),
    }

def first_block(x, attn_norm, ffn_norm, ev_w_in, ev_cmp_pos_k, ev_cmp_pos_v, ev_cmp_w_k, ev_cmp_w_v,
              ev_w_out, od_w_in, od_b_f, od_w_out, ffn_w_in, ffn_conv_w, ffn_conv_b, ffn_w_out,
              final_norm):
    for layer in range(DEPTH):
        h = rmsnorm(x, attn_norm[layer])
        if layer % 2 == 0:
            e = layer // 2
            x = x + even_mixer(h, ev_w_in[e], ev_cmp_pos_k[e], ev_cmp_pos_v[e],
                               ev_cmp_w_k[e], ev_cmp_w_v[e], ev_w_out[e])
        else:
            o = layer // 2
            x = x + odd_mixer(h, od_w_in[o], od_b_f[o], od_w_out[o])
        x = x + conv_glu_ffn(rmsnorm(x, ffn_norm[layer]), ffn_w_in[layer], ffn_conv_w[layer],
                             ffn_conv_b[layer], ffn_w_out[layer])
    return rmsnorm(x, final_norm)


N_A_LAYERS = DEPTH // 2
N_B_LAYERS = DEPTH - N_A_LAYERS
D_FF_2 = 2816
A_HEADS = 8
A_KEY_DIM = 128
A_VAL_DIM = D_MODEL // A_HEADS
A_FORGET_DIM = A_HEADS * A_KEY_DIM
A_VAL_WIDTH = A_HEADS * A_VAL_DIM
A_IN_WIDTH = 2 * A_FORGET_DIM + 2 * A_VAL_WIDTH
A_CHUNK = 64
B_WINDOWS = (128, 512, 2048)
B_DILATIONS = (1, 4, 16)
B_GROUPS = 3
B_HEADS = 16
B_HEAD_DIM = D_MODEL // B_HEADS
B_QKV_WIDTH = B_GROUPS * B_HEADS * B_HEAD_DIM
B_BLOCK = 128
NUM_BUCKETS = 32
MAX_DISTANCE = 2048
EPS = 1e-6


def _rms(x, gain):
    xf = x.astype(jnp.float32)
    y = xf * lax.rsqrt(jnp.mean(xf * xf, axis=-1, keepdims=True) + EPS)
    return (y * gain.astype(jnp.float32)).astype(x.dtype)

def _swiglu(h, w_in, w_out):
    gate, up = jnp.split(h @ w_in, 2, axis=-1)
    return (jax.nn.silu(gate) * up) @ w_out

def _lower_bounds(lb_logits):
    p = jax.nn.softmax(lb_logits.astype(jnp.float32), axis=0)
    return jnp.cumsum(p, axis=0)[:-1]

def _hgrn2(h, w_in, lb, out_gain, w_out):
    bsz, seq, _ = h.shape
    n_chunks = seq // A_CHUNK
    f32 = jnp.float32
    q, f, i, g = jnp.split(h @ w_in, [A_FORGET_DIM, 2 * A_FORGET_DIM, 2 * A_FORGET_DIM + A_VAL_WIDTH], axis=-1)
    log_f = jnp.logaddexp(jnp.log(lb), jnp.log1p(-lb) + jax.nn.log_sigmoid(f.astype(f32)))
    k = -jnp.expm1(log_f)
    q = jax.nn.silu(q.astype(f32))
    v = i.astype(f32)

    def to_chunks(t, dh):
        return t.reshape(bsz, n_chunks, A_CHUNK, A_HEADS, dh).transpose(1, 0, 3, 2, 4)

    qc, kc, gc = (to_chunks(t, A_KEY_DIM) for t in (q, k, log_f))
    vc = to_chunks(v, A_VAL_DIM)
    causal = jnp.tril(jnp.ones((A_CHUNK, A_CHUNK), dtype=bool))

    def step(state, inp):
        qb, kb, vb, gb = inp
        cum = jnp.cumsum(gb, axis=2)
        rel = cum[:, :, :, None, :] - cum[:, :, None, :, :]
        decay = jnp.exp(jnp.where(causal[:, :, None], rel, -jnp.inf))
        scores = jnp.einsum('bhtd,bhtsd,bhsd->bhts', qb, decay, kb)
        out = (jnp.einsum('bhts,bhse->bhte', scores, vb)
               + jnp.einsum('bhtd,bhde->bhte', qb * jnp.exp(cum), state))
        last = cum[:, :, -1, :]
        state = (jnp.exp(last)[..., None] * state
                 + jnp.einsum('bhsd,bhse->bhde', kb * jnp.exp(last[:, :, None, :] - cum), vb))
        return state, out

    state0 = jnp.zeros((bsz, A_HEADS, A_KEY_DIM, A_VAL_DIM), f32)
    _, o = lax.scan(step, state0, (qc, kc, vc, gc))
    o = o.transpose(1, 0, 3, 2, 4).reshape(bsz, seq, A_HEADS, A_VAL_DIM)
    o = _rms(o, out_gain) * jax.nn.silu(g.astype(f32)).reshape(bsz, seq, A_HEADS, A_VAL_DIM)
    return o.reshape(bsz, seq, A_VAL_WIDTH).astype(h.dtype) @ w_out

def _t5_bucket(dist):
    dist = np.asarray(dist, np.int32)
    max_exact = NUM_BUCKETS // 2
    large = max_exact + (np.log(np.maximum(dist, 1) / max_exact)
                         / math.log(MAX_DISTANCE / max_exact) * (NUM_BUCKETS - max_exact)).astype(np.int32)
    large = np.minimum(large, NUM_BUCKETS - 1)
    return np.where(dist < max_exact, dist, large).astype(np.int32)

def _band_static(window, dilation):
    nq = B_BLOCK // dilation
    wd = window // dilation
    nj = wd + nq
    m = np.arange(nj)[None, :] - np.arange(nq)[:, None]
    band = (m >= 0) & (m <= wd)
    bucket = _t5_bucket((wd - np.clip(m, 0, wd)) * dilation)
    return band, bucket

def _shared_kv(x, kv_norm, w_kv, k_gain):
    bsz, seq, _ = x.shape
    kv = (_rms(x, kv_norm) @ w_kv).reshape(bsz, seq, 2, B_GROUPS, B_HEADS, B_HEAD_DIM)
    k = _rms(kv[:, :, 0], k_gain[:, None, :])
    v = kv[:, :, 1]
    k_pads = [jnp.pad(k[:, :, g], ((0, 0), (w, 0), (0, 0), (0, 0))) for g, w in enumerate(B_WINDOWS)]
    v_pads = [jnp.pad(v[:, :, g], ((0, 0), (w, 0), (0, 0), (0, 0))) for g, w in enumerate(B_WINDOWS)]
    return k_pads, v_pads

def _dilated_attention(h, w_q, q_gain, w_o, k_pads, v_pads, rel_bias):
    bsz, seq, _ = h.shape
    n_blocks = seq // B_BLOCK
    f32 = jnp.float32
    q = (h @ w_q).reshape(bsz, seq, B_GROUPS, B_HEADS, B_HEAD_DIM)
    q = _rms(q, q_gain[:, None, :]) * (B_HEAD_DIM ** -0.5)
    q_groups = [q[:, :, g] for g in range(B_GROUPS)]
    statics = [_band_static(w, d) for w, d in zip(B_WINDOWS, B_DILATIONS)]
    biases = [rel_bias[bucket][..., g * B_HEADS:(g + 1) * B_HEADS].transpose(2, 0, 1).astype(f32)
              for g, (_, bucket) in enumerate(statics)]

    def block(b):
        start = b * B_BLOCK
        outs, lses = [], []
        for g, (window, dil) in enumerate(zip(B_WINDOWS, B_DILATIONS)):
            band = statics[g][0]
            nq = B_BLOCK // dil
            nj = window // dil + nq
            qb = lax.dynamic_slice_in_dim(q_groups[g], start, B_BLOCK, axis=1).reshape(bsz, nq, dil, B_HEADS, B_HEAD_DIM)
            kb = lax.dynamic_slice_in_dim(k_pads[g], start, window + B_BLOCK, axis=1).reshape(bsz, nj, dil, B_HEADS, B_HEAD_DIM)
            vb = lax.dynamic_slice_in_dim(v_pads[g], start, window + B_BLOCK, axis=1).reshape(bsz, nj, dil, B_HEADS, B_HEAD_DIM)
            s = jnp.einsum('birhd,bjrhd->bhrij', qb, kb).astype(f32) + biases[g][None, :, None]
            pos = start - window + jnp.arange(nj)[:, None] * dil + jnp.arange(dil)[None, :]
            valid = band[None, :, :] & (pos.T >= 0)[:, None, :]
            s = jnp.where(valid[None, None], s, -jnp.inf)
            lse = jax.nn.logsumexp(s, axis=-1)
            p = jnp.exp(s - lse[..., None]).astype(vb.dtype)
            o = jnp.einsum('bhrij,bjrhd->birhd', p, vb).reshape(bsz, B_BLOCK, B_HEADS, B_HEAD_DIM)
            outs.append(o.astype(f32))
            lses.append(lse.transpose(0, 3, 2, 1).reshape(bsz, B_BLOCK, B_HEADS))
        wts = jax.nn.softmax(jnp.stack(lses), axis=0)
        o = jnp.einsum('gbqh,gbqhd->bqhd', wts, jnp.stack(outs))
        return o.reshape(bsz, B_BLOCK, B_HEADS * B_HEAD_DIM).astype(h.dtype)

    o = lax.map(block, jnp.arange(n_blocks))
    o = o.transpose(1, 0, 2, 3).reshape(bsz, seq, B_HEADS * B_HEAD_DIM)
    return o @ w_o

def second_inputs(seed: int = 0) -> dict:
    key = jax.random.key(seed)
    ks = jax.random.split(key, 16)

    def dense(k, shape, fan_in):
        return jax.random.normal(k, shape, jnp.float32) * fan_in ** -0.5

    def gain(k, shape):
        return 1.0 + 0.1 * jax.random.normal(k, shape, jnp.float32)

    return {
        'x': jax.random.normal(ks[0], (BATCH, SEQ, D_MODEL), jnp.float32),
        'norm_gain': gain(ks[1], (DEPTH, 3, D_MODEL)),
        'ffn_w_in': dense(ks[2], (DEPTH, 2, D_MODEL, 2 * D_FF_2), D_MODEL),
        'ffn_w_out': dense(ks[3], (DEPTH, 2, D_FF_2, D_MODEL), D_FF_2),
        'a_w_in': dense(ks[4], (N_A_LAYERS, D_MODEL, A_IN_WIDTH), D_MODEL),
        'a_lb_logits': 0.5 * jax.random.normal(ks[5], (N_A_LAYERS + 1, A_FORGET_DIM), jnp.float32),
        'a_out_gain': gain(ks[6], (N_A_LAYERS, A_VAL_DIM)),
        'a_w_out': dense(ks[7], (N_A_LAYERS, A_VAL_WIDTH, D_MODEL), A_VAL_WIDTH),
        'kv_norm': gain(ks[8], (D_MODEL,)),
        'w_kv': dense(ks[9], (D_MODEL, 2 * B_QKV_WIDTH), D_MODEL),
        'k_gain': gain(ks[10], (B_GROUPS, B_HEAD_DIM)),
        'b_w_q': dense(ks[11], (N_B_LAYERS, D_MODEL, B_QKV_WIDTH), D_MODEL),
        'b_q_gain': gain(ks[12], (N_B_LAYERS, B_GROUPS, B_HEAD_DIM)),
        'b_w_o': dense(ks[13], (N_B_LAYERS, B_HEADS * B_HEAD_DIM, D_MODEL), B_HEADS * B_HEAD_DIM),
        'rel_bias': 0.5 * jax.random.normal(ks[14], (NUM_BUCKETS, B_GROUPS * B_HEADS), jnp.float32),
    }

def second_block(x, norm_gain, ffn_w_in, ffn_w_out, a_w_in, a_lb_logits, a_out_gain, a_w_out,
              kv_norm, w_kv, k_gain, b_w_q, b_q_gain, b_w_o, rel_bias):
    lower_bounds = _lower_bounds(a_lb_logits)
    k_pads, v_pads = None, None
    for layer in range(DEPTH):
        if layer == N_A_LAYERS:
            k_pads, v_pads = _shared_kv(x, kv_norm, w_kv, k_gain)
        x = x + 0.5 * _swiglu(_rms(x, norm_gain[layer, 0]), ffn_w_in[layer, 0], ffn_w_out[layer, 0])
        h = _rms(x, norm_gain[layer, 1])
        if layer < N_A_LAYERS:
            x = x + _hgrn2(h, a_w_in[layer], lower_bounds[layer], a_out_gain[layer], a_w_out[layer])
        else:
            j = layer - N_A_LAYERS
            x = x + _dilated_attention(h, b_w_q[j], b_q_gain[j], b_w_o[j], k_pads, v_pads, rel_bias)
        x = x + 0.5 * _swiglu(_rms(x, norm_gain[layer, 2]), ffn_w_in[layer, 1], ffn_w_out[layer, 1])
    return x


def setup_inputs(seed=0):
    out = dict(first_inputs(seed))
    for name, value in second_inputs(seed + 1).items():
        if name != "x":
            out[name + "_2"] = value
    return out


def reference(
    x, attn_norm, ffn_norm, ev_w_in, ev_cmp_pos_k, ev_cmp_pos_v, ev_cmp_w_k, ev_cmp_w_v,
    ev_w_out, od_w_in, od_b_f, od_w_out, ffn_w_in, ffn_conv_w, ffn_conv_b, ffn_w_out,
    final_norm, norm_gain_2, ffn_w_in_2, ffn_w_out_2, a_w_in_2, a_lb_logits_2, a_out_gain_2,
    a_w_out_2, kv_norm_2, w_kv_2, k_gain_2, b_w_q_2, b_q_gain_2, b_w_o_2, rel_bias_2,
):
    x = first_block(
        x, attn_norm, ffn_norm, ev_w_in, ev_cmp_pos_k, ev_cmp_pos_v, ev_cmp_w_k, ev_cmp_w_v,
        ev_w_out, od_w_in, od_b_f, od_w_out, ffn_w_in, ffn_conv_w, ffn_conv_b, ffn_w_out,
        final_norm,
    )
    return second_block(
        x, norm_gain_2, ffn_w_in_2, ffn_w_out_2, a_w_in_2, a_lb_logits_2, a_out_gain_2,
        a_w_out_2, kv_norm_2, w_kv_2, k_gain_2, b_w_q_2, b_q_gain_2, b_w_o_2, rel_bias_2,
    )


_drawn_inputs = setup_inputs


def setup_inputs(seed=0):
    import zlib

    import numpy as np

    out = dict(_drawn_inputs(seed))
    spreads = {}
    factors = {'ev_cmp_pos_k': 8.0, 'ffn_conv_b': 3.286, 'k_gain_2': 4.075, 'b_q_gain_2': 3.897}
    for name, (base, spread) in spreads.items():
        noise = np.random.default_rng([zlib.crc32(name.encode()), seed]).standard_normal(out[name].shape)
        drawn = base * np.exp(spread * noise) if base else spread * noise
        out[name] = jnp.asarray(drawn.astype(out[name].dtype))
    for name, factor in factors.items():
        out[name] = (out[name] * factor).astype(out[name].dtype)
    return out
```

```python
import math
from contextlib import ExitStack

import numpy as np

import concourse.bass as bass
from concourse import mybir

P = 128
T = 256
D = 1024
KT = D // P
DFF = 2816
CW = 256
NJ = DFF // CW
RING = 6
EPS = 1e-6
NEG = -1.0e30
DH = 64
N_CMP = 15
F32 = mybir.dt.float32
BF16 = mybir.dt.bfloat16
U32 = mybir.dt.uint32
ALU = mybir.AluOpType
ACT = mybir.ActivationFunctionType
AXX = mybir.AxisListType.X
AXXY = mybir.AxisListType.XY

PLAN = ("even", "conv0", "fox", "conv1", "final", "glu0", "hgrn", "glu1", "kv", "glu2", "dilated", "glu3")
GAIN_ROW = {"even": 0, "fox": 8, "conv0": 16, "conv1": 24, "final": 32, "kv": 40, "glu0": 48, "hgrn": 56,
            "glu1": 64, "glu2": 72, "dilated": 80, "glu3": 88}
ROW_OUT_GAIN, ROW_LB, ROW_KG, ROW_QG, VEC_ROWS = 96, 97, 113, 116, 119
CONV_ROWS = 4 * (DFF // P)


def constants():
    c = {}
    idx = np.arange(P)
    c["ident"] = np.eye(P, dtype=np.float32)
    d = idx % DH
    half = 8
    inv = (np.float32(500000.0) ** (-(np.arange(half, dtype=np.float32) * np.float32(2.0 / 16)))).astype(np.float32)
    ang = np.arange(T, dtype=np.float32)[None, :] * inv[:, None]
    cos = np.ones((P, T), np.float32)
    sin = np.zeros((P, T), np.float32)
    rot = np.zeros((P, P), np.float32)
    for p in range(P):
        if d[p] < 16:
            cos[p] = np.cos(ang[d[p] % 8])
            sin[p] = np.sin(ang[d[p] % 8])
            if d[p] < 8:
                rot[p + 8, p] = -1.0
            else:
                rot[p - 8, p] = 1.0
    dup = np.stack([(idx[:, None] == DH * g + idx[None, :] % DH).astype(np.float32) for g in range(2)])
    c["cos"], c["sin"], c["rot"] = cos, sin, rot
    c["dup"] = np.concatenate(list(dup), 1)
    c["rotdup"] = np.concatenate([(dup[g] @ rot).astype(np.float32) for g in range(2)], 1)
    tri = np.where(idx[None, :] <= idx[:, None], 0.0, NEG).astype(np.float32)
    c["causal"] = np.concatenate([np.zeros((P, P), np.float32), tri, tri], 1)
    st = (idx[:, None] < idx[None, :])
    one = np.ones((P, P), bool)
    keep = np.concatenate([st, one, st], 1)
    c["sb_negkeep"] = np.where(keep, -1.0, 0.0).astype(np.float32)
    c["sb_bias"] = np.where(keep, 0.0, NEG).astype(np.float32)
    c["suffix"] = (idx[:, None] >= idx[None, :]).astype(np.float32)
    tpos = (np.arange(2)[None, :, None] * P + idx[:, None, None])
    ok = (np.arange(N_CMP) * 16 + 31)[None, None, :] <= tpos
    c["cmp_bias"] = np.where(ok, 0.0, NEG).astype(np.float32).reshape(P, 2 * N_CMP)
    c["cmp_keep"] = ok.astype(np.float32).reshape(P, 2 * N_CMP)
    lv = [np.eye(P, dtype=bool)]
    for b in (64, 32, 16, 8, 4, 2, 1):
        s, t = idx[:, None] // b, idx[None, :] // b
        lv.append((s % 2 == 0) & (t == s + 1))
    c["level"] = np.stack(lv, 1).astype(np.float32).reshape(P, 8 * P)
    c["block64"] = ((idx[:, None] // DH == idx[None, :] // DH) / np.float32(DH)).astype(np.float32)
    sel = np.zeros((P, 16, P), np.float32)
    sel[np.arange(16), np.arange(16)] = -1.0
    sel[DH + np.arange(16), np.arange(16)] = -1.0
    c["selneg"] = sel.reshape(P, 16 * P)
    c["dup16"] = (idx[None, :] % DH == idx[:16, None]).astype(np.float32)
    u = np.arange(384)
    dist = 255 - u
    hot = np.zeros((32, 3, 384), np.float32)
    msk = np.zeros((16, 3, 384), np.float32)
    for g, (w, dil) in enumerate(((128, 1), (512, 4), (2048, 16))):
        okd = (dist >= 0) & (dist <= w) & (dist % dil == 0)
        dd = np.clip(dist, 0, w).astype(np.int32)
        large = 16 + (np.log(np.maximum(dd, 1) / 16) / math.log(2048 / 16) * 16).astype(np.int32)
        bucket = np.where(dd < 16, dd, np.minimum(large, 31))
        hot[bucket[okd], g, u[okd]] = 1.0
        msk[:, g, :] = np.where(okd, 0.0, NEG)[None, :]
    c["hot"] = hot.reshape(32, 3 * 384)
    c["rel_mask"] = msk.reshape(16, 3 * 384)
    return c


def build(nc, A, out, plan=PLAN):
    ctx = ExitStack()
    with ctx:
        names = [0]

        def sb(name, shape, dt=F32):
            return ctx.enter_context(nc.sbuf_tensor(name, shape, dt))

        def sem(name):
            return ctx.enter_context(nc.semaphore(name))

        ring = [sb(f"ring{i}", [P, 2048]) for i in range(RING)]
        x = sb("x", [P, KT, T])
        xg = sb("xg", [P, KT, T])
        sq = sb("sq", [P, KT, T])
        ssum = sb("ssum", [P, 4 + 2, T])
        ssq = sb("ssq", [P, T])
        std_b, rs_b = sb("std_b", [P, T]), sb("rs_b", [P, T])
        std_c, rs_c = sb("std_c", [P, 2]), sb("rs_c", [P, 2])
        vecs = sb("vecs", [P, VEC_ROWS])
        vec_in = sb("vec_in", [P, 3, P])
        convv = sb("convv", [P, 2, CONV_ROWS])
        K = {n: sb("k_" + n, list(a.shape)) for n, a in sorted(A.items()) if n in CONST_NAMES}
        eps_c, one_c = sb("eps_c", [P, 1]), sb("one_c", [P, 1])
        mean_d = sb("mean_d", [P, P])
        mean_e = sb("mean_e", [P, P])
        ones_w = sb("ones_w", [P, T])
        zero16 = sb("zero16", [1, 512], BF16)
        ident = K["ident"]
        bank = [ctx.enter_context(nc.psum_tensor(f"bank{i}", [P, 512], F32)) for i in range(8)]

        arena = sb("arena", [P, ARENA])
        top = [0]

        def take(*shape, at=None):
            n = int(np.prod(shape))
            o = top[0] if at is None else at
            top[0] = o + n
            assert top[0] <= ARENA, top[0]
            v = arena[:, o:o + n]
            if len(shape) == 2:
                return v.rearrange("p (a b) -> p a b", a=shape[0])
            if len(shape) == 3:
                return v.rearrange("p (a b c) -> p a b c", a=shape[0], b=shape[1])
            return v

        top[0] = 0
        DK, DV = take(24, T), take(2, 3 * D)
        F0 = top[0]
        x_rows = DK[:, 0:8, :].rearrange("p k t -> p (k t)").rearrange("p (a d) -> p a d", a=2)
        ff_a = take(2, 2, 260)
        ff_c, ff_b, ff_s, ff_g = take(2, 2, T), take(2, 2, T), take(2, 2, T), take(2, 2, T)

        chunk_in = [sem(f"chunk_in{i}") for i in range(RING)]
        chunk_mul = sem("chunk_mul")
        const_in = sem("const_in")
        first_in = sem("first_in")
        const_set = sem("const_set")
        vec_t = sem("vec_t")
        vec_ok = sem("vec_ok")
        y_bank = sem("y_bank")
        x_new = sem("x_new")
        xg_new = sem("xg_new")
        sq_new = sem("sq_new")
        sum_step = sem("sum_step")
        ssq_new = sem("ssq_new")
        stat_new = sem("stat_new")
        std_new = sem("std_new")
        rs_new = sem("rs_new")
        ff_read = sem("ff_read")
        ff_conv = sem("ff_conv")
        ff_silu = sem("ff_silu")
        ff_act = sem("ff_act")
        out_sent = sem("out_sent")
        x_tok = sem("x_tok")

        def cols(w, c0, n=CW):
            return ("cols", w, c0, n)

        W = {
            "ev_in": A["ev_w_in"], "ev_out": A["ev_w_out"], "od_in": A["od_w_in"], "od_out": A["od_w_out"],
            "hg_in": A["a_w_in_2"], "hg_out": A["a_w_out_2"], "kv": A["w_kv_2"], "dq": A["b_w_q_2"],
            "do": A["b_w_o_2"],
        }
        ffn_in = {"conv0": A["ffn_w_in"][0], "conv1": A["ffn_w_in"][1]}
        ffn_out = {"conv0": A["ffn_w_out"][0], "conv1": A["ffn_w_out"][1]}
        for i in range(4):
            ffn_in[f"glu{i}"] = A["ffn_w_in_2"][i // 2, i % 2]
            ffn_out[f"glu{i}"] = A["ffn_w_out_2"][i // 2, i % 2]
        streams = {
            "even": [cols("ev_in", CW * c) for c in range(11)] + [cols("ev_in", 2816, 24)]
            + [cols("ev_out", CW * c) for c in range(4)],
            "fox": [cols("od_in", 3072, 16)] + [cols("od_in", CW * c) for c in range(12)]
            + [cols("od_out", CW * c) for c in range(4)],
            "hgrn": [cols("hg_in", c0 + CW * c) for c0 in (D, 0, 3 * D, 2 * D) for c in range(4)]
            + [cols("hg_out", CW * c) for c in range(4)],
            "kv": [cols("kv", CW * c) for c in range(24)],
            "dilated": [cols("dq", CW * c) for c in range(12)] + [cols("do", CW * c) for c in range(4)],
            "final": [],
        }
        info = {}
        n_chunk = n_y = n_x = n_ff = n_st = n_xg = n_sq = 0

        def prep(block, y):
            nonlocal n_x, n_st, n_xg, n_sq
            r = {"y": y, "x0": n_x, "xg0": n_xg, "sq0": n_sq, "st": n_st, "kind": y if isinstance(y, str) else "add"}
            if block == "end":
                n_x += 4
            else:
                n_xg += 4
                if y != "regain":
                    n_x += 4
                    n_sq += 4
                    n_st += 1
            info.setdefault(block, {})["prep"] = r

        y_events = [("y", b + 1) for b in range(4)]
        n_y = 4
        prep(plan[0], y_events)
        for pos, b in enumerate(plan):
            me = info[b]
            me["c0"] = n_chunk
            me["st"] = n_st
            nxt = plan[pos + 1] if pos + 1 < len(plan) else "end"
            if b in ffn_in:
                me["ff0"] = n_ff
                n_ff += NJ
                n_chunk += 3 * NJ
                me["y"] = [("y", n_y + k + 1) for k in range(3)] + [("c", n_chunk)]
                n_y += 3
                prep(nxt, me["y"])
            elif b == "final":
                prep(nxt, "final")
            elif b == "kv":
                n_chunk += len(streams[b])
                prep(nxt, "regain")
            else:
                n_chunk += len(streams[b])
                me["y"] = [("c", n_chunk - 3 + k) for k in range(4)]
                prep(nxt, me["y"])
        total_chunks = n_chunk

        def alpha(b):
            return 0.5 if b.startswith("glu") else 1.0

        before = {plan[i + 1] if i + 1 < len(plan) else "end": plan[i] for i in range(len(plan))}

        def ready(eng, n, it=0):
            eng.wait_ge(chunk_in[n % RING], 16 * (n // RING + 1) + 16 * it)

        def slot(n, width=CW):
            return ring[n % RING][:, 0:KT * width].rearrange("p (k n) -> p k n", k=KT)

        exec_ns = {}

        class Soft:
            def __init__(self, tag, units, ns, att, pt, nm, rr, copies):
                self.units, self.ns, self.att, self.pt, self.nm, self.rr = units, ns, att, pt, nm, rr
                self.lag = 2 if ns == 1 else 1
                self.nr = len(att)
                self.copies = copies
                self.qk = sem(tag + "_qk")
                self.masked = sem(tag + "_masked")
                self.max = sem(tag + "_max")
                self.exp = sem(tag + "_exp")
                self.rec = sem(tag + "_rec")
                self.p = sem(tag + "_p")
                self.turned = sem(tag + "_turned")
                self.ptok = sem(tag + "_pt")
                self.pv = sem(tag + "_pv")
                self.o = sem(tag + "_o")

        def soft_pe(pe, s):
            U, ns = len(s.units), s.ns

            def pv(w):
                u, g = divmod(w, ns)
                un = s.units[u]
                ob, pb = bank[6 + un["pair"] % 2], un["pb"]
                pe.wait_ge(s.ptok, w + 1)
                if un["first"] and pb == 0 and g == 0 and un["pair"] >= 2:
                    pe.wait_ge(s.o, un["pair"] - 1)
                q = s.pt[w % 3]
                sub = un["subs"][g]
                if un.get("cmp") is not None:
                    lhs, rhs = un["cmp"]
                    nc.tensor.matmul(ob[pb:pb + DH, 0:T], lhs, rhs, start=False, stop=False, skip_group_check=True)
                nc.tensor.matmul(ob[pb:pb + DH, 0:T], sub["v"][0], q[:, 0:T], start=un["first"] and g == 0,
                                 stop=False, skip_group_check=True)
                nc.tensor.matmul(ob[pb:pb + DH, P:T], sub["v"][1], q[:, T:384], start=False,
                                 stop=un["last"] and g == ns - 1, skip_group_check=True).then_inc(s.pv, 1)

            for i in range(U + s.lag):
                if i < U:
                    for g in range(ns):
                        w = i * ns + g
                        sub = s.units[i]["subs"][g]
                        if w >= 3:
                            pe.wait_ge(s.masked, w - 2)
                        S = bank[w % 3]
                        cum = s.units[i].get("cum")
                        one = cum is None
                        nc.tensor.matmul(S[:, 0:T], sub["q"][:, P:T], sub["k"][:, 0:T], start=True, stop=one)
                        if not one:
                            nc.tensor.matmul(S[:, 0:T], cum[0], cum[1][:, 0:T], start=False, stop=True)
                        last = nc.tensor.matmul(S[:, T:384], sub["q"][:, 0:P], sub["k"][:, 0:P], start=True, stop=one)
                        if not one:
                            last = nc.tensor.matmul(S[:, T:384], cum[0], cum[1][:, 0:P], start=False, stop=True)
                        last.then_inc(s.qk, 1)
                j = i - s.lag
                if j >= 0:
                    pe.wait_ge(s.p, j + 1)
                    for g in range(ns):
                        w = j * ns + g
                        if w >= 2:
                            pe.wait_ge(s.ptok, w - 1)
                        B = bank[3 + w % 2]
                        e = s.att[j % s.nr][:, g, :]
                        nc.tensor.transpose(B[:, 0:P], e[:, T:384], ident[:, :])
                        nc.tensor.transpose(B[:, P:T], e[:, 0:P], ident[:, :])
                        nc.tensor.transpose(B[:, T:384], e[:, P:T], ident[:, :]).then_inc(s.turned, 1)
                        if w >= 1:
                            pv(w - 1)
            pv(U * ns - 1)

        def soft_dve(dve, s):
            U, ns = len(s.units), s.ns
            nrec = [0]

            def weights(u):
                un = s.units[u]
                dve.wait_ge(s.exp, u + 1)
                r = s.rr[:, u % 4, 2:4]
                nc.vector.reciprocal(r, s.rr[:, u % 4, 0:2]).then_inc(s.rec, 1)
                nrec[0] += 1
                dve.wait_ge(s.rec, nrec[0])
                if un.get("gate") is not None:
                    nc.vector.tensor_tensor(r, r, un["gate"], ALU.mult).then_inc(s.rec, 1)
                    nrec[0] += 1
                    dve.wait_ge(s.rec, nrec[0])
                e = s.att[u % s.nr]
                nc.vector.tensor_scalar(e[:, :, 0:T], e[:, :, 0:T], s.rr[:, u % 4, 3:4], None, ALU.mult)
                nc.vector.tensor_scalar(e[:, :, T:384], e[:, :, T:384], s.rr[:, u % 4, 2:3], None,
                                        ALU.mult).then_inc(s.p, 1)

            for i in range(U + 1):
                if i < U:
                    un = s.units[i]
                    if i >= s.nr:
                        dve.wait_ge(s.turned, ns * (i - s.nr + 1))
                    e = s.att[i % s.nr]
                    if un.get("wait") is not None:
                        dve.wait_ge(*un["wait"])
                    for g in range(ns):
                        w = i * ns + g
                        S = bank[w % 3]
                        add = un["subs"][g]["add"]
                        dve.wait_ge(s.qk, w + 1)
                        if un.get("cq") is not None:
                            nc.vector.scalar_tensor_tensor(e[:, g, 0:T], S[:, 0:T], un["cq"][1], add[:, 0:T],
                                                           ALU.add, ALU.add)
                            nc.vector.scalar_tensor_tensor(e[:, g, T:384], S[:, T:384], un["cq"][0], add[:, T:384],
                                                           ALU.add, ALU.add).then_inc(s.masked, 1)
                        else:
                            nc.vector.tensor_tensor(e[:, g, :], S[:, 0:384], add, ALU.add).then_inc(s.masked, 1)
                    dve.wait_ge(s.masked, (i + 1) * ns)
                    nm = s.nm[:, i % 4, :]
                    nc.vector.tensor_reduce(nm[:, 1:2], e[:, :, 0:T], AXXY, ALU.max, negate=True)
                    nc.vector.tensor_reduce(nm[:, 0:1], e[:, :, T:384], AXXY, ALU.max, negate=True).then_inc(s.max, 1)
                if i >= 1:
                    weights(i - 1)

        def soft_act(act, s):
            U, ns = len(s.units), s.ns

            def pair_out(u):
                un = s.units[u]
                if un["last"] and un["pb"] == DH:
                    act.wait_ge(s.pv, ns * (u + 1))
                    src, dst = bank[6 + un["pair"] % 2][:, 0:T], s.copies[un["pair"]]
                    if len(dst.shape) == 3:
                        src = src.rearrange("p (a b) -> p a b", a=2)
                    nc.scalar.activation(dst, src, ACT.Copy).then_inc(s.o, 1)

            for i in range(U + s.lag):
                if i < U:
                    act.wait_ge(s.max, i + 1)
                    e = s.att[i % s.nr]
                    nc.scalar.activation(e[:, :, 0:T], e[:, :, 0:T], ACT.Exp, bias=s.nm[:, i % 4, 1:2],
                                         accum_out=s.rr[:, i % 4, 1:2])
                    nc.scalar.activation(e[:, :, T:384], e[:, :, T:384], ACT.Exp, bias=s.nm[:, i % 4, 0:1],
                                         accum_out=s.rr[:, i % 4, 0:1]).then_inc(s.exp, 1)
                j = i - s.lag
                if j >= 1:
                    pair_out(j - 1)
                if j >= 0:
                    for g in range(ns):
                        w = j * ns + g
                        act.wait_ge(s.turned, w + 1)
                        if w >= 3:
                            act.wait_ge(s.pv, w - 2)
                        nc.scalar.activation(s.pt[w % 3], bank[3 + w % 2][:, 0:384], ACT.Copy).then_inc(s.ptok, 1)
            pair_out(U - 1)

        def pe_stats(pe, b):
            st = info[b]["st"]
            pe.wait_ge(ssq_new, st)
            nc.tensor.matmul(bank[7][:, 0:T], mean_d[:, :], ssq[:, :], start=True, stop=True)
            nc.tensor.matmul(bank[7][:, T:T + 1], ssq[:, 0:P], mean_d[:, 0:1], start=True, stop=True)
            nc.tensor.matmul(bank[7][:, T + 1:T + 2], ssq[:, P:T], mean_d[:, 0:1], start=True,
                             stop=True).then_inc(stat_new, 1)

        def pe_chunk(pe, n, B, mode, width=CW, src=None):
            ready(pe, n)
            w = slot(n, width)
            src = xg if src is None else src
            last = None
            if mode == "fm":
                for e in range(0, width, P):
                    m = min(P, width - e)
                    for k in range(KT):
                        last = nc.tensor.matmul(B[0:m, (e // P) * T:(e // P + 1) * T], w[:, k, e:e + m], src[:, k, :],
                                                start=k == 0, stop=k == KT - 1)
            elif mode == "tm":
                for t in range(2):
                    for k in range(KT):
                        last = nc.tensor.matmul(B[:, t * CW:t * CW + width], src[:, k, t * P:(t + 1) * P], w[:, k, :],
                                                start=k == 0, stop=k == KT - 1)
            last.then_inc(chunk_mul, 1)

        def pe_residual(pe, b, n0, src, wait):
            wait(pe)
            for i in range(4):
                pe_chunk(pe, n0 + i, bank[4 + i], "fm", src=src)

        def wait_xg(pe, b):
            pe.wait_ge(xg_new, info[b]["prep"]["xg0"] + 4)

        def ff_in(pe, j, par, n, F, first, it=None):
            turn = 0 if it is None else it
            if not first:
                pe.wait_ge(ff_read, 2 * (F + j))
            for h in range(2):
                ready(pe, n + h, turn)
                w = slot(n + h)
                B = bank[2 * par + h]
                for e in range(2):
                    for k in range(KT):
                        last = nc.tensor.matmul(B[:, e * T:(e + 1) * T], w[:, k, e * P:(e + 1) * P], xg[:, k, :],
                                                start=k == 0, stop=k == KT - 1)
                last.then_inc(chunk_mul, 1)

        def ff_out(pe, j, par, n, F, it=None, tail=False):
            pe.wait_ge(ff_act, F + j + 1)
            ready(pe, n, 0 if it is None else it)
            w = ring[n % RING][:, :].rearrange("p (k n) -> p k n", k=2)
            for d in range(KT):
                for k in range(2):
                    last = nc.tensor.matmul(bank[4 + d // 2][:, (d % 2) * T:(d % 2 + 1) * T], w[:, k, d * P:(d + 1) * P],
                                            ff_g[:, par, k, :], start=False, stop=tail and k == 1,
                                            skip_group_check=True)
                if tail and d in (1, 3, 5):
                    last.then_inc(y_bank, 1)
            last.then_inc(chunk_mul, 1)

        def pe_ffn(pe, b):
            F, n = info[b]["ff0"], info[b]["c0"]
            wait_xg(pe, b)
            ff_in(pe, 0, 0, n, F, True)
            if info[b]["prep"]["kind"] != "regain":
                pe_stats(pe, b)
            for y in range(4, 8):
                if y == 7 and info[b]["prep"]["kind"] != "regain":
                    pe.wait_ge(std_new, info[b]["st"])
                nc.tensor.matmul(bank[y][:, :], zero16[:, 0:P], zero16[:, :], start=True, stop=False,
                                 skip_group_check=True)
            with pe.Fori(0, (NJ - 1) // 2) as i:
                for s in range(2):
                    m = n + 2 + 3 * s
                    ff_in(pe, 2 * i + (1 + s), (1 + s) % 2, m, F, False, i)
                    ff_out(pe, 2 * i + s, s, m + 2, F, i)
            ff_out(pe, NJ - 1, (NJ - 1) % 2, n + 3 * NJ - 1, F, None, True)

        def dve_ff_step(dve, b, j, par, F, first, conv):
            c_of = chunk_of_step(b, j, first)
            rs2 = rs_b[:, :].unsqueeze(1).broadcast_to([P, 2, T])
            dve.wait_ge(chunk_mul, c_of)
            ga = bank[2 * par][:, :].rearrange("p (e t) -> p e t", e=2)
            ub = bank[2 * par + 1][:, :].rearrange("p (e t) -> p e t", e=2)
            dst = ff_a[:, par, :, 2:2 + T] if conv is not None else ff_c[:, par, :, :]
            nc.vector.tensor_tensor(dst, ga, rs2, ALU.mult).then_inc(ff_read, 1)
            nc.vector.tensor_tensor(ff_b[:, par, :, :], ub, rs2, ALU.mult).then_inc(ff_read, 1)
            if conv is not None:
                layer, G = conv
                C = 3 * (G + j)
                nt = DFF // P
                for tap in range(3):
                    if tap == 0:
                        dve.wait_ge(ff_read, 2 * (F + j) + 3)
                    else:
                        dve.wait_ge(ff_conv, C + tap)
                    for e in range(2):
                        w = convv[:, layer, bass.ds(2 * j + (tap * nt + e), 1)]
                        a = ff_a[:, par, e, tap:tap + T]
                        c = ff_c[:, par, e, :]
                        if tap == 0:
                            last = nc.vector.tensor_scalar(c, a, w, None, ALU.mult)
                        else:
                            last = nc.vector.scalar_tensor_tensor(c, a, w, c, ALU.mult, ALU.add)
                    last.then_inc(ff_conv, 1)
            dve.wait_ge(ff_silu, F + j + 1)
            dve.wait_ge(ff_read, 2 * (F + j) + 4)
            nc.vector.tensor_tensor(ff_g[:, par, :, :], ff_s[:, par, :, :], ff_b[:, par, :, :],
                                    ALU.mult).then_inc(ff_act, 1)

        def chunk_of_step(b, j, first):
            n = info[b]["c0"]
            return n + 2 if first else (j * 3) + (n + 1)

        def act_ff_step(act, b, j, par, F, conv):
            if conv is None:
                act.wait_ge(ff_read, 2 * (F + j) + 3)
                nc.scalar.activation(ff_s[:, par, :, :], ff_c[:, par, :, :], ACT.Silu).then_inc(ff_silu, 1)
            else:
                layer, G = conv
                act.wait_ge(ff_conv, 3 * (G + j) + 3)
                for e in range(2):
                    last = nc.scalar.activation(ff_s[:, par, e, :], ff_c[:, par, e, :], ACT.Silu,
                                                bias=convv[:, layer, bass.ds(2 * j + (3 * (DFF // P) + e), 1)])
                last.then_inc(ff_silu, 1)

        def ff_loop(eng, step, b):
            F = info[b]["ff0"]
            conv = None
            if b.startswith("conv"):
                before_convs = [c for c in plan[:plan.index(b)] if c.startswith("conv")]
                conv = (int(b[-1]), NJ * len(before_convs))
            step(0, 0, F, True, conv)
            with eng.Fori(0, (NJ - 1) // 2) as i:
                for s in range(2):
                    step(2 * i + (1 + s), (1 + s) % 2, F, False, conv)

        def dve_prep(dve, b, scale):
            r = info[b]["prep"]
            g0 = GAIN_ROW.get(b, 0)
            for i in range(4):
                xs = x[:, 2 * i:2 * i + 2, :]
                if r["kind"] == "add":
                    kind, val = r["y"][i]
                    dve.wait_ge(y_bank if kind == "y" else chunk_mul, val)
                    y = bank[4 + i][:, :].rearrange("p (e t) -> p e t", e=2)
                    if scale is None:
                        nc.vector.tensor_copy(xs, y).then_inc(x_new, 1)
                    else:
                        nc.vector.scalar_tensor_tensor(xs, y, scale, xs, ALU.mult, ALU.add).then_inc(x_new, 1)
                elif r["kind"] == "final":
                    for e in range(2):
                        t = 2 * i + e
                        last = nc.vector.scalar_tensor_tensor(x[:, t, :], x[:, t, :],
                                                              vecs[:, GAIN_ROW["final"] + t:GAIN_ROW["final"] + t + 1],
                                                              rs_b[:, :], ALU.mult, ALU.mult)
                    last.then_inc(x_new, 1)
                else:
                    if i == 0:
                        dve.wait_ge(chunk_mul, info[b]["c0"])
                if b == "end":
                    continue
                if r["kind"] != "regain":
                    dve.wait_ge(x_new, r["x0"] + i + 1)
                for e in range(2):
                    t = 2 * i + e
                    last = nc.vector.tensor_scalar(xg[:, t, :], x[:, t, :], vecs[:, g0 + t:g0 + t + 1], None, ALU.mult)
                last.then_inc(xg_new, 1)
            if b == "end" or r["kind"] == "regain":
                return
            dve.wait_ge(sq_new, r["sq0"] + 4)
            s0 = 2 * r["st"]
            nc.vector.tensor_tensor(ssum[:, 0:4, :], sq[:, 0:4, :], sq[:, 4:8, :], ALU.add).then_inc(sum_step, 1)
            dve.wait_ge(sum_step, s0 + 1)
            nc.vector.tensor_tensor(ssum[:, 4:6, :], ssum[:, 0:2, :], ssum[:, 2:4, :], ALU.add).then_inc(sum_step, 1)
            dve.wait_ge(sum_step, s0 + 2)
            nc.vector.tensor_tensor(ssq[:, :], ssum[:, 4, :], ssum[:, 5, :], ALU.add).then_inc(ssq_new, 1)

        def dve_rs(dve, b):
            st = info[b]["st"]
            dve.wait_ge(std_new, st)
            nc.vector.reciprocal(rs_c[:, :], std_c[:, :])
            nc.vector.reciprocal(rs_b[:, :], std_b[:, :]).then_inc(rs_new, 1)
            dve.wait_ge(rs_new, st)

        def act_prep(act, b):
            r = info[b]["prep"]
            if b == "end" or r["kind"] == "regain":
                return
            for i in range(4):
                act.wait_ge(x_new, r["x0"] + i + 1)
                nc.scalar.activation(sq[:, 2 * i:2 * i + 2, :], x[:, 2 * i:2 * i + 2, :], ACT.Square).then_inc(sq_new, 1)
            act.wait_ge(stat_new, r["st"] + 1)
            nc.scalar.activation(std_c[:, :], bank[7][:, T:T + 2], ACT.Sqrt, bias=eps_c[:, :])
            nc.scalar.activation(std_b[:, :], bank[7][:, 0:T], ACT.Sqrt, bias=eps_c[:, :]).then_inc(std_new, 1)

        def make_even():
            top[0] = 0
            SQ, SK, NQ = take(4, T), take(4, T), take(4, T)
            KD = take(4, T)
            KRAW, KCR = take(2, T), take(16)
            KCV = take(2, T)
            SV = take(2, 512)
            VSW = take(2, 2, P)
            GT = take(2, 24)
            CW_ = take(2, 2048)
            BLK = take(2, 32, 16)
            PE_ = take(P)
            PEK = take(2, 32)
            KC = take(2, 16)
            VC = take(2, DH)
            RT = take(2, T)
            OT = take(KT, T)
            m0 = top[0]
            LK, AZ = take(8, 384), take(8, 384)
            top[0] = m0
            att = [take(1, 384) for _ in range(6)]
            pt = [take(384) for _ in range(3)]
            NM, RR = take(4, 2), take(4, 4)
            CS, CP = take(16, 16), take(16, 16)
            CM, CD = take(16), take(16)
            PTC = take(8, T)
            pj_fm, pj_tm = sem("ev_fm"), sem("ev_tm")
            cmp_in = sem("ev_cmp_in")
            pos_t, pos_ok = sem("ev_pos_t"), sem("ev_pos_ok")
            rot_mm, rope = sem("ev_rot_mm"), sem("ev_rope")
            blk_ok, comp = sem("ev_blk"), sem("ev_comp")
            kc_raw, vc_ok = sem("ev_kc_raw"), sem("ev_vc")
            z_mm, z_abs, z_ln, lk_ok = sem("sb_z"), sem("sb_abs"), sem("sb_ln"), sem("sb_lk")
            sp_ok, a_mm, am_ok, a_ok = sem("sb_sp"), sem("sb_a_mm"), sem("sb_am"), sem("sb_a")
            sb_pv, sb_o = sem("sb_pv"), sem("sb_o")
            c_qk, c_v, c_e, c_p = sem("cm_qk"), sem("cm_v"), sem("cm_e"), sem("cm_p")
            c_t, c_pt = sem("cm_t"), sem("cm_pt")
            n0 = info["even"]["c0"]
            gone = []
            v = a = 0
            for m in ["fm"] * 4 + ["tm"] * 2 + ["fm"] * 2 + ["fm", "mix", "mix", "tm"]:
                if m == "tm":
                    a += 1
                else:
                    v += 1
                    if m == "mix":
                        a += 1
                gone.append((v, a))
            units = []
            for h in range(8):
                g, pb = h // 4, (h % 2) * DH
                for br in range(2):
                    un = {"pair": h // 2, "pb": pb, "first": br == 0, "last": br == 1,
                          "gate": GT[:, :, 3 * h + 1 + br],
                          "subs": [{"q": NQ[pb:pb + DH, h // 2, :], "k": KD[pb:pb + DH, 2 * br + g, :],
                                    "v": [VSW[:, br, t, g * DH:(g + 1) * DH] for t in range(2)],
                                    "add": K["causal"][:, :]}]}
                    if br == 1:
                        un["cmp"] = (VC[0:N_CMP, g, :], PTC[0:N_CMP, h, :])
                    units.append(un)
            soft = Soft("nsa", units, 1, att, pt, NM, RR, [OT[:, 4 + p, :] for p in range(4)])

            ropes = [(NQ[:, t, :], NQ[:, t, :], T, None) for t in range(4)]
            ropes += [(KRAW[:, t // 2, :], KD[:, t, :], T, t % 2) for t in range(4)]
            ropes += [(KCR[:, 0:N_CMP], KC[:, g, 0:N_CMP], N_CMP, g) for g in range(2)]

            def pe_part(pe):
                wait_xg(pe, "even")
                for c in range(12):
                    if c == 1:
                        pe_stats(pe, "even")
                    if c >= 4:
                        vv, aa = gone[c - 4]
                        pe.wait_ge(pj_fm, vv)
                        if aa:
                            pe.wait_ge(pj_tm, aa)
                    B = bank[c % 4]
                    if c in (9, 10):
                        ready(pe, n0 + c)
                        w = slot(n0 + c)
                        for k in range(KT):
                            nc.tensor.matmul(B[:, 0:T], w[:, k, 0:P], xg[:, k, :], start=k == 0, stop=k == KT - 1)
                        for t in range(2):
                            for k in range(KT):
                                last = nc.tensor.matmul(bank[4 + c - 9][:, t * P:(t + 1) * P],
                                                        xg[:, k, t * P:(t + 1) * P], w[:, k, P:2 * P],
                                                        start=k == 0, stop=k == KT - 1)
                        last.then_inc(chunk_mul, 1)
                    elif c == 11:
                        pe_chunk(pe, n0 + c, B, "tm", 24)
                    else:
                        pe_chunk(pe, n0 + c, B, "tm" if c in (4, 5) else "fm")
                pe.wait_ge(cmp_in, 16 * 6)
                nc.tensor.transpose(bank[6][:, 0:32], PE_[0:32, :], ident[0:32, 0:32]).then_inc(pos_t, 1)
                pe.wait_ge(pos_ok, 1)
                nc.tensor.transpose(bank[6][:, 0:32], PE_[32:64, :], ident[32:64, 32:64]).then_inc(pos_t, 1)
                pe.wait_ge(blk_ok, 4)
                pe.wait_ge(pos_ok, 2)
                for g in range(2):
                    r = slice(g * DH, (g + 1) * DH)
                    for l in range(32):
                        last = nc.tensor.matmul(bank[6][r, 0:N_CMP], CW_[r, 0, l * DH:(l + 1) * DH],
                                                BLK[r, 0, l, 0:N_CMP], start=l == 0, stop=l == 31)
                for g in range(2):
                    r = slice(g * DH, (g + 1) * DH)
                    for l in range(32):
                        last = nc.tensor.matmul(bank[6 + g][0:N_CMP, 64:64 + DH],
                                                BLK[r, 1, l, 0:N_CMP], CW_[r, 1, l * DH:(l + 1) * DH],
                                                start=l == 0, stop=l == 31)
                last.then_inc(comp, 1)
                pe.wait_ge(pj_fm, gone[11][0])
                pe.wait_ge(pj_tm, gone[11][1])
                pe.wait_ge(kc_raw, 1)
                for i, (src, buf, n, g) in enumerate(ropes):
                    if i >= 4:
                        pe.wait_ge(rope, 3 * (i - 4) + 2)
                    rot = K["rot"][:, :]
                    if g is not None:
                        rot = K["rotdup"][:, g * P:(g + 1) * P]
                        nc.tensor.matmul(bank[i % 4][:, T:T + n], K["dup"][:, g * P:(g + 1) * P], src,
                                         start=True, stop=True)
                    nc.tensor.matmul(bank[i % 4][:, 0:n], rot, src, start=True, stop=True).then_inc(rot_mm, 1)
                pe.wait_ge(rope, 3 * len(ropes))
                pe.wait_ge(vc_ok, 2)
                for h in range(8):
                    pb = (h % 2) * DH
                    k, q, B = SK[pb:pb + DH, h // 2, :], SQ[pb:pb + DH, h // 2, :], bank[h]
                    nc.tensor.matmul(B[:, 0:T], k[:, 0:P], q, start=True, stop=False, skip_group_check=True)
                    nc.tensor.matmul(B[:, T:384], k[:, P:T], q[:, P:T], start=False, stop=False,
                                     skip_group_check=True).then_inc(z_mm, 1)
                for h in range(8):
                    pe.wait_ge(lk_ok, h + 1)
                    B, L = bank[h], LK[:, h, :]
                    nc.tensor.matmul(B[:, 0:T], K["suffix"][:, :], L[:, 0:T], start=False, stop=False,
                                     skip_group_check=True)
                    nc.tensor.matmul(B[:, T:384], K["suffix"][:, :], L[:, T:384], start=False, stop=False,
                                     skip_group_check=True)
                    nc.tensor.matmul(B[:, P:T], ones_w[:, 0:P], L[:, T:384], start=False, stop=True,
                                     skip_group_check=True).then_inc(a_mm, 1)
                for h in range(8):
                    pb = (h % 2) * DH
                    pe.wait_ge(a_ok, h + 1)
                    O, L = bank[h - h % 2][pb:pb + DH, :], LK[:, h, :]
                    nc.tensor.matmul(O[:, 0:T], SV[:, 0, h * DH:(h + 1) * DH], L[:, 0:T], start=True, stop=False,
                                     skip_group_check=True)
                    nc.tensor.matmul(O[:, P:T], SV[:, 1, h * DH:(h + 1) * DH], L[:, T:384], start=False, stop=True,
                                     skip_group_check=True).then_inc(sb_pv, 1)
                pe.wait_ge(sb_o, 4)
                for h in range(8):
                    pb = (h % 2) * DH
                    for t in range(2):
                        o = (2 * (h // 2) + t) * 16
                        last = nc.tensor.matmul(bank[5 - h % 2][:, o:o + N_CMP],
                                                NQ[pb:pb + DH, h // 2, t * P:(t + 1) * P], KC[pb:pb + DH, h // 4, 0:N_CMP],
                                                start=True, stop=True)
                last.then_inc(c_qk, 1)
                pe.wait_ge(c_p, 1)
                for h in range(8):
                    for t in range(2):
                        last = nc.tensor.transpose(bank[h // 2][0:N_CMP, (h % 2) * T + t * P:(h % 2) * T + (t + 1) * P],
                                                   CP[:, 8 * (h % 2) + 2 * (h // 2) + t, 0:N_CMP], ident[:, :])
                last.then_inc(c_t, 1)
                pe.wait_ge(c_pt, 4)
                soft_pe(pe, soft)
                pe_residual(pe, "even", n0 + 12, OT, lambda e: e.wait_ge(soft.o, 4))

            def dve_part(dve):
                def rs2(n=2):
                    return rs_b[:, :].unsqueeze(1).broadcast_to([P, n, T])

                for c in range(11):
                    if c in (4, 5):
                        continue
                    dve.wait_ge(chunk_mul, n0 + c + 1)
                    B = bank[c % 4][:, :].rearrange("p (e t) -> p e t", e=2)
                    if c in (0, 1, 6, 7):
                        dst, s = (SQ if c < 2 else NQ)[:, 2 * (c % 2):2 * (c % 2) + 2, :], DH ** -0.5
                    elif c < 4:
                        dst, s = SK[:, 2 * (c - 2):2 * (c - 2) + 2, :], 1.0
                    elif c == 8:
                        dst, s = KCV, 1.0
                    else:
                        nc.vector.tensor_tensor(KRAW[:, c - 9, :], B[:, 0, :], rs_b[:, :], ALU.mult).then_inc(pj_fm, 1)
                        continue
                    nc.vector.scalar_tensor_tensor(dst, B, s, rs2(), ALU.mult, ALU.mult).then_inc(pj_fm, 1)
                for i in range(2):
                    dve.wait_ge(pos_t, i + 1)
                    nc.vector.tensor_copy(PEK[:, i, :], bank[6][:, 0:32]).then_inc(pos_ok, 1)
                dve.wait_ge(pos_ok, 2)
                dve.wait_ge(pj_fm, 7)
                for i in range(2):
                    kv = KCV[:, i, :].rearrange("p (c l) -> p l c", l=16)
                    for hf in range(2):
                        pe_b = PEK[:, i, 16 * hf:16 * hf + 16].unsqueeze(2).broadcast_to([P, 16, N_CMP])
                        nc.vector.tensor_tensor(BLK[:, i, 16 * hf:16 * hf + 16, 0:N_CMP], kv[:, :, hf:hf + N_CMP], pe_b,
                                                ALU.add).then_inc(blk_ok, 1)
                dve.wait_ge(comp, 1)
                for g in range(2):
                    nc.vector.tensor_copy(VC[0:N_CMP, g, :], bank[6 + g][0:N_CMP, 64:64 + DH]).then_inc(vc_ok, 1)
                nc.vector.tensor_copy(KCR[:, 0:N_CMP], bank[6][:, 0:N_CMP]).then_inc(kc_raw, 1)
                for i, (src, buf, n, g) in enumerate(ropes):
                    cos, sin = K["cos"][:, :], K["sin"][:, :]
                    if n != T:
                        cos = cos.rearrange("p (c l) -> p c l", l=16)[:, 1:16, 15]
                        sin = sin.rearrange("p (c l) -> p c l", l=16)[:, 1:16, 15]
                    dve.wait_ge(rot_mm, i + 1)
                    t = RT[:, i % 2, 0:n]
                    nc.vector.tensor_tensor(t, bank[i % 4][:, 0:n], sin, ALU.mult).then_inc(rope, 1)
                    nc.vector.tensor_tensor(buf, src if g is None else bank[i % 4][:, T:T + n], cos,
                                            ALU.mult).then_inc(rope, 1)
                    dve.wait_ge(rope, 3 * i + 2)
                    nc.vector.tensor_tensor(buf, buf, t, ALU.add).then_inc(rope, 1)
                for h in range(8):
                    if h == 0:
                        dve.wait_ge(z_ln, 3)
                    nc.vector.scalar_tensor_tensor(LK[:, h, :], bank[h][:, 0:384], 0.0, AZ[:, h, :],
                                                   ALU.max, ALU.add).then_inc(sp_ok, 1)
                    dve.wait_ge(sp_ok, h + 1)
                    nc.vector.tensor_tensor(LK[:, h, :], LK[:, h, :], K["sb_negkeep"][:, :], ALU.mult).then_inc(lk_ok, 1)
                for h in range(8):
                    dve.wait_ge(a_mm, h + 1)
                    nc.vector.tensor_tensor(LK[:, h, :], bank[h][:, 0:384], K["sb_bias"][:, :], ALU.add).then_inc(am_ok, 1)
                dve.wait_ge(c_qk, 1)
                bias = K["cmp_bias"][:, :].rearrange("p (t c) -> p t c", t=2).unsqueeze(1).broadcast_to([P, 4, 2, N_CMP])
                keep = K["cmp_keep"][:, :].rearrange("p (t c) -> p t c", t=2).unsqueeze(1).broadcast_to([P, 8, 2, N_CMP])
                cs4 = CS[:, :, 0:N_CMP].rearrange("p (h t) c -> p h t c", t=2)
                cs, cp = CS[:, :, 0:N_CMP], CP[:, :, 0:N_CMP]

                def step(ins, n):
                    ins.then_inc(c_v, 1)
                    dve.wait_ge(c_v, n)

                dve.wait_ge(sb_o, 4)
                for par in range(2):
                    sc = bank[5 - par][:, 0:P].rearrange("p (h t c) -> p h t c", t=2, c=16)[:, :, :, 0:N_CMP]
                    last = nc.vector.tensor_tensor(cs4[:, 4 * par:4 * par + 4], sc, bias, ALU.add)
                step(last, 1)
                step(nc.vector.tensor_reduce(CM[:, :], cs, AXX, ALU.max), 2)
                step(nc.vector.tensor_tensor(cs, cs, CM[:, :].unsqueeze(2).broadcast_to([P, 16, N_CMP]),
                                             ALU.subtract), 3)
                dve.wait_ge(c_e, 1)
                step(nc.vector.tensor_tensor(cs4, cs4, keep, ALU.mult), 4)
                step(nc.vector.tensor_reduce(CD[:, :], cs, AXX, ALU.add), 5)
                step(nc.vector.tensor_scalar(CD[:, :], CD[:, :], 1.0, None, ALU.max), 6)
                step(nc.vector.reciprocal(CM[:, :], CD[:, :]), 7)
                for par in range(2):
                    gate = GT[:, :, :].rearrange("p t (h e b) -> p e h t b", e=2, b=3)[:, par, :, :, 0]
                    cm2 = CM[:, 8 * par:8 * par + 8].rearrange("p (h t) -> p h t", t=2)
                    last = nc.vector.tensor_tensor(cm2, cm2, gate, ALU.mult)
                step(last, 8)
                nc.vector.tensor_tensor(cp, cs, CM[:, :].unsqueeze(2).broadcast_to([P, 16, N_CMP]),
                                        ALU.mult).then_inc(c_p, 1)
                soft_dve(dve, soft)

            def act_part(act):
                for i, w in enumerate(("cmp_w_k", "cmp_w_v")):
                    src = A[w].rearrange("(l d) e -> d l e", d=DH)
                    for hf in range(2):
                        act.dma_start(CW_[hf * DH:(hf + 1) * DH, i, :].rearrange("p (l e) -> p l e", e=DH),
                                      src).then_inc(cmp_in, 16)
                for i in range(2):
                    act.dma_start(PE_[32 * i:32 * i + 32, :], A["cmp_pos"][:, i * P:(i + 1) * P]).then_inc(cmp_in, 16)
                act.wait_ge(rs_new, info["even"]["st"])
                for c in (4, 5, 9, 10, 11):
                    act.wait_ge(chunk_mul, n0 + c + 1)
                    for t in range(2):
                        if c < 6:
                            last = nc.scalar.activation(SV[:, t, (c - 4) * CW:(c - 3) * CW], bank[c % 4][:, t * CW:(t + 1) * CW],
                                                        ACT.Copy, scale=rs_c[:, t:t + 1])
                        elif c < 11:
                            last = nc.scalar.activation(VSW[:, c - 9, t, :], bank[4 + c - 9][:, t * P:(t + 1) * P],
                                                        ACT.Copy, scale=rs_c[:, t:t + 1])
                        else:
                            last = nc.scalar.activation(GT[:, t, :], bank[c % 4][:, t * CW:t * CW + 24],
                                                        ACT.Sigmoid, scale=rs_c[:, t:t + 1])
                    last.then_inc(pj_tm, 1)
                for h in range(8):
                    act.wait_ge(z_mm, h + 1)
                    nc.scalar.activation(AZ[:, h, :], bank[h][:, 0:384], ACT.Abs).then_inc(z_abs, 1)
                act.wait_ge(z_abs, 8)
                nc.scalar.activation(AZ[:, :, :], AZ[:, :, :], ACT.Exp, scale=-1.0).then_inc(z_ln, 2)
                act.wait_ge(z_ln, 2)
                nc.scalar.activation(AZ[:, :, :], AZ[:, :, :], ACT.Ln, bias=one_c[:, :]).then_inc(z_ln, 1)
                for h in range(8):
                    act.wait_ge(am_ok, h + 1)
                    nc.scalar.activation(LK[:, h, :], LK[:, h, :], ACT.Exp).then_inc(a_ok, 1)
                for p in range(4):
                    act.wait_ge(sb_pv, 2 * p + 2)
                    nc.scalar.activation(OT[:, p, :], bank[2 * p][:, 0:T], ACT.Copy).then_inc(sb_o, 1)
                act.wait_ge(c_v, 3)
                cs = CS[:, :, 0:N_CMP]
                nc.scalar.activation(cs, cs, ACT.Exp).then_inc(c_e, 1)
                act.wait_ge(c_t, 1)
                for i in range(4):
                    nc.scalar.activation(PTC[0:N_CMP, 2 * i:2 * i + 2, :], bank[i][0:N_CMP, :].rearrange(
                        "p (h t) -> p h t", h=2), ACT.Copy).then_inc(c_pt, 1)
                soft_act(act, soft)

            return {"pe": pe_part, "dve": dve_part, "act": act_part}

        def make_fox():
            top[0] = 0
            Q, KF, V = take(8, T), take(8, T), take(2, D)
            SEL, CUM2, CQ = take(2048), take(T), take(2, 16)
            LF, AB, CUM, BF = take(T), take(T), take(T), take(1)
            D16 = take(P)
            OT = take(KT, T)
            att = [take(1, 384) for _ in range(6)]
            pt = [take(384) for _ in range(3)]
            NM, RR = take(4, 2), take(4, 4)
            pj_fm, pj_tm = sem("fx_fm"), sem("fx_tm")
            small_in = sem("fx_small_in")
            f_lin, f_abs, f_log, f_cum = sem("fx_lin"), sem("fx_abs"), sem("fx_log"), sem("fx_cum")
            cum_t, cum_ok = sem("fx_cum_t"), sem("fx_cum_ok")
            n0 = info["fox"]["c0"]
            units = []
            for h in range(16):
                pb = (h % 2) * DH
                units.append({"pair": h // 2, "pb": pb, "first": True, "last": True,
                              "cq": [CQ[:, t, h:h + 1] for t in range(2)],
                              "cum": (SEL[pb:pb + DH, h * P:(h + 1) * P], CUM2[pb:pb + DH, :]),
                              "subs": [{"q": Q[pb:pb + DH, h // 2, :], "k": KF[pb:pb + DH, h // 2, :],
                                        "v": [V[:, t, h * DH:(h + 1) * DH] for t in range(2)],
                                        "add": K["causal"][:, :]}]})
            soft = Soft("fox", units, 1, att, pt, NM, RR, [OT[:, p, :] for p in range(8)])

            def pe_part(pe):
                wait_xg(pe, "fox")
                for c in range(13):
                    if c == 1:
                        pe_stats(pe, "fox")
                    if c >= 4:
                        pe.wait_ge(pj_fm, min(c - 3, 9))
                        if c - 4 >= 9:
                            pe.wait_ge(pj_tm, c - 12)
                    pe_chunk(pe, n0 + c, bank[c % 4], "tm" if c >= 9 else "fm", 16 if c == 0 else CW)
                pe.wait_ge(f_cum, 1)
                pe.wait_ge(small_in, 16 * 3)
                nc.tensor.matmul(bank[4][:, 0:T], D16[0:16, :], CUM[0:16, :], start=True, stop=True).then_inc(cum_t, 1)
                for t in range(2):
                    last = nc.tensor.transpose(bank[5][:, t * 16:(t + 1) * 16], CUM[0:16, t * P:(t + 1) * P],
                                               ident[0:16, 0:16])
                last.then_inc(cum_t, 1)
                pe.wait_ge(cum_ok, 2)
                pe.wait_ge(pj_tm, 4)
                soft_pe(pe, soft)
                pe_residual(pe, "fox", n0 + 13, OT, lambda e: e.wait_ge(soft.o, 8))

            def dve_part(dve):
                dve.wait_ge(chunk_mul, n0 + 1)
                dve.wait_ge(small_in, 16 * 3)
                nc.vector.tensor_tensor(LF[0:16, :], bank[0][0:16, 0:T], rs_b[0:16, :], ALU.mult).then_inc(pj_fm, 1)
                dve.wait_ge(pj_fm, 1)
                nc.vector.tensor_scalar(LF[0:16, :], LF[0:16, :], BF[0:16, :], None, ALU.add).then_inc(f_lin, 1)
                rs2 = rs_b[:, :].unsqueeze(1).broadcast_to([P, 2, T])
                for c in range(1, 9):
                    dve.wait_ge(chunk_mul, n0 + c + 1)
                    B = bank[c % 4][:, :].rearrange("p (e t) -> p e t", e=2)
                    i = c - 1
                    dst, s = (Q[:, 2 * i:2 * i + 2, :], DH ** -0.5) if i < 4 else (KF[:, 2 * i - 8:2 * i - 6, :], 1.0)
                    nc.vector.scalar_tensor_tensor(dst, B, s, rs2, ALU.mult, ALU.mult).then_inc(pj_fm, 1)
                dve.wait_ge(f_abs, 3)
                nc.vector.scalar_tensor_tensor(LF[0:16, :], LF[0:16, :], 0.0, AB[0:16, :], ALU.min,
                                               ALU.subtract).then_inc(f_log, 1)
                dve.wait_ge(f_log, 1)
                nc.vector.tensor_tensor_scan(CUM[0:16, :], ones_w[0:16, :], LF[0:16, :], 0.0, ALU.mult,
                                             ALU.add).then_inc(f_cum, 1)
                dve.wait_ge(cum_t, 1)
                nc.vector.tensor_copy(CUM2[:, :], bank[4][:, 0:T]).then_inc(cum_ok, 1)
                dve.wait_ge(cum_t, 2)
                nc.vector.tensor_copy(CQ[:, :, :], bank[5][:, 0:32].rearrange("p (t h) -> p t h", t=2)).then_inc(cum_ok, 1)
                dve.wait_ge(cum_ok, 2)
                soft_dve(dve, soft)

            def act_part(act):
                act.dma_start(SEL[:, :], A["selneg"]).then_inc(small_in, 16)
                act.dma_start(BF[0:16, :], A["b_f"]).then_inc(small_in, 16)
                act.dma_start(D16[0:16, :], A["dup16"]).then_inc(small_in, 16)
                act.wait_ge(f_lin, 1)
                nc.scalar.activation(AB[0:16, :], LF[0:16, :], ACT.Abs).then_inc(f_abs, 1)
                act.wait_ge(f_abs, 1)
                nc.scalar.activation(AB[0:16, :], AB[0:16, :], ACT.Exp, scale=-1.0).then_inc(f_abs, 1)
                act.wait_ge(f_abs, 2)
                nc.scalar.activation(AB[0:16, :], AB[0:16, :], ACT.Ln, bias=one_c[0:16, :]).then_inc(f_abs, 1)
                act.wait_ge(rs_new, info["fox"]["st"])
                for c in range(9, 13):
                    act.wait_ge(chunk_mul, n0 + c + 1)
                    for t in range(2):
                        last = nc.scalar.activation(V[:, t, (c - 9) * CW:(c - 8) * CW], bank[c % 4][:, t * CW:(t + 1) * CW],
                                                    ACT.Copy, scale=rs_c[:, t:t + 1])
                    last.then_inc(pj_tm, 1)
                soft_act(act, soft)

            return {"pe": pe_part, "dve": dve_part, "act": act_part}

        def make_hgrn():
            top[0] = 0
            FP, SG, KK, Q, GG = (take(8, T) for _ in range(5))
            LV = [take(8, T) for _ in range(2)]
            V = take(2, D)
            SA, SBt = take(8, T), take(8, P)
            LB, OML = take(8), take(8)
            OSQ, RN, OT = FP, LV[0], LV[1]
            pj_fm, pj_tm = sem("hg_fm"), sem("hg_tm")
            lb_d, lb_s, lb_o = sem("hg_lb_d"), sem("hg_lb_s"), sem("hg_lb_o")
            sig, gate, lnf, silu, cum = sem("hg_sig"), sem("hg_gate"), sem("hg_ln"), sem("hg_silu"), sem("hg_cum")
            d_k, d_q, l_e, l_k, l_q = sem("lv_dk"), sem("lv_dq"), sem("lv_exp"), sem("lv_k"), sem("lv_q")
            l_mm, l_s = sem("lv_mm"), sem("lv_s")
            o_mm, o_sq, o_mean, o_rn, o_n, o_g = (sem("hg_o_mm"), sem("hg_o_sq"), sem("hg_o_mean"), sem("hg_o_rn"),
                                                  sem("hg_o_n"), sem("hg_o_g"))
            n0 = info["hgrn"]["c0"]
            st = info["hgrn"]["st"]
            blocks = [128, 64, 32, 16, 8, 4, 2, 1]
            groups = [("diag", 0, t, hh) for t in range(2) for hh in range(2)]
            groups += [("cross", 0, 1, hh) for hh in range(2)]
            groups += [("level", l, t, hh) for l in range(1, 8) for t in range(2) for hh in range(2)]
            by_level = [groups[0:4], groups[4:6]] + [groups[6 + 4 * l:10 + 4 * l] for l in range(7)]
            first_of = [0, 4] + [6 + 4 * l for l in range(7)]

            def level_pe(pe, l):
                if l == 0:
                    pe.wait_ge(silu, 4)
                    pe.wait_ge(gate, 16)
                else:
                    pe.wait_ge(l_k, l)
                    pe.wait_ge(l_q, l)
                for i, (kind, lv, t, hh) in enumerate(by_level[l]):
                    g = first_of[l] + i
                    if g >= 3:
                        pe.wait_ge(l_s, g - 2)
                    B = bank[4 + g % 3]
                    for k in range(4):
                        hd = 4 * hh + k
                        tt = slice(t * P, (t + 1) * P)
                        if kind == "diag":
                            lhs, rhs = KK[:, hd, tt], Q[:, hd, tt]
                        elif kind == "cross":
                            lhs, rhs = LV[0][:, hd, 0:P], LV[0][:, hd, P:T]
                        else:
                            lhs = rhs = LV[lv % 2][:, hd, tt]
                        last = nc.tensor.matmul(B[:, k * P:(k + 1) * P], lhs, rhs, start=True, stop=True)
                    last.then_inc(l_mm, 1)

            def pe_part(pe):
                wait_xg(pe, "hgrn")
                done = 0
                for c in range(16):
                    if c == 1:
                        pe_stats(pe, "hgrn")
                    if c >= 4:
                        pe.wait_ge(pj_fm, min(c - 3, 12))
                    pe_chunk(pe, n0 + c, bank[c % 4], "tm" if c >= 12 else "fm")
                    if c >= 9 and done < 9:
                        level_pe(pe, done)
                        done += 1
                for l in range(done, 9):
                    level_pe(pe, l)
                pe.wait_ge(pj_tm, 4)
                pe.wait_ge(l_s, len(groups))
                for p in range(4):
                    for e in range(2):
                        hd = 2 * p + e
                        o = bank[p][:, e * T:(e + 1) * T]
                        nc.tensor.matmul(o, V[:, 0, hd * P:(hd + 1) * P], SA[:, hd, :], start=True, stop=False)
                        last = nc.tensor.matmul(o[:, P:T], V[:, 1, hd * P:(hd + 1) * P], SBt[:, hd, :], start=False,
                                                stop=True)
                    last.then_inc(o_mm, 1)
                for p in range(4):
                    pe.wait_ge(o_sq, p + 1)
                    nc.tensor.matmul(bank[4 + p][:, :], mean_e[:, :], OSQ[:, 2 * p:2 * p + 2, :], start=True,
                                     stop=True).then_inc(o_mean, 1)
                pe_residual(pe, "hgrn", n0 + 16, OT, lambda e: e.wait_ge(o_g, 4))

            def dve_part(dve):
                rs2 = rs_b[:, :].unsqueeze(1).broadcast_to([P, 2, T])

                def evac(c):
                    dve.wait_ge(chunk_mul, n0 + c + 1)
                    B = bank[c % 4][:, :].rearrange("p (e t) -> p e t", e=2)
                    dst = (FP, Q, GG)[c // 4][:, 2 * (c % 4):2 * (c % 4) + 2, :]
                    nc.vector.tensor_tensor(dst, B, rs2, ALU.mult).then_inc(pj_fm, 1)

                nc.vector.tensor_tensor(LB[:, :], vecs[:, ROW_LB:ROW_LB + 8], vecs[:, ROW_LB + 8:ROW_LB + 16],
                                        ALU.subtract).then_inc(lb_d, 1)
                dve.wait_ge(lb_s, 1)
                nc.vector.tensor_scalar(OML[:, :], LB[:, :], -1.0, 1.0, ALU.mult, ALU.add).then_inc(lb_o, 1)
                dve.wait_ge(lb_o, 1)
                for c in range(4):
                    evac(c)
                for hd in range(8):
                    dve.wait_ge(sig, 2 * (hd // 2) + 2)
                    nc.vector.tensor_scalar(SG[:, hd, :], SG[:, hd, :], OML[:, hd:hd + 1], LB[:, hd:hd + 1], ALU.mult,
                                            ALU.add).then_inc(gate, 1)
                    nc.vector.tensor_scalar(KK[:, hd, :], KK[:, hd, :], OML[:, hd:hd + 1], None,
                                            ALU.mult).then_inc(gate, 1)
                for c in range(4, 8):
                    evac(c)
                dve.wait_ge(lnf, 1)
                for hd in range(8):
                    nc.vector.tensor_tensor_scan(FP[:, hd, :], ones_w[:, :], SG[:, hd, :], 0.0, ALU.mult,
                                                 ALU.add).then_inc(cum, 1)
                dve.wait_ge(cum, 8)
                evac(8)

                def diff(l):
                    b, buf = blocks[l], LV[l % 2]
                    if l >= 2:
                        dve.wait_ge(l_mm, first_of[l])
                    cv = FP[:, :, :].rearrange("p h (n two b) -> p (h n) two b", two=2, b=b)
                    lv = buf[:, :, :].rearrange("p h (n two b) -> p (h n) two b", two=2, b=b)
                    ref = cv[:, :, 1, 0:1].broadcast_to([P, 8 * T // (2 * b), b])
                    nc.vector.tensor_tensor(lv[:, :, 0, :], ref, cv[:, :, 0, :], ALU.subtract).then_inc(d_k, 1)

                def keys(l):
                    b, buf = blocks[l], LV[l % 2]
                    dve.wait_ge(l_e, l + 1)
                    kv = KK[:, :, :].rearrange("p h (n two b) -> p (h n) two b", two=2, b=b)
                    lv = buf[:, :, :].rearrange("p h (n two b) -> p (h n) two b", two=2, b=b)
                    nc.vector.tensor_tensor(lv[:, :, 0, :], lv[:, :, 0, :], kv[:, :, 0, :], ALU.mult).then_inc(l_k, 1)

                def take_out(l):
                    for i, (kind, lv, t, hh) in enumerate(by_level[l]):
                        g = first_of[l] + i
                        dve.wait_ge(l_mm, g + 1)
                        B = bank[4 + g % 3][:, :].rearrange("p (h t) -> p h t", h=4)
                        hs = slice(4 * hh, 4 * hh + 4)
                        dst = SBt[:, hs, :] if t and kind != "cross" else SA[:, hs, 0:P]
                        m = K["level"][:, lv * P:(lv + 1) * P]
                        if kind == "diag":
                            ins = nc.vector.tensor_tensor(dst, B, m.unsqueeze(1).broadcast_to([P, 4, P]), ALU.mult)
                        elif kind == "cross":
                            ins = nc.vector.tensor_copy(SA[:, hs, P:T], B)
                        else:
                            ins = nc.vector.copy_predicated(dst, m.bitcast(U32).unsqueeze(1).broadcast_to([P, 4, P]), B)
                        ins.then_inc(l_s, 1)

                more = [9, 10, 11]
                diff(0)
                for l in range(8):
                    keys(l)
                    if more:
                        evac(more.pop(0))
                    take_out(l)
                    if l + 1 < 8:
                        diff(l + 1)
                take_out(8)
                for p in range(4):
                    dve.wait_ge(o_rn, 8)
                    dst = OT[:, 2 * p:2 * p + 2, :]
                    nc.vector.scalar_tensor_tensor(dst, bank[p][:, :].rearrange("p (e t) -> p e t", e=2),
                                                   vecs[:, ROW_OUT_GAIN:ROW_OUT_GAIN + 1], RN[:, 2 * p:2 * p + 2, :],
                                                   ALU.mult, ALU.mult).then_inc(o_n, 1)
                    dve.wait_ge(o_n, p + 1)
                    nc.vector.tensor_tensor(dst, dst, GG[:, 2 * p:2 * p + 2, :], ALU.mult).then_inc(o_g, 1)

            def act_part(act):
                act.wait_ge(lb_d, 1)
                nc.scalar.activation(LB[:, :], LB[:, :], ACT.Sigmoid).then_inc(lb_s, 1)
                for c in range(4):
                    act.wait_ge(pj_fm, c + 1)
                    two = slice(2 * c, 2 * c + 2)
                    nc.scalar.activation(SG[:, two, :], FP[:, two, :], ACT.Sigmoid).then_inc(sig, 1)
                    nc.scalar.activation(KK[:, two, :], FP[:, two, :], ACT.Sigmoid, scale=-1.0).then_inc(sig, 1)
                act.wait_ge(gate, 15)
                nc.scalar.activation(SG[:, :, :], SG[:, :, :], ACT.Ln).then_inc(lnf, 1)
                for c in range(4):
                    act.wait_ge(pj_fm, 5 + c)
                    nc.scalar.activation(Q[:, 2 * c:2 * c + 2, :], Q[:, 2 * c:2 * c + 2, :], ACT.Silu).then_inc(silu, 1)
                act.wait_ge(rs_new, st)

                def v_out(c):
                    act.wait_ge(chunk_mul, n0 + c + 1)
                    for t in range(2):
                        last = nc.scalar.activation(V[:, t, (c - 12) * CW:(c - 11) * CW],
                                                    bank[c % 4][:, t * CW:(t + 1) * CW], ACT.Copy, scale=rs_c[:, t:t + 1])
                    last.then_inc(pj_tm, 1)

                for l in range(8):
                    act.wait_ge(d_k, l + 1)
                    act.wait_ge(d_q, l + 1)
                    nc.scalar.activation(LV[l % 2][:, :, :], LV[l % 2][:, :, :], ACT.Exp).then_inc(l_e, 1)
                    if 4 <= l:
                        v_out(12 + l - 4)
                act.wait_ge(pj_fm, 12)
                nc.scalar.activation(GG[:, :, :], GG[:, :, :], ACT.Silu).then_inc(silu, 1)
                for p in range(4):
                    act.wait_ge(o_mm, p + 1)
                    nc.scalar.activation(OSQ[:, 2 * p:2 * p + 2, :], bank[p][:, :].rearrange("p (e t) -> p e t", e=2),
                                         ACT.Square).then_inc(o_sq, 1)
                for p in range(4):
                    act.wait_ge(o_mean, p + 1)
                    nc.scalar.activation(RN[:, 2 * p:2 * p + 2, :], bank[4 + p][:, :].rearrange("p (e t) -> p e t", e=2),
                                         ACT.Ln, bias=eps_c[:, :]).then_inc(o_rn, 1)
                for p in range(4):
                    act.wait_ge(o_rn, p + 1)
                    nc.scalar.activation(RN[:, 2 * p:2 * p + 2, :], RN[:, 2 * p:2 * p + 2, :], ACT.Exp,
                                         scale=-0.5).then_inc(o_rn, 1)

            def pool_part(pool):
                for l in range(8):
                    b, buf = blocks[l], LV[l % 2]
                    cv = FP[:, :, :].rearrange("p h (n two b) -> p (h n) two b", two=2, b=b)
                    lv = buf[:, :, :].rearrange("p h (n two b) -> p (h n) two b", two=2, b=b)
                    qv = Q[:, :, :].rearrange("p h (n two b) -> p (h n) two b", two=2, b=b)
                    ref = cv[:, :, 1, 0:1].broadcast_to([P, 8 * T // (2 * b), b])
                    pool.wait_ge(cum, 8)
                    if l >= 2:
                        pool.wait_ge(l_mm, first_of[l])
                    nc.gpsimd.tensor_tensor(lv[:, :, 1, :], cv[:, :, 1, :], ref, ALU.subtract).then_inc(d_q, 1)
                    pool.wait_ge(silu, 4)
                    pool.wait_ge(l_e, l + 1)
                    nc.gpsimd.tensor_tensor(lv[:, :, 1, :], lv[:, :, 1, :], qv[:, :, 1, :], ALU.mult).then_inc(l_q, 1)

            return {"pe": pe_part, "dve": dve_part, "act": act_part, "pool": pool_part}

        def turned_round(v):
            return v.rearrange("p e (a b) -> p e a b", a=2)[:, :, :, ::-1]

        def make_head_norm(tag, dst, gain, tmp_sq, tmp_r, reverse=False):
            s = {k: sem(f"{tag}_{k}") for k in ("lin", "sqr", "mean", "root", "rec", "done")}
            n0, st = info[tag]["c0"], info[tag]["st"]

            def mean(pe, c):
                pe.wait_ge(s["sqr"], c + 1)
                if c >= 2:
                    pe.wait_ge(s["root"], c - 1)
                nc.tensor.matmul(bank[4 + c % 2][:, :], K["block64"][:, :], tmp_sq[c % 2], start=True,
                                 stop=True).then_inc(s["mean"], 1)

            def pe_part(pe):
                for c in range(12):
                    if c == 1:
                        pe_stats(pe, tag)
                    if c >= 4:
                        pe.wait_ge(s["lin"], c - 3)
                    pe_chunk(pe, n0 + c, bank[c % 4], "fm")
                    if c >= 1:
                        mean(pe, c - 1)

            def dve_part(dve):
                rs2 = rs_b[:, :].unsqueeze(1).broadcast_to([P, 2, T])
                for c in range(13):
                    if c < 12:
                        dve.wait_ge(chunk_mul, n0 + c + 1)
                        B = bank[c % 4][:, :].rearrange("p (e t) -> p e t", e=2)
                        d2, r2 = dst[:, 2 * c:2 * c + 2, :], rs2
                        if reverse:
                            d2, B, r2 = turned_round(d2), *(v.rearrange("p e (a b) -> p e a b", a=2) for v in (B, rs2))
                        nc.vector.tensor_tensor(d2, B, r2, ALU.mult).then_inc(s["lin"], 1)
                    if c >= 1:
                        k = c - 1
                        dve.wait_ge(s["root"], k + 1)
                        nc.vector.reciprocal(tmp_r[k % 2], tmp_r[k % 2]).then_inc(s["rec"], 1)
                        dve.wait_ge(s["rec"], k + 1)
                        d2 = dst[:, 2 * k:2 * k + 2, :]
                        nc.vector.scalar_tensor_tensor(d2, d2, gain(k // 4), tmp_r[k % 2], ALU.mult,
                                                       ALU.mult).then_inc(s["done"], 1)

            def act_part(act):
                for c in range(13):
                    if c < 12:
                        act.wait_ge(s["lin"], c + 1)
                        if c >= 2:
                            act.wait_ge(s["mean"], c - 1)
                        nc.scalar.activation(tmp_sq[c % 2], dst[:, 2 * c:2 * c + 2, :], ACT.Square).then_inc(s["sqr"], 1)
                    if c >= 1:
                        k = c - 1
                        act.wait_ge(s["mean"], k + 1)
                        if k >= 2:
                            act.wait_ge(s["done"], k - 1)
                        nc.scalar.activation(tmp_r[k % 2], bank[4 + k % 2][:, :].rearrange("p (e t) -> p e t", e=2),
                                             ACT.Sqrt, bias=eps_c[:, :]).then_inc(s["root"], 1)

            return s, mean, pe_part, dve_part, act_part

        rel_rows = nc.dram_tensor("rel_rows", (16, 3 * 384), F32, kind="Internal").ap() if "kv" in plan else None
        rel_sent = sem("rel_sent") if "kv" in plan else None

        def make_kv():
            top[0] = F0
            tmp_sq, tmp_r = [take(2, T) for _ in range(2)], [take(2, T) for _ in range(2)]
            HOT, RM, RV, RB = take(3, 384), take(3, 384), take(3, 384), take(48)
            n0 = info["kv"]["c0"]
            s, mean, pe_n, dve_n, act_n = make_head_norm(
                "kv", DK, lambda g: vecs[:, ROW_KG + g:ROW_KG + g + 1], tmp_sq, tmp_r)
            small_in, rel_mm, rel_ok, v_ok = sem("kv_small_in"), sem("kv_rel_mm"), sem("kv_rel_ok"), sem("kv_v")

            def pe_part(pe):
                wait_xg(pe, "kv")
                pe_n(pe)
                for c in range(12, 24):
                    if c < 16:
                        pe.wait_ge(s["lin"], c - 3)
                    else:
                        pe.wait_ge(v_ok, c - 15)
                    pe_chunk(pe, n0 + c, bank[c % 4], "tm")
                    if c == 12:
                        mean(pe, 11)
                    if c == 13:
                        pe.wait_ge(small_in, 16 * 3)
                        for g in range(3):
                            if g == 2:
                                pe.wait_ge(rel_ok, 1)
                            nc.tensor.matmul(bank[6 + g % 2][0:16, 0:384], RB[0:32, 16 * g:16 * g + 16],
                                             HOT[0:32, g, :], start=True, stop=True).then_inc(rel_mm, 1)
                pe.wait_ge(v_ok, 12)
                pe.wait_ge(rel_ok, 3)

            def dve_part(dve):
                dve_n(dve)
                dve.wait_ge(small_in, 16 * 3)
                for g in range(3):
                    dve.wait_ge(rel_mm, g + 1)
                    nc.vector.tensor_tensor(RV[0:16, g, :], bank[6 + g % 2][0:16, 0:384], RM[0:16, g, :],
                                            ALU.add).then_inc(rel_ok, 1)

            def act_part(act):
                act.dma_start(HOT[0:32, :, :], A["hot"].rearrange("b (g u) -> b g u", g=3)).then_inc(small_in, 16)
                act.dma_start(RM[0:16, :, :], A["rel_mask"].rearrange("b (g u) -> b g u", g=3)).then_inc(small_in, 16)
                act.dma_start(RB[0:32, :], A["rel_bias"]).then_inc(small_in, 16)
                act_n(act)
                act.wait_ge(rs_new, info["kv"]["st"])
                for c in range(12, 24):
                    act.wait_ge(chunk_mul, n0 + c + 1)
                    for t in range(2):
                        last = nc.scalar.activation(DV[:, t, (c - 12) * CW:(c - 11) * CW],
                                                    bank[c % 4][:, t * CW:(t + 1) * CW], ACT.Copy, scale=rs_c[:, t:t + 1])
                    last.then_inc(v_ok, 1)
                    if c == 16:
                        act.wait_ge(rel_ok, 3)
                        act.dma_start(rel_rows.rearrange("h (g u) -> h g u", g=3), RV[0:16, :, :]).then_inc(rel_sent, 16)
                act.wait_ge(rel_sent, 16)

            return {"pe": pe_part, "dve": dve_part, "act": act_part}

        def make_dilated():
            top[0] = F0
            DQ = take(24, T)
            m0 = top[0]
            tmp_sq, tmp_r = [take(2, T) for _ in range(2)], [take(2, T) for _ in range(2)]
            top[0] = m0
            att = [take(3, 384) for _ in range(3)]
            pt = [take(384) for _ in range(3)]
            REL = [take(3, 384) for _ in range(2)]
            NM, RR, QG = take(4, 2), take(4, 4), take(3)
            OT = DQ[:, 0:8, :]
            n0 = info["dilated"]["c0"]
            s, mean, pe_n, dve_n, act_n = make_head_norm("dilated", DQ, lambda g: QG[:, g:g + 1], tmp_sq, tmp_r, True)
            rel_in, qg_ok = [sem("dl_rel_in0"), sem("dl_rel_in1")], sem("dl_qg")
            units = []
            for h in range(16):
                pb = (h % 2) * DH
                units.append({"pair": h // 2, "pb": pb, "first": True, "last": True, "wait": (rel_in[h % 2], 32 * (h // 2 + 1)),
                              "subs": [{"q": DQ[pb:pb + DH, 8 * g + h // 2, :], "k": DK[pb:pb + DH, 8 * g + h // 2, :],
                                        "v": [DV[:, t, g * D + h * DH:g * D + (h + 1) * DH] for t in range(2)],
                                        "add": REL[h % 2][:, g, :]} for g in range(3)]})
            soft = Soft("dil", units, 3, att, pt, NM, RR, [turned_round(OT[:, p:p + 1, :])[:, 0] for p in range(8)])

            def pe_part(pe):
                wait_xg(pe, "dilated")
                pe_n(pe)
                mean(pe, 11)
                pe.wait_ge(s["done"], 12)
                soft_pe(pe, soft)
                pe_residual(pe, "dilated", n0 + 12, OT, lambda e: e.wait_ge(soft.o, 8))

            def dve_part(dve):
                nc.vector.tensor_scalar(QG[:, :], vecs[:, ROW_QG:ROW_QG + 3], DH ** -0.5, None, ALU.mult).then_inc(qg_ok, 1)
                dve.wait_ge(qg_ok, 1)
                dve_n(dve)
                soft_dve(dve, soft)

            def act_part(act):
                act_n(act)
                soft_act(act, soft)

            def pool_part(pool):
                pool.wait_ge(rel_sent, 16)
                pool.wait_ge(s["done"], 12)
                for h in range(16):
                    if h >= 2:
                        pool.wait_ge(soft.masked, 3 * (h - 1))
                    for lo, n, u0 in ((0, T, 0), (T, P, P)):
                        src = bass.AP(tensor=rel_rows.tensor, offset=h * 1152 + u0, ap=[[1, P], [384, 3], [1, n]])
                        pool.dma_start(REL[h % 2][:, :, lo:lo + n], src).then_inc(rel_in[h % 2], 16)

            return {"pe": pe_part, "dve": dve_part, "act": act_part, "pool": pool_part}

        makers = {"even": make_even, "fox": make_fox, "hgrn": make_hgrn, "kv": make_kv, "dilated": make_dilated}
        parts = {b: makers[b]() for b in plan if b in makers}

        block = ctx.enter_context(nc.Block())
        const_names = [n for n in sorted(K) if n != "ident"]
        loads = len(const_names)

        @block.sync
        def _(sp):
            sp.dma_start(x_rows, A["x"].rearrange("(a p) d -> p a d", p=P)).then_inc(x_tok, 16)

            def free(n, it=None):
                if it is not None:
                    sp.wait_ge(chunk_mul, RING * it + (n - RING + 1))
                elif n >= RING:
                    sp.wait_ge(chunk_mul, n - RING + 1)

            def load_cols(n, w, c0, width, it=None):
                free(n, it)
                src = w.rearrange("(k p) n -> p k n", p=P)
                sp.dma_start(slot(n, width), src[:, :, bass.ds(c0, width)] if it is not None
                             else src[:, :, c0:c0 + width]).then_inc(chunk_in[n % RING], 16)

            def load_rows(n, w, j, it=None):
                free(n, it)
                src = w[bass.ds(j * CW, CW), :] if it is not None else w[j * CW:(j + 1) * CW, :]
                sp.dma_start(ring[n % RING][:, :].rearrange("p (k n) -> p k n", k=2),
                             src.rearrange("(k p) n -> p k n", p=P)).then_inc(chunk_in[n % RING], 16)

            for b in plan:
                n = info[b]["c0"]
                if b in ffn_in:
                    wi, wo = ffn_in[b], ffn_out[b]
                    load_cols(n, wi, 0, CW)
                    load_cols(n + 1, wi, DFF, CW)
                    early = max(0, RING - (n + 2))
                    assert early == 0 or n == 0

                    def turn(i, it):
                        for s in range(2):
                            m = n + 2 + 3 * s
                            load_cols(m, wi, CW * (2 * i + 1 + s) if it is None else i * (2 * CW) + CW * (1 + s), CW, it)
                            load_cols(m + 1, wi, DFF + CW * (2 * i + 1 + s) if it is None
                                      else i * (2 * CW) + (DFF + CW * (1 + s)), CW, it)
                            load_rows(m + 2, wo, 2 * i + s if it is None else i * 2 + s, it)

                    first = 0
                    if early:
                        turn(0, None)
                        first = 1
                    with sp.Fori(first, (NJ - 1) // 2) as i:
                        turn(i, i)
                    load_rows(n + 3 * NJ - 1, wo, NJ - 1)
                else:
                    for c, (_, w, c0, width) in enumerate(streams[b]):
                        load_cols(n + c, W[w], c0, width)
            sp.wait_ge(out_sent, 16 * 2)

        @block.scalar
        def _(act):
            act.dma_start(ident[:, :], A["ident"]).then_inc(first_in, 16)
            act.dma_start(vec_in[0:VEC_ROWS, 0, :], A["vec_rows"]).then_inc(first_in, 16)
            for l in range(2):
                act.dma_start(vec_in[0:CONV_ROWS, 1 + l, :], A["conv_rows"][l]).then_inc(first_in, 16)
            for n in const_names:
                act.dma_start(K[n][:, :], A[n]).then_inc(const_in, 16)
            act.wait_ge(const_set, 1)
            act.wait_ge(vec_ok, 3)
            for b in plan:
                act_prep(act, b)
                if b in ffn_in:
                    ff_loop(act, lambda j, par, F, first, conv: act_ff_step(act, b, j, par, F, conv), b)
                elif b in parts:
                    parts[b]["act"](act)
            for t in range(2):
                for h in range(2):
                    act.wait_ge(vec_t, 4 + 2 * t + h)
                    nc.scalar.activation(sq[:, 4 * t + 2 * h:4 * t + 2 * h + 2, :], bank[2 * t + h][:, :].rearrange(
                        "p (e t) -> p e t", e=2), ACT.Copy).then_inc(sq_new, 1)
                act.wait_ge(sq_new, info["end"]["prep"]["sq0"] + 2 * t + 2)
                act.dma_start(out[t * P:(t + 1) * P, :],
                              sq[:, 4 * t:4 * t + 4, :].rearrange("p k t -> p (k t)")).then_inc(out_sent, 16)

        @block.gpsimd
        def _(pool):
            for b in plan:
                if b in parts and "pool" in parts[b]:
                    parts[b]["pool"](pool)

        @block.tensor
        def _(pe):
            pe.wait_ge(first_in, 16 * 4)
            for l in range(3):
                rows = VEC_ROWS if l == 0 else CONV_ROWS
                last = nc.tensor.transpose(bank[l][:, 0:rows], vec_in[0:rows, l, :], ident[0:rows, 0:rows])
                last.then_inc(vec_t, 1)
            pe.wait_ge(x_tok, 16)
            for b in range(4):
                for e in range(2):
                    for t in range(2):
                        d = 2 * b + e
                        last = nc.tensor.transpose(bank[4 + b][:, e * T + t * P:e * T + (t + 1) * P],
                                                   x_rows[:, t, d * P:(d + 1) * P], ident[:, :])
                last.then_inc(y_bank, 1)
            pe.wait_ge(const_set, 3)
            for b in plan:
                if b in ffn_in:
                    pe_ffn(pe, b)
                elif b == "final":
                    pe_stats(pe, b)
                else:
                    parts[b]["pe"](pe)
            pe.wait_ge(x_new, info["end"]["prep"]["x0"] + 4)
            for t in range(2):
                for h in range(2):
                    for q in range(4):
                        d = 4 * h + q
                        last = nc.tensor.transpose(bank[2 * t + h][:, q * P:(q + 1) * P], x[:, d, t * P:(t + 1) * P],
                                                   ident[:, :])
                    last.then_inc(vec_t, 1)

        @block.vector
        def _(dve):
            nc.vector.memset(one_c[:, :], 1.0).then_inc(ff_read, 2)
            nc.vector.memset(eps_c[:, :], EPS).then_inc(const_set, 1)
            nc.vector.memset(mean_d[:, :], 1.0 / D)
            nc.vector.memset(mean_e[:, :], 1.0 / P)
            nc.vector.memset(ones_w[:, :], 1.0).then_inc(const_set, 1)
            nc.vector.memset(zero16[:, :], 0.0).then_inc(const_set, 1)
            for l in range(3):
                rows = VEC_ROWS if l == 0 else CONV_ROWS
                dve.wait_ge(vec_t, l + 1)
                nc.vector.tensor_copy(vecs[:, :] if l == 0 else convv[:, l - 1, :],
                                      bank[l][:, 0:rows]).then_inc(vec_ok, 1)
            dve.wait_ge(vec_ok, 3)
            dve.wait_ge(const_set, 3)
            dve_prep(dve, plan[0], None)
            for pos, b in enumerate(plan):
                nxt = plan[pos + 1] if pos + 1 < len(plan) else "end"
                if info[b]["prep"]["kind"] != "regain":
                    dve_rs(dve, b)
                if pos == 0:
                    dve.wait_ge(const_in, 16 * loads)
                if b.startswith("conv"):
                    nc.vector.memset(ff_a[:, :, :, 0:2], 0.0)
                if b in ffn_in:
                    ff_loop(dve, lambda j, par, F, first, conv: dve_ff_step(dve, b, j, par, F, first, conv), b)
                elif b in parts:
                    parts[b]["dve"](dve)
                dve_prep(dve, nxt, alpha(b))



CONST_NAMES = ("block64", "causal", "cmp_bias", "cmp_keep", "cos", "dup", "ident", "level", "rot", "rotdup", "sb_bias",
               "sb_negkeep", "sin", "suffix")
ARENA = 27000


def lay_out(inputs):
    g = {k: np.asarray(v) for k, v in inputs.items()}
    arrays = {
        "x": g["x"].reshape(T, D),
        "ev_w_in": g["ev_w_in"][0], "ev_w_out": g["ev_w_out"][0], "od_w_in": g["od_w_in"][0],
        "od_w_out": g["od_w_out"][0], "a_w_in_2": g["a_w_in_2"][0], "a_w_out_2": g["a_w_out_2"][0],
        "w_kv_2": g["w_kv_2"], "b_w_q_2": g["b_w_q_2"][0], "b_w_o_2": g["b_w_o_2"][0],
        "ffn_w_in": g["ffn_w_in"], "ffn_w_out": g["ffn_w_out"], "ffn_w_in_2": g["ffn_w_in_2"],
        "ffn_w_out_2": g["ffn_w_out_2"], "cmp_w_k": g["ev_cmp_w_k"][0], "cmp_w_v": g["ev_cmp_w_v"][0],
        "cmp_pos": np.concatenate([g["ev_cmp_pos_k"][0]] * 2 + [g["ev_cmp_pos_v"][0]] * 2, 1),
        "b_f": g["od_b_f"].reshape(16, 1), "rel_bias": g["rel_bias_2"],
        "vec_rows": np.concatenate([
            g["attn_norm"].reshape(16, P), g["ffn_norm"].reshape(16, P), g["final_norm"].reshape(8, P),
            g["kv_norm_2"].reshape(8, P), g["norm_gain_2"].reshape(48, P), g["a_out_gain_2"].reshape(1, P),
            g["a_lb_logits_2"].reshape(16, P), np.concatenate([g["k_gain_2"]] * 2, 1),
            np.concatenate([g["b_q_gain_2"][0]] * 2, 1)], 0),
        "conv_rows": np.concatenate([g["ffn_conv_w"].reshape(2, 66, P), g["ffn_conv_b"].reshape(2, 22, P)], 1),
    }
    arrays.update(constants())
    return {k: np.ascontiguousarray(v) for k, v in arrays.items()}


def kernel(**inputs):
    import concourse.bacc as _bacc
    from concourse.bass_utils import run_bass_kernel_spmd as _run

    nc = _bacc.Bacc("TRN2", target_bir_lowering=False, num_devices=1)
    arrays = {f"in_{k}": v for k, v in lay_out(inputs).items()}
    aps = {k[3:]: nc.dram_tensor(k, a.shape, mybir.dt.from_np(a.dtype), kind="ExternalInput").ap()
           for k, a in arrays.items()}
    out = nc.dram_tensor("out", (T, D), F32, kind="ExternalOutput").ap()
    build(nc, aps, out)
    r = _run(nc, [arrays], core_ids=[0])
    return r.results[0]["out"].reshape(1, T, D)
```

```python
import math
from contextlib import ExitStack

import numpy as np

import concourse.bass as bass
from concourse import mybir

P = 128
T = 256
D = 1024
KT = D // P
DFF = 2816
CW = 256
NJ = DFF // CW
RING = 3
EPS = 1e-6
NEG = -1.0e30
DH = 64
N_CMP = 15
F32 = mybir.dt.float32
F32R = mybir.dt.float32r
BF16 = mybir.dt.bfloat16
U32 = mybir.dt.uint32
ALU = mybir.AluOpType
ACT = mybir.ActivationFunctionType
AXX = mybir.AxisListType.X
AXXY = mybir.AxisListType.XY

PLAN = ("even", "conv0", "fox", "conv1", "final", "glu0", "hgrn", "glu1", "kv", "glu2", "dilated", "glu3")
GAIN_ROW = {"even": 0, "fox": 8, "conv0": 16, "conv1": 24, "final": 32, "kv": 40, "glu0": 48, "hgrn": 56,
            "glu1": 64, "glu2": 72, "dilated": 80, "glu3": 88}
ROW_OUT_GAIN, ROW_LB, ROW_KG, ROW_QG, VEC_ROWS = 96, 97, 113, 116, 119
CONV_ROWS = 4 * (DFF // P)


def constants():
    c = {}
    idx = np.arange(P)
    c["ident"] = np.eye(P, dtype=np.float32)
    d = idx % DH
    half = 8
    inv = (np.float32(500000.0) ** (-(np.arange(half, dtype=np.float32) * np.float32(2.0 / 16)))).astype(np.float32)
    ang = np.arange(T, dtype=np.float32)[None, :] * inv[:, None]
    cos = np.ones((P, T), np.float32)
    sin = np.zeros((P, T), np.float32)
    rot = np.zeros((P, P), np.float32)
    for p in range(P):
        if d[p] < 16:
            cos[p] = np.cos(ang[d[p] % 8])
            sin[p] = np.sin(ang[d[p] % 8])
            if d[p] < 8:
                rot[p + 8, p] = -1.0
            else:
                rot[p - 8, p] = 1.0
    dup = np.stack([(idx[:, None] == DH * g + idx[None, :] % DH).astype(np.float32) for g in range(2)])
    c["cos"], c["sin"], c["rot"] = cos, sin, rot
    c["dup"] = np.concatenate(list(dup), 1)
    c["rotdup"] = np.concatenate([(dup[g] @ rot).astype(np.float32) for g in range(2)], 1)
    tri = np.where(idx[None, :] <= idx[:, None], 0.0, NEG).astype(np.float32)
    c["causal"] = np.concatenate([np.zeros((P, P), np.float32), tri, tri], 1)
    st = (idx[:, None] < idx[None, :])
    one = np.ones((P, P), bool)
    keep = np.concatenate([st, one, st], 1)
    c["sb_negkeep"] = np.where(keep, -1.0, 0.0).astype(np.float32)
    c["sb_bias"] = np.where(keep, 0.0, NEG).astype(np.float32)
    c["suffix"] = (idx[:, None] >= idx[None, :]).astype(np.float32)
    tpos = (np.arange(2)[None, :, None] * P + idx[:, None, None])
    ok = (np.arange(N_CMP) * 16 + 31)[None, None, :] <= tpos
    c["cmp_bias"] = np.where(ok, 0.0, NEG).astype(np.float32).reshape(P, 2 * N_CMP)
    c["cmp_keep"] = ok.astype(np.float32).reshape(P, 2 * N_CMP)
    lv = [np.eye(P, dtype=bool)]
    for b in (64, 32, 16, 8, 4, 2, 1):
        s, t = idx[:, None] // b, idx[None, :] // b
        lv.append((s % 2 == 0) & (t == s + 1))
    c["level"] = np.stack(lv, 1).astype(np.float32).reshape(P, 8 * P)
    c["block64"] = ((idx[:, None] // DH == idx[None, :] // DH) / np.float32(DH)).astype(np.float32)
    sel = np.zeros((P, 16, P), np.float32)
    sel[np.arange(16), np.arange(16)] = -1.0
    sel[DH + np.arange(16), np.arange(16)] = -1.0
    c["selneg"] = sel.reshape(P, 16 * P)
    c["dup16"] = (idx[None, :] % DH == idx[:16, None]).astype(np.float32)
    u = np.arange(384)
    dist = 255 - u
    hot = np.zeros((32, 3, 384), np.float32)
    msk = np.zeros((16, 3, 384), np.float32)
    for g, (w, dil) in enumerate(((128, 1), (512, 4), (2048, 16))):
        okd = (dist >= 0) & (dist <= w) & (dist % dil == 0)
        dd = np.clip(dist, 0, w).astype(np.int32)
        large = 16 + (np.log(np.maximum(dd, 1) / 16) / math.log(2048 / 16) * 16).astype(np.int32)
        bucket = np.where(dd < 16, dd, np.minimum(large, 31))
        hot[bucket[okd], g, u[okd]] = 1.0
        msk[:, g, :] = np.where(okd, 0.0, NEG)[None, :]
    c["hot"] = hot.reshape(32, 3 * 384)
    c["rel_mask"] = msk.reshape(16, 3 * 384)
    packed = {"ident": c["ident"]}
    layout = {}
    for b, names in BLOCK_CONSTS.items():
        layout[b], at = {}, 0
        for n in names:
            layout[b][n] = (at, c[n].shape[1])
            at += c[n].shape[1]
        packed["consts_" + b] = np.concatenate([c[n] for n in names], 1)
    packed.update({n: c[n] for n in ("selneg", "dup16", "hot", "rel_mask")})
    return packed, layout


BLOCK_CONSTS = {
    "even": ("causal", "cmp_bias", "cmp_keep", "cos", "sin", "rot", "dup", "rotdup", "sb_bias", "sb_negkeep",
             "suffix"),
    "fox": ("causal",), "hgrn": ("level",), "kv": ("block64",), "dilated": ("block64",),
}


def build(nc, A, out, plan=PLAN):
    ctx = ExitStack()
    with ctx:
        names = [0]

        def sb(name, shape, dt=F32):
            return ctx.enter_context(nc.sbuf_tensor(name, shape, dt))

        def sem(name):
            return ctx.enter_context(nc.semaphore(name))

        ring = [sb(f"ring{i}", [P, 2048]) for i in range(RING)]
        x = sb("x", [P, KT, T])
        hi = [sb(f"hi{i}", [P, 2048], F32R) for i in range(RING)]
        lo = [sb(f"lo{i}", [P, 2048], F32R) for i in range(RING)]
        xh = sb("xh", [P, KT, T], F32R)
        xl = sb("xl", [P, KT, T], F32R)
        gh = sb("gh", [P, 2, 2, T], F32R)
        gl = sb("gl", [P, 2, 2, T], F32R)
        rs_b = sb("rs_b", [P, T])
        std_c, rs_c = sb("std_c", [P, 2]), sb("rs_c", [P, 2])
        vecs = sb("vecs", [P, VEC_ROWS])
        convv = sb("convv", [P, 2, CONV_ROWS])
        eps_c, one_c = sb("eps_c", [P, 1]), sb("one_c", [P, 1])
        mean_d = sb("mean_d", [P, P])
        zero16 = sb("zero16", [1, P], BF16)
        ident = sb("ident", [P, P])
        bank = [ctx.enter_context(nc.psum_tensor(f"bank{i}", [P, 512], F32)) for i in range(8)]

        arena = sb("arena", [P, ARENA])
        top = [0]

        def take(*shape, at=None):
            n = int(np.prod(shape))
            o = top[0] if at is None else at
            top[0] = o + n
            assert top[0] <= ARENA, top[0]
            v = arena[:, o:o + n]
            if len(shape) == 2:
                return v.rearrange("p (a b) -> p a b", a=shape[0])
            if len(shape) == 3:
                return v.rearrange("p (a b c) -> p a b c", a=shape[0], b=shape[1])
            return v

        layout = constants()[1]

        def block_consts(b):
            n = sum(w for _, w in layout[b].values())
            buf = take(n)
            return buf, {k: buf[:, o:o + w] for k, (o, w) in layout[b].items()}, sem(b + "_const_in")

        top[0] = 0
        DK, DV = take(24, T), take(2, 3 * D)
        F0 = top[0]
        vec_in = take(3, P)
        top[0] = ARENA - (8 + 6 + 1 + 1) * T
        sq, ssum, ssq, std_b = take(8, T), take(6, T), take(T), take(T)
        top[0] = F0
        x_rows = DK[:, 0:8, :].rearrange("p k t -> p (k t)").rearrange("p (a d) -> p a d", a=2)
        ff_a = take(2, 2, 260)
        ff_c, ff_b, ff_s, ff_g = take(2, 2, T), take(2, 2, T), take(2, 2, T), take(2, 2, T)

        chunk_in = [sem(f"chunk_in{i}") for i in range(RING)]
        hi_ok = sem("hi_ok")
        lo_ok = {"V": sem("lo_ok_v"), "P": sem("lo_ok_p")}
        xh_new = sem("xh_new")
        gh_ok = sem("gh_ok")
        chunk_mul = sem("chunk_mul")
        first_in = sem("first_in")
        const_set = sem("const_set")
        vec_t = sem("vec_t")
        vec_ok = sem("vec_ok")
        y_bank = sem("y_bank")
        x_new = sem("x_new")
        xg_new = sem("xg_new")
        sq_new = sem("sq_new")
        sum_step = sem("sum_step")
        ssq_new = sem("ssq_new")
        stat_new = sem("stat_new")
        std_new = sem("std_new")
        rs_new = sem("rs_new")
        ff_read = sem("ff_read")
        ff_conv = sem("ff_conv")
        ff_silu = sem("ff_silu")
        ff_prod = sem("ff_prod")
        ff_act = sem("ff_act")
        out_sent = sem("out_sent")
        x_tok = sem("x_tok")

        def cols(w, c0, n=CW):
            return ("cols", w, c0, n)

        W = {
            "ev_in": A["ev_w_in"], "ev_out": A["ev_w_out"], "od_in": A["od_w_in"], "od_out": A["od_w_out"],
            "hg_in": A["a_w_in_2"], "hg_out": A["a_w_out_2"], "kv": A["w_kv_2"], "dq": A["b_w_q_2"],
            "do": A["b_w_o_2"],
        }
        ffn_in = {"conv0": A["ffn_w_in"][0], "conv1": A["ffn_w_in"][1]}
        ffn_out = {"conv0": A["ffn_w_out"][0], "conv1": A["ffn_w_out"][1]}
        for i in range(4):
            ffn_in[f"glu{i}"] = A["ffn_w_in_2"][i // 2, i % 2]
            ffn_out[f"glu{i}"] = A["ffn_w_out_2"][i // 2, i % 2]
        streams = {
            "even": [cols("ev_in", CW * c) for c in range(11)] + [cols("ev_in", 2816, 24)]
            + [cols("ev_out", CW * c) for c in range(4)],
            "fox": [cols("od_in", 3072, 16)] + [cols("od_in", CW * c) for c in range(12)]
            + [cols("od_out", CW * c) for c in range(4)],
            "hgrn": [cols("hg_in", c0 + CW * c) for c0 in (D, 0, 3 * D, 2 * D) for c in range(4)]
            + [cols("hg_out", CW * c) for c in range(4)],
            "kv": [cols("kv", CW * c) for c in range(24)],
            "dilated": [cols("dq", CW * c) for c in range(12)] + [cols("do", CW * c) for c in range(4)],
            "final": [],
        }
        info = {}
        n_chunk = n_y = n_x = n_ff = n_st = n_xg = n_sq = 0

        def prep(block, y):
            nonlocal n_x, n_st, n_xg, n_sq
            r = {"y": y, "x0": n_x, "xg0": n_xg, "sq0": n_sq, "st": n_st, "kind": y if isinstance(y, str) else "add"}
            if block == "end":
                n_x += 4
            else:
                if block != "final":
                    n_xg += 4
                if y != "regain":
                    n_x += 4
                    n_sq += 4
                    n_st += 1
            info.setdefault(block, {})["prep"] = r

        y_events = [("y", b + 1) for b in range(4)]
        n_y = 4
        prep(plan[0], y_events)
        for pos, b in enumerate(plan):
            me = info[b]
            me["c0"] = n_chunk
            me["st"] = n_st
            nxt = plan[pos + 1] if pos + 1 < len(plan) else "end"
            if b in ffn_in:
                me["ff0"] = n_ff
                n_ff += NJ
                n_chunk += 3 * NJ
                me["y"] = [("y", n_y + k + 1) for k in range(3)] + [("c", n_chunk)]
                n_y += 3
                prep(nxt, me["y"])
            elif b == "final":
                prep(nxt, "final")
            elif b == "kv":
                n_chunk += len(streams[b])
                prep(nxt, "regain")
            else:
                n_chunk += len(streams[b])
                me["y"] = [("c", n_chunk - 3 + k) for k in range(4)]
                prep(nxt, me["y"])
        total_chunks = n_chunk

        lo_by = []
        for b in plan:
            if b in ffn_in:
                lo_by += ["V", "V"] + ["V", "V", "P"] * (NJ - 1) + ["P"]
            elif b in ("kv", "dilated"):
                lo_by += ["P" if c < 12 else "V" for c in range(len(streams[b]))]
            elif b == "hgrn":
                lo_by += ["V"] * len(streams[b])
            else:
                lo_by += ["P" if c % 3 == 2 else "V" for c in range(len(streams[b]))]
        lo_count = [lo_by[:n + 1].count(e) for n, e in enumerate(lo_by)]
        words = []
        for b in plan:
            words += [2 * D] * (3 * NJ) if b in ffn_in else [KT * width for _, _, _, width in streams[b]]
        assert len(lo_by) == len(words) == total_chunks
        PER_TURN = {"V": 4, "P": 2}
        CHUNKS_TURN = 6
        done_hi, done_lo = [0], [0]

        def wait_split(eng, n, it=None):
            if it is None:
                eng.wait_ge(lo_ok[lo_by[n]], lo_count[n])
            else:
                e = lo_by[n + CHUNKS_TURN]
                eng.wait_ge(lo_ok[e], PER_TURN[e] * it + (lo_count[n + CHUNKS_TURN] - PER_TURN[e]))

        def split_hi(act, n, it=0):
            act.wait_ge(chunk_in[n % RING], 16 * (n // RING + 1) + 16 * (CHUNKS_TURN // RING) * it)
            if n >= RING:
                act.wait_ge(chunk_mul, n - RING + 1 + CHUNKS_TURN * it)
            nc.scalar.activation(hi[n % RING][:, 0:words[n]], ring[n % RING][:, 0:words[n]], ACT.Copy).then_inc(hi_ok, 1)

        def split_lo(eng, ns, n, it=0):
            eng.wait_ge(hi_ok, n + 1 + CHUNKS_TURN * it)
            w = words[n]
            ns.tensor_tensor(lo[n % RING][:, 0:w], ring[n % RING][:, 0:w], hi[n % RING][:, 0:w].bitcast(F32),
                             ALU.subtract).then_inc(lo_ok[lo_by[n]], 1)

        def hi_until(act, n):
            while done_hi[0] <= min(n, total_chunks - 1):
                split_hi(act, done_hi[0])
                done_hi[0] += 1

        def lo_until(dve, n):
            while done_lo[0] <= min(n, total_chunks - 1):
                if lo_by[done_lo[0]] == "V":
                    split_lo(dve, nc.vector, done_lo[0])
                done_lo[0] += 1

        def alpha(b):
            return 0.5 if b.startswith("glu") else 1.0

        before = {plan[i + 1] if i + 1 < len(plan) else "end": plan[i] for i in range(len(plan))}

        def slot(n, width=CW, of=None):
            return (ring if of is None else of)[n % RING][:, 0:KT * width].rearrange("p (k n) -> p k n", k=KT)

        def product(out_, lh, ll, rh, rl, start, stop, **kw):
            nc.tensor.matmul(out_, lh, rh, start=start, stop=False, **kw)
            nc.tensor.matmul(out_, lh, rl, start=False, stop=False, **kw)
            return nc.tensor.matmul(out_, ll, rh, start=False, stop=stop, **kw)

        class Soft:
            def __init__(self, tag, units, ns, att, pt, nm, rr, copies):
                self.units, self.ns, self.att, self.pt, self.nm, self.rr = units, ns, att, pt, nm, rr
                self.lag = 3 if ns == 1 else 2
                self.nr = len(att)
                self.copies = copies
                self.before = {"pe": {}, "dve": {}, "act": {}}
                self.qk = sem(tag + "_qk")
                self.masked = sem(tag + "_masked")
                self.max = sem(tag + "_max")
                self.exp = sem(tag + "_exp")
                self.rec = sem(tag + "_rec")
                self.p = sem(tag + "_p")
                self.turned = sem(tag + "_turned")
                self.ptok = sem(tag + "_pt")
                self.pv = sem(tag + "_pv")
                self.oh = sem(tag + "_oh")
                self.o = sem(tag + "_o")

        def soft_pe(pe, s):
            U, ns = len(s.units), s.ns

            def pv(w):
                u, g = divmod(w, ns)
                un = s.units[u]
                ob, pb = bank[6 + un["pair"] % 2], un["pb"]
                pe.wait_ge(s.ptok, w + 1)
                if un["first"] and pb == 0 and g == 0 and un["pair"] >= 2:
                    pe.wait_ge(s.o, un["pair"] - 1)
                q = s.pt[w % 3]
                sub = un["subs"][g]
                if un.get("cmp") is not None:
                    lhs, rhs = un["cmp"]
                    nc.tensor.matmul(ob[pb:pb + DH, 0:T], lhs, rhs, start=False, stop=False, skip_group_check=True)
                nc.tensor.matmul(ob[pb:pb + DH, 0:T], sub["v"][0], q[:, 0:T], start=un["first"] and g == 0,
                                 stop=False, skip_group_check=True)
                nc.tensor.matmul(ob[pb:pb + DH, P:T], sub["v"][1], q[:, T:384], start=False,
                                 stop=un["last"] and g == ns - 1, skip_group_check=True).then_inc(s.pv, 1)

            for i in range(U + s.lag):
                if i in s.before["pe"]:
                    s.before["pe"][i](pe)
                if i < U:
                    if s.units[i].get("ready") is not None:
                        pe.wait_ge(*s.units[i]["ready"])
                    for g in range(ns):
                        w = i * ns + g
                        sub = s.units[i]["subs"][g]
                        if w >= 3:
                            pe.wait_ge(s.masked, w - 2)
                        S = bank[w % 3]
                        cum = s.units[i].get("cum")
                        one = cum is None
                        nc.tensor.matmul(S[:, 0:T], sub["q"][:, P:T], sub["k"][:, 0:T], start=True, stop=one)
                        if not one:
                            nc.tensor.matmul(S[:, 0:T], cum[0], cum[1][:, 0:T], start=False, stop=True)
                        last = nc.tensor.matmul(S[:, T:384], sub["q"][:, 0:P], sub["k"][:, 0:P], start=True, stop=one)
                        if not one:
                            last = nc.tensor.matmul(S[:, T:384], cum[0], cum[1][:, 0:P], start=False, stop=True)
                        last.then_inc(s.qk, 1)
                j = i - s.lag
                if j >= 0:
                    pe.wait_ge(s.p, j + 1)
                    for g in range(ns):
                        w = j * ns + g
                        if w >= 2:
                            pe.wait_ge(s.ptok, w - 1)
                        B = bank[3 + w % 2]
                        e = s.att[j % s.nr][:, g, :]
                        nc.tensor.transpose(B[:, 0:P], e[:, T:384], ident[:, :])
                        nc.tensor.transpose(B[:, P:T], e[:, 0:P], ident[:, :])
                        nc.tensor.transpose(B[:, T:384], e[:, P:T], ident[:, :]).then_inc(s.turned, 1)
                        if w >= 1:
                            pv(w - 1)
            pv(U * ns - 1)

        def soft_dve(dve, s):
            U, ns = len(s.units), s.ns
            nrec = [0]

            def weights(u):
                un = s.units[u]
                dve.wait_ge(s.exp, u + 1)
                r = s.rr[:, u % 4, 2:4]
                nc.vector.reciprocal(r, s.rr[:, u % 4, 0:2]).then_inc(s.rec, 1)
                nrec[0] += 1
                dve.wait_ge(s.rec, nrec[0])
                if un.get("gate") is not None:
                    nc.vector.tensor_tensor(r, r, un["gate"], ALU.mult).then_inc(s.rec, 1)
                    nrec[0] += 1
                    dve.wait_ge(s.rec, nrec[0])
                e = s.att[u % s.nr]
                nc.vector.tensor_scalar(e[:, :, 0:T], e[:, :, 0:T], s.rr[:, u % 4, 3:4], None, ALU.mult)
                nc.vector.tensor_scalar(e[:, :, T:384], e[:, :, T:384], s.rr[:, u % 4, 2:3], None,
                                        ALU.mult).then_inc(s.p, 1)

            def pair_low(u):
                if u >= 0 and s.units[u]["last"] and s.units[u]["pb"] == DH:
                    pair = s.units[u]["pair"]
                    dve.wait_ge(s.oh, pair + 1)
                    h, l, src = s.copies(pair, bank[6 + pair % 2][:, 0:T])
                    nc.vector.tensor_tensor(l, src, h.bitcast(F32), ALU.subtract).then_inc(s.o, 1)

            for i in range(U + 1):
                if i in s.before["dve"]:
                    s.before["dve"][i](dve)
                if i >= s.lag + 2:
                    pair_low(i - s.lag - 2)
                if i < U:
                    un = s.units[i]
                    if i >= s.nr:
                        dve.wait_ge(s.turned, ns * (i - s.nr + 1))
                    e = s.att[i % s.nr]
                    if un.get("wait") is not None:
                        dve.wait_ge(*un["wait"])
                    for g in range(ns):
                        w = i * ns + g
                        S = bank[w % 3]
                        add = un["subs"][g]["add"]
                        dve.wait_ge(s.qk, w + 1)
                        if un.get("cq") is not None:
                            nc.vector.scalar_tensor_tensor(e[:, g, 0:T], S[:, 0:T], un["cq"][1], add[:, 0:T],
                                                           ALU.add, ALU.add)
                            nc.vector.scalar_tensor_tensor(e[:, g, T:384], S[:, T:384], un["cq"][0], add[:, T:384],
                                                           ALU.add, ALU.add).then_inc(s.masked, 1)
                        else:
                            nc.vector.tensor_tensor(e[:, g, :], S[:, 0:384], add, ALU.add).then_inc(s.masked, 1)
                    dve.wait_ge(s.masked, (i + 1) * ns)
                    nm = s.nm[:, i % 4, :]
                    nc.vector.tensor_reduce(nm[:, 1:2], e[:, :, 0:T], AXXY, ALU.max, negate=True)
                    nc.vector.tensor_reduce(nm[:, 0:1], e[:, :, T:384], AXXY, ALU.max, negate=True).then_inc(s.max, 1)
                if i >= 1:
                    weights(i - 1)
            for u in range(U - 1 - s.lag, U):
                pair_low(u)

        def soft_act(act, s):
            U, ns = len(s.units), s.ns

            def pair_out(u):
                un = s.units[u]
                if un["last"] and un["pb"] == DH:
                    act.wait_ge(s.pv, ns * (u + 1))
                    h, _, src = s.copies(un["pair"], bank[6 + un["pair"] % 2][:, 0:T])
                    nc.scalar.activation(h, src, ACT.Copy).then_inc(s.oh, 1)

            for i in range(U + s.lag):
                if i in s.before["act"]:
                    s.before["act"][i](act)
                u = i - 1
                if 0 <= u < U:
                    act.wait_ge(s.max, u + 1)
                    e = s.att[u % s.nr]
                    nc.scalar.activation(e[:, :, 0:T], e[:, :, 0:T], ACT.Exp, bias=s.nm[:, u % 4, 1:2],
                                         accum_out=s.rr[:, u % 4, 1:2])
                    nc.scalar.activation(e[:, :, T:384], e[:, :, T:384], ACT.Exp, bias=s.nm[:, u % 4, 0:1],
                                         accum_out=s.rr[:, u % 4, 0:1]).then_inc(s.exp, 1)
                j = i - s.lag
                if j >= 1:
                    pair_out(j - 1)
                if j >= 0:
                    for g in range(ns):
                        w = j * ns + g
                        act.wait_ge(s.turned, w + 1)
                        if w >= 3:
                            act.wait_ge(s.pv, w - 2)
                        nc.scalar.activation(s.pt[w % 3], bank[3 + w % 2][:, 0:384], ACT.Copy).then_inc(s.ptok, 1)
            pair_out(U - 1)

        def pe_stats(pe, b):
            st = info[b]["st"]
            pe.wait_ge(ssq_new, st)
            nc.tensor.matmul(bank[7][:, 0:T], mean_d[:, :], ssq[:, :], start=True, stop=True)
            nc.tensor.matmul(bank[7][:, T:T + 1], ssq[:, 0:P], mean_d[:, 0:1], start=True, stop=True)
            nc.tensor.matmul(bank[7][:, T + 1:T + 2], ssq[:, P:T], mean_d[:, 0:1], start=True,
                             stop=True).then_inc(stat_new, 1)

        def pe_chunk(pe, n, B, mode, width=CW, first=None, tiles=None):
            wait_split(pe, n)
            wh, wl = slot(n, width, hi), slot(n, width, lo)
            last = None
            if mode == "fm":
                for e in range(0, width, P):
                    m = min(P, width - e)
                    for k in range(KT):
                        if first is not None and e == 0 and k % 2 == 0:
                            pe.wait_ge(xg_new, first + k // 2 + 1)
                        if tiles is not None and e == 0:
                            tiles(k)
                        last = product(B[0:m, (e // P) * T:(e // P + 1) * T], wh[:, k, e:e + m], wl[:, k, e:e + m],
                                       xh[:, k, :], xl[:, k, :], k == 0, k == KT - 1)
            elif mode == "tm":
                for t in range(2):
                    tt = slice(t * P, (t + 1) * P)
                    for k in range(KT):
                        last = product(B[:, t * CW:t * CW + width], xh[:, k, tt], xl[:, k, tt], wh[:, k, :], wl[:, k, :],
                                       k == 0, k == KT - 1)
            last.then_inc(chunk_mul, 1)

        def pe_residual(pe, b, n0, tiles):
            for i in range(4):
                pe_chunk(pe, n0 + i, bank[4 + i], "fm", tiles=tiles if i == 0 else None)

        def first_xg(b):
            return info[b]["prep"]["xg0"]

        def ff_in(pe, j, par, n, F, first, it=None):
            if first is None:
                pe.wait_ge(ff_read, 2 * (F + j))
            for h in range(2):
                wait_split(pe, n + h, it)
                wh, wl = slot(n + h, of=hi), slot(n + h, of=lo)
                B = bank[2 * par + h]
                for e in range(2):
                    ee = slice(e * P, (e + 1) * P)
                    for k in range(KT):
                        if first is not None and h == 0 and e == 0 and k % 2 == 0:
                            pe.wait_ge(xg_new, first + k // 2 + 1)
                        last = product(B[:, e * T:(e + 1) * T], wh[:, k, ee], wl[:, k, ee], xh[:, k, :], xl[:, k, :],
                                       k == 0, k == KT - 1)
                last.then_inc(chunk_mul, 1)

        def ff_out(pe, j, par, n, F, it=None, tail=False):
            pe.wait_ge(ff_act, F + j + 1)
            wait_split(pe, n, it)
            wh = hi[n % RING][:, :].rearrange("p (k n) -> p k n", k=2)
            wl = lo[n % RING][:, :].rearrange("p (k n) -> p k n", k=2)
            for d in range(KT):
                dd = slice(d * P, (d + 1) * P)
                for k in range(2):
                    last = product(bank[4 + d // 2][:, (d % 2) * T:(d % 2 + 1) * T], wh[:, k, dd], wl[:, k, dd],
                                   gh[:, par, k, :], gl[:, par, k, :], False, tail and k == 1, skip_group_check=True)
                if tail and d in (1, 3, 5):
                    last.then_inc(y_bank, 1)
            last.then_inc(chunk_mul, 1)

        LOOPED = (NJ - 1) // 2 - 1

        def pe_ffn(pe, b):
            F, n = info[b]["ff0"], info[b]["c0"]
            ff_in(pe, 0, 0, n, F, first_xg(b))
            if info[b]["prep"]["kind"] != "regain":
                pe_stats(pe, b)
            for y in range(4, 8):
                if y == 7 and info[b]["prep"]["kind"] != "regain":
                    pe.wait_ge(std_new, info[b]["st"])
                nc.tensor.matmul(bank[y][:, :], zero16[:, :], zero16[:, :].unsqueeze(1).broadcast_to([1, 4, P]), start=True, stop=False,
                                 skip_group_check=True)

            def turn(j0, m0, it):
                for s in range(2):
                    m = m0 + 3 * s
                    ff_in(pe, j0 + s, (1 + s) % 2, m, F, None, it)
                    ff_out(pe, j0 + (s - 1), s, m + 2, F, it)

            with pe.Fori(0, LOOPED) as i:
                turn(2 * i + 1, n + 2, i)
            turn(2 * LOOPED + 1, n + 2 + CHUNKS_TURN * LOOPED, None)
            ff_out(pe, NJ - 1, (NJ - 1) % 2, n + 3 * NJ - 1, F, None, True)

        def dve_ff_step(dve, b, j, par, F, first, conv, it=None):
            n = info[b]["c0"] + (0 if first else 2)
            m = n if first else n + 3 * (par == 0) + (0 if it is not None else CHUNKS_TURN * LOOPED)
            c_of = chunk_of_step(b, j, first)
            if it is not None:
                split_lo(dve, nc.vector, m + 3, it)
            elif not first:
                lo_until(dve, m + 3)
            rs2 = rs_b[:, :].unsqueeze(1).broadcast_to([P, 2, T])
            dve.wait_ge(chunk_mul, c_of)
            ga = bank[2 * par][:, :].rearrange("p (e t) -> p e t", e=2)
            ub = bank[2 * par + 1][:, :].rearrange("p (e t) -> p e t", e=2)
            dst = ff_a[:, par, :, 2:2 + T] if conv is not None else ff_c[:, par, :, :]
            nc.vector.tensor_tensor(dst, ga, rs2, ALU.mult).then_inc(ff_read, 1)
            nc.vector.tensor_tensor(ff_b[:, par, :, :], ub, rs2, ALU.mult).then_inc(ff_read, 1)
            if it is not None:
                split_lo(dve, nc.vector, m + 4, it)
            else:
                lo_until(dve, m + 4)
            if conv is not None:
                layer, G = conv
                C = 3 * (G + j)
                nt = DFF // P
                for tap in range(3):
                    if tap == 0:
                        dve.wait_ge(ff_read, 2 * (F + j) + 3)
                    else:
                        dve.wait_ge(ff_conv, C + tap)
                    for e in range(2):
                        w = convv[:, layer, bass.ds(2 * j + (tap * nt + e), 1)]
                        a = ff_a[:, par, e, tap:tap + T]
                        c = ff_c[:, par, e, :]
                        if tap == 0:
                            last = nc.vector.tensor_scalar(c, a, w, None, ALU.mult)
                        else:
                            last = nc.vector.scalar_tensor_tensor(c, a, w, c, ALU.mult, ALU.add)
                    last.then_inc(ff_conv, 1)
            dve.wait_ge(ff_silu, F + j + 1)
            dve.wait_ge(ff_read, 2 * (F + j) + 4)
            nc.vector.tensor_tensor(ff_g[:, par, :, :], ff_s[:, par, :, :], ff_b[:, par, :, :],
                                    ALU.mult).then_inc(ff_prod, 1)
            dve.wait_ge(gh_ok, F + j + 1)
            nc.vector.tensor_tensor(gl[:, par, :, :], ff_g[:, par, :, :], gh[:, par, :, :].bitcast(F32),
                                    ALU.subtract).then_inc(ff_act, 1)

        def chunk_of_step(b, j, first):
            n = info[b]["c0"]
            return n + 2 if first else (j * 3) + (n + 1)

        def act_ff_step(act, b, j, par, F, first, conv, it=None):
            n = info[b]["c0"] + (0 if first else 2)
            m = n if first else n + 3 * (par == 0) + (0 if it is not None else CHUNKS_TURN * LOOPED)
            if it is None:
                hi_until(act, m + 4)
            else:
                for c in (m + 3, m + 4):
                    split_hi(act, c, it)
            if conv is None:
                act.wait_ge(ff_read, 2 * (F + j) + 3)
                nc.scalar.activation(ff_s[:, par, :, :], ff_c[:, par, :, :], ACT.Silu).then_inc(ff_silu, 1)
            else:
                layer, G = conv
                act.wait_ge(ff_conv, 3 * (G + j) + 3)
                for e in range(2):
                    last = nc.scalar.activation(ff_s[:, par, e, :], ff_c[:, par, e, :], ACT.Silu,
                                                bias=convv[:, layer, bass.ds(2 * j + (3 * (DFF // P) + e), 1)])
                last.then_inc(ff_silu, 1)
            act.wait_ge(ff_prod, F + j + 1)
            nc.scalar.activation(gh[:, par, :, :], ff_g[:, par, :, :], ACT.Copy).then_inc(gh_ok, 1)
            if it is not None:
                split_hi(act, m + 5, it)
            elif not first:
                hi_until(act, m + 5)

        def ff_loop(eng, step, b, done):
            F = info[b]["ff0"]
            conv = None
            if b.startswith("conv"):
                before_convs = [c for c in plan[:plan.index(b)] if c.startswith("conv")]
                conv = (int(b[-1]), NJ * len(before_convs))
            step(0, 0, F, True, conv, None)
            with eng.Fori(0, LOOPED) as i:
                for s in range(2):
                    step(2 * i + (1 + s), (1 + s) % 2, F, False, conv, i)
            done[0] += CHUNKS_TURN * LOOPED
            for s in range(2):
                step(2 * LOOPED + 1 + s, (1 + s) % 2, F, False, conv, None)

        def dve_prep(dve, b, scale):
            r = info[b]["prep"]
            g0 = GAIN_ROW.get(b, 0)

            def low(i):
                dve.wait_ge(xh_new, r["xg0"] + i + 1)
                for e in range(2):
                    t = 2 * i + e
                    last = nc.vector.scalar_tensor_tensor(xl[:, t, :], x[:, t, :], vecs[:, g0 + t:g0 + t + 1],
                                                          xh[:, t, :].bitcast(F32), ALU.mult, ALU.subtract)
                last.then_inc(xg_new, 1)

            for i in range(4):
                xs = x[:, 2 * i:2 * i + 2, :]
                if r["kind"] == "add":
                    kind, val = r["y"][i]
                    dve.wait_ge(y_bank if kind == "y" else chunk_mul, val)
                    y = bank[4 + i][:, :].rearrange("p (e t) -> p e t", e=2)
                    if scale is None:
                        nc.vector.tensor_copy(xs, y).then_inc(x_new, 1)
                    else:
                        nc.vector.scalar_tensor_tensor(xs, y, scale, xs, ALU.mult, ALU.add).then_inc(x_new, 1)
                elif r["kind"] == "final":
                    for e in range(2):
                        t = 2 * i + e
                        last = nc.vector.scalar_tensor_tensor(x[:, t, :], x[:, t, :],
                                                              vecs[:, GAIN_ROW["final"] + t:GAIN_ROW["final"] + t + 1],
                                                              rs_b[:, :], ALU.mult, ALU.mult)
                    last.then_inc(x_new, 1)
                if r["kind"] == "add" and r["y"][i][0] == "c" and i < 3:
                    lo_until(dve, r["y"][i][1] + 2)
                if i >= 1 and b not in ("final", "end") and scale is not None and not outputs_in_xh(r):
                    low(i - 1)
            if scale is None:
                lo_until(dve, 0)
            if b not in ("final", "end"):
                for i in range(0 if scale is None or outputs_in_xh(r) else 3, 4):
                    low(i)
            if b not in ("final", "end"):
                lo_until(dve, info[b]["c0"] + 2)
            if b == "end" or r["kind"] == "regain":
                return
            dve.wait_ge(sq_new, r["sq0"] + 4)
            s0 = 2 * r["st"]
            nc.vector.tensor_tensor(ssum[:, 0:4, :], sq[:, 0:4, :], sq[:, 4:8, :], ALU.add).then_inc(sum_step, 1)
            dve.wait_ge(sum_step, s0 + 1)
            nc.vector.tensor_tensor(ssum[:, 4:6, :], ssum[:, 0:2, :], ssum[:, 2:4, :], ALU.add).then_inc(sum_step, 1)
            dve.wait_ge(sum_step, s0 + 2)
            nc.vector.tensor_tensor(ssq[:, :], ssum[:, 4, :], ssum[:, 5, :], ALU.add).then_inc(ssq_new, 1)

        def dve_rs(dve, b):
            st = info[b]["st"]
            dve.wait_ge(std_new, st)
            nc.vector.reciprocal(rs_c[:, :], std_c[:, :])
            nc.vector.reciprocal(rs_b[:, :], std_b[:, :]).then_inc(rs_new, 1)
            dve.wait_ge(rs_new, st)

        def outputs_in_xh(r):
            return r["kind"] == "add" and r["y"][0][0] == "c"

        def act_prep(act, b):
            r = info[b]["prep"]
            if outputs_in_xh(r):
                hi_until(act, r["y"][2][1] + 2 if b != "end" else total_chunks - 1)
            if b == "end":
                return
            g0 = GAIN_ROW.get(b, 0)
            if b != "final" and r["kind"] != "final" and info[b]["c0"] > 0:
                act.wait_ge(chunk_mul, info[b]["c0"] - (2 if r["kind"] == "add" and not outputs_in_xh(r) else 0))
            if b == plan[0]:
                hi_until(act, 0)
            for i in range(4):
                if r["kind"] != "regain":
                    act.wait_ge(x_new, r["x0"] + i + 1)
                if b == "final":
                    nc.scalar.activation(sq[:, 2 * i:2 * i + 2, :], x[:, 2 * i:2 * i + 2, :], ACT.Square).then_inc(sq_new, 1)
                    continue
                for e in range(2):
                    t = 2 * i + e
                    last = nc.scalar.activation(xh[:, t, :], x[:, t, :], ACT.Copy, scale=vecs[:, g0 + t:g0 + t + 1])
                last.then_inc(xh_new, 1)
            if b != "final":
                hi_until(act, info[b]["c0"] + 2)
            if r["kind"] == "regain":
                return
            for i in range(4 if b != "final" else 0):
                nc.scalar.activation(sq[:, 2 * i:2 * i + 2, :], x[:, 2 * i:2 * i + 2, :], ACT.Square).then_inc(sq_new, 1)
            act.wait_ge(stat_new, r["st"] + 1)
            nc.scalar.activation(std_c[:, :], bank[7][:, T:T + 2], ACT.Sqrt, bias=eps_c[:, :])
            nc.scalar.activation(std_b[:, :], bank[7][:, 0:T], ACT.Sqrt, bias=eps_c[:, :]).then_inc(std_new, 1)


        def make_even():
            top[0] = 0
            SQ, SK, NQ = take(4, T), take(4, T), take(4, T)
            KD = take(4, T)
            KRAW, KCR = take(2, T), take(16)
            KCV = take(2, T)
            SV = take(2, 512)
            VSW = take(2, 2, P)
            GT = take(2, 24)
            CW_ = take(2, 2048)
            BLK = take(2, 32, 16)
            PE_ = take(P)
            PEK = take(2, 32)
            KC = take(2, 16)
            VC = take(2, DH)
            RT = take(2, T)
            m0 = top[0]
            LK, AZ = take(8, 384), take(8, 384)
            top[0] = m0
            att = [take(1, 384) for _ in range(6)]
            pt = [take(384) for _ in range(3)]
            NM, RR = take(4, 2), take(4, 4)
            CS, CP = take(16, 16), take(16, 16)
            CM, CD = take(16), take(16)
            PTC = take(8, T)
            top[0] = max(top[0], m0 + 2 * 8 * 384)
            consts, C, const_in = block_consts("even")
            ONES = take(P)
            pj_fm, pj_tm = sem("ev_fm"), sem("ev_tm")
            cmp_in = sem("ev_cmp_in")
            pos_t, pos_ok = sem("ev_pos_t"), sem("ev_pos_ok")
            rot_mm, rope = sem("ev_rot_mm"), sem("ev_rope")
            blk_ok, comp = sem("ev_blk"), sem("ev_comp")
            kc_raw, vc_ok = sem("ev_kc_raw"), sem("ev_vc")
            z_mm, z_abs, z_exp, z_ln, lk_ok = sem("sb_z"), sem("sb_abs"), sem("sb_exp"), sem("sb_ln"), sem("sb_lk")
            sp_ok, a_mm, am_ok, a_ok = sem("sb_sp"), sem("sb_a_mm"), sem("sb_am"), sem("sb_a")
            sb_pv, sb_o, sb_ol = sem("sb_pv"), sem("sb_o"), sem("sb_ol")
            c_qk, c_v, c_e, c_p = sem("cm_qk"), sem("cm_v"), sem("cm_e"), sem("cm_p")
            c_t, c_pt = sem("cm_t"), sem("cm_pt")
            ones_ok = sem("ev_ones")
            n0 = info["even"]["c0"]
            gone = []
            v = a = 0
            for m in ["fm"] * 4 + ["tm"] * 2 + ["fm"] * 2 + ["fm", "mix", "mix", "tm"]:
                if m == "tm":
                    a += 1
                else:
                    v += 1
                    if m == "mix":
                        a += 1
                gone.append((v, a))
            units = []
            for h in range(8):
                g, pb = h // 4, (h % 2) * DH
                for br in range(2):
                    un = {"pair": h // 2, "pb": pb, "first": br == 0, "last": br == 1,
                          "gate": GT[:, :, 3 * h + 1 + br],
                          "subs": [{"q": NQ[pb:pb + DH, h // 2, :], "k": KD[pb:pb + DH, 2 * br + g, :],
                                    "v": [VSW[:, br, t, g * DH:(g + 1) * DH] for t in range(2)],
                                    "add": C["causal"][:, :]}]}
                    if br == 1:
                        un["cmp"] = (VC[0:N_CMP, g, :], PTC[0:N_CMP, h, :])
                    units.append(un)
            soft = Soft("nsa", units, 1, att, pt, NM, RR,
                        lambda p, y: (xh[:, 4 + p, :], xl[:, 4 + p, :], y))

            ropes = [(NQ[:, t, :], NQ[:, t, :], T, None) for t in range(4)]
            ropes += [(KRAW[:, t // 2, :], KD[:, t, :], T, t % 2) for t in range(4)]
            ropes += [(KCR[:, 0:N_CMP], KC[:, g, 0:N_CMP], N_CMP, g) for g in range(2)]
            sb_heads = [4, 5, 6, 7, 0, 1, 2, 3]

            def pe_part(pe):
                for c in range(12):
                    if c == 1:
                        pe_stats(pe, "even")
                    if c >= 4:
                        vv, aa = gone[c - 4]
                        pe.wait_ge(pj_fm, vv)
                        if aa:
                            pe.wait_ge(pj_tm, aa)
                    B = bank[c % 4]
                    if c in (9, 10):
                        wait_split(pe, n0 + c)
                        wh, wl = slot(n0 + c, of=hi), slot(n0 + c, of=lo)
                        for k in range(KT):
                            product(B[:, 0:T], wh[:, k, 0:P], wl[:, k, 0:P], xh[:, k, :], xl[:, k, :],
                                    k == 0, k == KT - 1)
                        for t in range(2):
                            tt = slice(t * P, (t + 1) * P)
                            for k in range(KT):
                                last = product(bank[4 + c - 9][:, t * T:(t + 1) * T], xh[:, k, tt], xl[:, k, tt],
                                               wh[:, k, :], wl[:, k, :], k == 0, k == KT - 1)
                        last.then_inc(chunk_mul, 1)
                    elif c == 11:
                        pe_chunk(pe, n0 + c, B, "tm", 24)
                    else:
                        pe_chunk(pe, n0 + c, B, "tm" if c in (4, 5) else "fm", first=first_xg("even") if c == 0 else None)
                pe.wait_ge(cmp_in, 16 * 6)
                nc.tensor.transpose(bank[6][:, 0:32], PE_[0:32, :], ident[0:32, 0:32]).then_inc(pos_t, 1)
                pe.wait_ge(pos_ok, 1)
                nc.tensor.transpose(bank[6][:, 0:32], PE_[32:64, :], ident[32:64, 32:64]).then_inc(pos_t, 1)
                pe.wait_ge(blk_ok, 4)
                pe.wait_ge(pos_ok, 2)
                for g in range(2):
                    r = slice(g * DH, (g + 1) * DH)
                    for l in range(32):
                        last = nc.tensor.matmul(bank[6][r, 0:N_CMP], CW_[r, 0, l * DH:(l + 1) * DH],
                                                BLK[r, 0, l, 0:N_CMP], start=l == 0, stop=l == 31)
                for g in range(2):
                    r = slice(g * DH, (g + 1) * DH)
                    for l in range(32):
                        last = nc.tensor.matmul(bank[6 + g][0:N_CMP, 64:64 + DH],
                                                BLK[r, 1, l, 0:N_CMP], CW_[r, 1, l * DH:(l + 1) * DH],
                                                start=l == 0, stop=l == 31)
                last.then_inc(comp, 1)
                pe.wait_ge(const_in, 16)
                pe.wait_ge(pj_fm, gone[11][0])
                pe.wait_ge(pj_tm, gone[11][1])
                pe.wait_ge(kc_raw, 1)
                def sb_scores(h):
                    pb = (h % 2) * DH
                    k, q, B = SK[pb:pb + DH, h // 2, :], SQ[pb:pb + DH, h // 2, :], bank[h]
                    nc.tensor.matmul(B[:, 0:T], k[:, 0:P], q, start=True, stop=False, skip_group_check=True)
                    nc.tensor.matmul(B[:, T:384], k[:, P:T], q[:, P:T], start=False, stop=False,
                                     skip_group_check=True).then_inc(z_mm, 1)

                for i, (src, buf, n, g) in enumerate(ropes):
                    if i >= 4:
                        if i == 4:
                            pe.wait_ge(vc_ok, 2)
                        if i < 8:
                            sb_scores(sb_heads[i - 4])
                        pe.wait_ge(rope, 3 * (i - 4) + 2)
                    rot = C["rot"][:, :]
                    if g is not None:
                        rot = C["rotdup"][:, g * P:(g + 1) * P]
                        nc.tensor.matmul(bank[i % 4][:, T:T + n], C["dup"][:, g * P:(g + 1) * P], src,
                                         start=True, stop=True)
                    nc.tensor.matmul(bank[i % 4][:, 0:n], rot, src, start=True, stop=True).then_inc(rot_mm, 1)
                pe.wait_ge(ones_ok, 1)
                pe.wait_ge(rope, 3 * len(ropes))
                for h in sb_heads[4:]:
                    sb_scores(h)
                for i, h in enumerate(sb_heads):
                    pe.wait_ge(lk_ok, i + 1)
                    B, L = bank[h], LK[:, h, :]
                    nc.tensor.matmul(B[:, 0:T], C["suffix"][:, :], L[:, 0:T], start=False, stop=False,
                                     skip_group_check=True)
                    nc.tensor.matmul(B[:, T:384], C["suffix"][:, :], L[:, T:384], start=False, stop=False,
                                     skip_group_check=True)
                    nc.tensor.matmul(B[:, P:T], ONES[:, :], L[:, T:384], start=False, stop=True,
                                     skip_group_check=True).then_inc(a_mm, 1)
                for i, h in enumerate(sb_heads):
                    pb = (h % 2) * DH
                    pe.wait_ge(a_ok, i + 1)
                    O, L = bank[h - h % 2][pb:pb + DH, :], LK[:, h, :]
                    nc.tensor.matmul(O[:, 0:T], SV[:, 0, h * DH:(h + 1) * DH], L[:, 0:T], start=True, stop=False,
                                     skip_group_check=True)
                    nc.tensor.matmul(O[:, P:T], SV[:, 1, h * DH:(h + 1) * DH], L[:, T:384], start=False, stop=True,
                                     skip_group_check=True).then_inc(sb_pv, 1)
                pe.wait_ge(sb_ol, 4)
                for h in range(8):
                    pb = (h % 2) * DH
                    for t in range(2):
                        o = (2 * (h // 2) + t) * 16
                        last = nc.tensor.matmul(bank[5 - h % 2][:, o:o + N_CMP],
                                                NQ[pb:pb + DH, h // 2, t * P:(t + 1) * P], KC[pb:pb + DH, h // 4, 0:N_CMP],
                                                start=True, stop=True)
                last.then_inc(c_qk, 1)
                pe.wait_ge(c_p, 1)
                for h in range(8):
                    for t in range(2):
                        last = nc.tensor.transpose(bank[h // 2][0:N_CMP, (h % 2) * T + t * P:(h % 2) * T + (t + 1) * P],
                                                   CP[:, 8 * (h % 2) + 2 * (h // 2) + t, 0:N_CMP], ident[:, :])
                last.then_inc(c_t, 1)
                pe.wait_ge(c_pt, 4)
                soft_pe(pe, soft)
                pe_residual(pe, "even", n0 + 12, lambda k: pe.wait_ge(soft.o, k - 3) if k >= 4 else None)

            def dve_part(dve):
                dve.wait_ge(const_in, 16)
                nc.vector.memset(ONES[:, :], 1.0).then_inc(ones_ok, 1)

                def rs2(n=2):
                    return rs_b[:, :].unsqueeze(1).broadcast_to([P, n, T])

                for c in range(11):
                    lo_until(dve, n0 + c + 2)
                    if c in (4, 5):
                        continue
                    dve.wait_ge(chunk_mul, n0 + c + 1)
                    B = bank[c % 4][:, :].rearrange("p (e t) -> p e t", e=2)
                    if c in (0, 1, 6, 7):
                        dst, s = (SQ if c < 2 else NQ)[:, 2 * (c % 2):2 * (c % 2) + 2, :], DH ** -0.5
                    elif c < 4:
                        dst, s = SK[:, 2 * (c - 2):2 * (c - 2) + 2, :], 1.0
                    elif c == 8:
                        dst, s = KCV, 1.0
                    else:
                        nc.vector.tensor_tensor(KRAW[:, c - 9, :], B[:, 0, :], rs_b[:, :], ALU.mult).then_inc(pj_fm, 1)
                        continue
                    nc.vector.scalar_tensor_tensor(dst, B, s, rs2(), ALU.mult, ALU.mult).then_inc(pj_fm, 1)
                lo_until(dve, n0 + 14)
                for i in range(2):
                    dve.wait_ge(pos_t, i + 1)
                    nc.vector.tensor_copy(PEK[:, i, :], bank[6][:, 0:32]).then_inc(pos_ok, 1)
                dve.wait_ge(pos_ok, 2)
                dve.wait_ge(pj_fm, 7)
                for i in range(2):
                    kv = KCV[:, i, :].rearrange("p (c l) -> p l c", l=16)
                    for hf in range(2):
                        pe_b = PEK[:, i, 16 * hf:16 * hf + 16].unsqueeze(2).broadcast_to([P, 16, N_CMP])
                        nc.vector.tensor_tensor(BLK[:, i, 16 * hf:16 * hf + 16, 0:N_CMP], kv[:, :, hf:hf + N_CMP], pe_b,
                                                ALU.add).then_inc(blk_ok, 1)
                dve.wait_ge(comp, 1)
                for g in range(2):
                    nc.vector.tensor_copy(VC[0:N_CMP, g, :], bank[6 + g][0:N_CMP, 64:64 + DH]).then_inc(vc_ok, 1)
                nc.vector.tensor_copy(KCR[:, 0:N_CMP], bank[6][:, 0:N_CMP]).then_inc(kc_raw, 1)
                for i, (src, buf, n, g) in enumerate(ropes):
                    cos, sin = C["cos"][:, :], C["sin"][:, :]
                    if n != T:
                        cos = cos.rearrange("p (c l) -> p c l", l=16)[:, 1:16, 15]
                        sin = sin.rearrange("p (c l) -> p c l", l=16)[:, 1:16, 15]
                    dve.wait_ge(rot_mm, i + 1)
                    t = RT[:, i % 2, 0:n]
                    nc.vector.tensor_tensor(t, bank[i % 4][:, 0:n], sin, ALU.mult).then_inc(rope, 1)
                    nc.vector.tensor_tensor(buf, src if g is None else bank[i % 4][:, T:T + n], cos,
                                            ALU.mult).then_inc(rope, 1)
                    dve.wait_ge(rope, 3 * i + 2)
                    nc.vector.tensor_tensor(buf, buf, t, ALU.add).then_inc(rope, 1)
                for i, h in enumerate(sb_heads):
                    dve.wait_ge(z_ln, i // 2 + 1)
                    nc.vector.scalar_tensor_tensor(LK[:, h, :], bank[h][:, 0:384], 0.0, AZ[:, h, :],
                                                   ALU.max, ALU.add).then_inc(sp_ok, 1)
                    dve.wait_ge(sp_ok, i + 1)
                    nc.vector.tensor_tensor(LK[:, h, :], LK[:, h, :], C["sb_negkeep"][:, :], ALU.mult).then_inc(lk_ok, 1)
                for i, h in enumerate(sb_heads):
                    dve.wait_ge(a_mm, i + 1)
                    nc.vector.tensor_tensor(LK[:, h, :], bank[h][:, 0:384], C["sb_bias"][:, :], ALU.add).then_inc(am_ok, 1)
                bias = C["cmp_bias"][:, :].rearrange("p (t c) -> p t c", t=2).unsqueeze(1).broadcast_to([P, 4, 2, N_CMP])
                keep = C["cmp_keep"][:, :].rearrange("p (t c) -> p t c", t=2).unsqueeze(1).broadcast_to([P, 8, 2, N_CMP])
                cs4 = CS[:, :, 0:N_CMP].rearrange("p (h t) c -> p h t c", t=2)
                cs, cp = CS[:, :, 0:N_CMP], CP[:, :, 0:N_CMP]

                def step(ins, n):
                    ins.then_inc(c_v, 1)
                    dve.wait_ge(c_v, n)

                for i, p in enumerate(h // 2 for h in sb_heads[::2]):
                    dve.wait_ge(sb_o, i + 1)
                    nc.vector.tensor_tensor(xl[:, p, :], bank[2 * p][:, 0:T], xh[:, p, :].bitcast(F32),
                                            ALU.subtract).then_inc(sb_ol, 1)
                dve.wait_ge(c_qk, 1)
                for par in range(2):
                    sc = bank[5 - par][:, 0:P].rearrange("p (h t c) -> p h t c", t=2, c=16)[:, :, :, 0:N_CMP]
                    last = nc.vector.tensor_tensor(cs4[:, 4 * par:4 * par + 4], sc, bias, ALU.add)
                step(last, 1)
                step(nc.vector.tensor_reduce(CM[:, :], cs, AXX, ALU.max), 2)
                step(nc.vector.tensor_tensor(cs, cs, CM[:, :].unsqueeze(2).broadcast_to([P, 16, N_CMP]),
                                             ALU.subtract), 3)
                dve.wait_ge(c_e, 1)
                step(nc.vector.tensor_tensor(cs4, cs4, keep, ALU.mult), 4)
                step(nc.vector.tensor_reduce(CD[:, :], cs, AXX, ALU.add), 5)
                step(nc.vector.tensor_scalar(CD[:, :], CD[:, :], 1.0, None, ALU.max), 6)
                step(nc.vector.reciprocal(CM[:, :], CD[:, :]), 7)
                for par in range(2):
                    gate = GT[:, :, :].rearrange("p t (h e b) -> p e h t b", e=2, b=3)[:, par, :, :, 0]
                    cm2 = CM[:, 8 * par:8 * par + 8].rearrange("p (h t) -> p h t", t=2)
                    last = nc.vector.tensor_tensor(cm2, cm2, gate, ALU.mult)
                step(last, 8)
                nc.vector.tensor_tensor(cp, cs, CM[:, :].unsqueeze(2).broadcast_to([P, 16, N_CMP]),
                                        ALU.mult).then_inc(c_p, 1)
                soft_dve(dve, soft)

            def act_part(act):
                act.dma_start(consts, A["consts_even"]).then_inc(const_in, 16)
                for i, w in enumerate(("cmp_w_k", "cmp_w_v")):
                    src = A[w].rearrange("(l d) e -> d l e", d=DH)
                    for hf in range(2):
                        act.dma_start(CW_[hf * DH:(hf + 1) * DH, i, :].rearrange("p (l e) -> p l e", e=DH),
                                      src).then_inc(cmp_in, 16)
                for i in range(2):
                    act.dma_start(PE_[32 * i:32 * i + 32, :], A["cmp_pos"][:, i * P:(i + 1) * P]).then_inc(cmp_in, 16)
                act.wait_ge(rs_new, info["even"]["st"])
                for c in (4, 5, 9, 10, 11):
                    hi_until(act, n0 + c + 2)
                    act.wait_ge(chunk_mul, n0 + c + 1)
                    for t in range(2):
                        if c < 6:
                            last = nc.scalar.activation(SV[:, t, (c - 4) * CW:(c - 3) * CW], bank[c % 4][:, t * CW:(t + 1) * CW],
                                                        ACT.Copy, scale=rs_c[:, t:t + 1])
                        elif c < 11:
                            last = nc.scalar.activation(VSW[:, c - 9, t, :], bank[4 + c - 9][:, t * T + P:(t + 1) * T],
                                                        ACT.Copy, scale=rs_c[:, t:t + 1])
                        else:
                            last = nc.scalar.activation(GT[:, t, :], bank[c % 4][:, t * CW:t * CW + 24],
                                                        ACT.Sigmoid, scale=rs_c[:, t:t + 1])
                    last.then_inc(pj_tm, 1)
                hi_until(act, n0 + 14)
                for i, h in enumerate(sb_heads):
                    act.wait_ge(z_mm, i + 1)
                    nc.scalar.activation(AZ[:, h, :], bank[h][:, 0:384], ACT.Abs).then_inc(z_abs, 1)
                    if i % 4 == 3:
                        act.wait_ge(z_abs, i + 1)
                        half = AZ[:, h - 3:h + 1, :]
                        nc.scalar.activation(half, half, ACT.Exp, scale=-1.0).then_inc(z_exp, 1)
                act.wait_ge(z_exp, 2)
                for p in (h // 2 for h in sb_heads[::2]):
                    two = AZ[:, 2 * p:2 * p + 2, :]
                    nc.scalar.activation(two, two, ACT.Ln, bias=one_c[:, :]).then_inc(z_ln, 1)
                for i, h in enumerate(sb_heads):
                    act.wait_ge(am_ok, i + 1)
                    nc.scalar.activation(LK[:, h, :], LK[:, h, :], ACT.Exp).then_inc(a_ok, 1)
                for i, p in enumerate(h // 2 for h in sb_heads[::2]):
                    act.wait_ge(sb_pv, 2 * i + 2)
                    nc.scalar.activation(xh[:, p, :], bank[2 * p][:, 0:T], ACT.Copy).then_inc(sb_o, 1)
                act.wait_ge(c_v, 3)
                cs = CS[:, :, 0:N_CMP]
                nc.scalar.activation(cs, cs, ACT.Exp).then_inc(c_e, 1)
                act.wait_ge(c_t, 1)
                for i in range(4):
                    nc.scalar.activation(PTC[0:N_CMP, 2 * i:2 * i + 2, :], bank[i][0:N_CMP, :].rearrange(
                        "p (h t) -> p h t", h=2), ACT.Copy).then_inc(c_pt, 1)
                soft_act(act, soft)

            return {"pe": pe_part, "dve": dve_part, "act": act_part}

        def make_fox():
            top[0] = 0
            Q, KF, V = take(8, T), take(8, T), take(2, D)
            SEL, CUM2, CQ = take(2048), take(T), take(2, 16)
            LF, AB, CUM, BF = take(T), take(T), take(T), take(1)
            D16 = take(P)
            att = [take(1, 384) for _ in range(6)]
            pt = [take(384) for _ in range(3)]
            NM, RR = take(4, 2), take(4, 4)
            consts, C, const_in = block_consts("fox")
            pj_fm, pj_tm = sem("fx_fm"), sem("fx_tm")
            small_in = sem("fx_small_in")
            f_lin, f_abs, f_log, f_cum = sem("fx_lin"), sem("fx_abs"), sem("fx_log"), sem("fx_cum")
            cum_t, cum_ok = sem("fx_cum_t"), sem("fx_cum_ok")
            n0 = info["fox"]["c0"]
            units = []
            for h in range(16):
                pb = (h % 2) * DH
                units.append({"pair": h // 2, "pb": pb, "first": True, "last": True,
                              "cq": [CQ[:, t, h:h + 1] for t in range(2)],
                              "cum": (SEL[pb:pb + DH, h * P:(h + 1) * P], CUM2[pb:pb + DH, :]),
                              "subs": [{"q": Q[pb:pb + DH, h // 2, :], "k": KF[pb:pb + DH, h // 2, :],
                                        "v": [V[:, t, h * DH:(h + 1) * DH] for t in range(2)],
                                        "add": C["causal"][:, :]}]})
            soft = Soft("fox", units, 1, att, pt, NM, RR, lambda p, y: (xh[:, p, :], xl[:, p, :], y))

            def pe_part(pe):
                for c in range(13):
                    if c == 2:
                        pe_stats(pe, "fox")
                    if c >= 4:
                        pe.wait_ge(pj_fm, min(c - 3, 9))
                        if c - 4 >= 9:
                            pe.wait_ge(pj_tm, c - 12)
                    pe_chunk(pe, n0 + c, bank[c % 4], "tm" if c >= 9 else "fm", 16 if c == 0 else CW,
                             first_xg("fox") if c == 0 else None)
                pe.wait_ge(f_cum, 1)
                pe.wait_ge(small_in, 16 * 3)
                nc.tensor.matmul(bank[4][:, 0:T], D16[0:16, :], CUM[0:16, :], start=True, stop=True).then_inc(cum_t, 1)
                for t in range(2):
                    last = nc.tensor.transpose(bank[5][:, t * 16:(t + 1) * 16], CUM[0:16, t * P:(t + 1) * P],
                                               ident[0:16, 0:16])
                last.then_inc(cum_t, 1)
                pe.wait_ge(cum_ok, 2)
                pe.wait_ge(pj_tm, 4)
                soft_pe(pe, soft)
                pe_residual(pe, "fox", n0 + 13, lambda k: pe.wait_ge(soft.o, k + 1))

            def dve_part(dve):
                dve.wait_ge(chunk_mul, n0 + 1)
                dve.wait_ge(small_in, 16 * 3)
                nc.vector.tensor_tensor(LF[0:16, :], bank[0][0:16, 0:T], rs_b[0:16, :], ALU.mult).then_inc(pj_fm, 1)
                dve.wait_ge(pj_fm, 1)
                nc.vector.tensor_scalar(LF[0:16, :], LF[0:16, :], BF[0:16, :], None, ALU.add).then_inc(f_lin, 1)
                rs2 = rs_b[:, :].unsqueeze(1).broadcast_to([P, 2, T])
                for c in range(1, 9):
                    lo_until(dve, n0 + c + 2)
                    dve.wait_ge(chunk_mul, n0 + c + 1)
                    B = bank[c % 4][:, :].rearrange("p (e t) -> p e t", e=2)
                    i = c - 1
                    dst, s = (Q[:, 2 * i:2 * i + 2, :], DH ** -0.5) if i < 4 else (KF[:, 2 * i - 8:2 * i - 6, :], 1.0)
                    nc.vector.scalar_tensor_tensor(dst, B, s, rs2, ALU.mult, ALU.mult).then_inc(pj_fm, 1)
                lo_until(dve, n0 + 15)
                dve.wait_ge(f_abs, 3)
                nc.vector.scalar_tensor_tensor(LF[0:16, :], LF[0:16, :], 0.0, AB[0:16, :], ALU.min,
                                               ALU.subtract).then_inc(f_log, 1)
                dve.wait_ge(f_log, 1)
                nc.vector.tensor_tensor_scan(CUM[0:16, :], one_c[0:16, :].broadcast_to([16, T]), LF[0:16, :], 0.0, ALU.mult,
                                             ALU.add).then_inc(f_cum, 1)
                dve.wait_ge(cum_t, 1)
                nc.vector.tensor_copy(CUM2[:, :], bank[4][:, 0:T]).then_inc(cum_ok, 1)
                dve.wait_ge(cum_t, 2)
                nc.vector.tensor_copy(CQ[:, :, :], bank[5][:, 0:32].rearrange("p (t h) -> p t h", t=2)).then_inc(cum_ok, 1)
                dve.wait_ge(cum_ok, 2)
                dve.wait_ge(const_in, 16)
                soft_dve(dve, soft)

            def act_part(act):
                act.dma_start(consts, A["consts_fox"]).then_inc(const_in, 16)
                act.dma_start(SEL[:, :], A["selneg"]).then_inc(small_in, 16)
                act.dma_start(BF[0:16, :], A["b_f"]).then_inc(small_in, 16)
                act.dma_start(D16[0:16, :], A["dup16"]).then_inc(small_in, 16)
                hi_until(act, n0 + 3)
                act.wait_ge(f_lin, 1)
                nc.scalar.activation(AB[0:16, :], LF[0:16, :], ACT.Abs).then_inc(f_abs, 1)
                act.wait_ge(f_abs, 1)
                nc.scalar.activation(AB[0:16, :], AB[0:16, :], ACT.Exp, scale=-1.0).then_inc(f_abs, 1)
                act.wait_ge(f_abs, 2)
                nc.scalar.activation(AB[0:16, :], AB[0:16, :], ACT.Ln, bias=one_c[0:16, :]).then_inc(f_abs, 1)
                act.wait_ge(rs_new, info["fox"]["st"])
                for c in range(9, 13):
                    hi_until(act, n0 + c + 2)
                    act.wait_ge(chunk_mul, n0 + c + 1)
                    for t in range(2):
                        last = nc.scalar.activation(V[:, t, (c - 9) * CW:(c - 8) * CW], bank[c % 4][:, t * CW:(t + 1) * CW],
                                                    ACT.Copy, scale=rs_c[:, t:t + 1])
                    last.then_inc(pj_tm, 1)
                hi_until(act, n0 + 15)
                soft_act(act, soft)

            return {"pe": pe_part, "dve": dve_part, "act": act_part}

        def make_hgrn():
            top[0] = 0
            FP, SG, KK, Q, GG = (take(8, T) for _ in range(5))
            LV = [take(8, T) for _ in range(2)]
            V = take(2, D)
            SA, SBt = take(8, T), take(8, P)
            LB, OML = take(8), take(8)
            OSQ, RN, OT = FP, LV[0], LV[1]
            consts, C, const_in = block_consts("hgrn")
            mean_e = take(P)
            mean_ok = sem("hg_mean_ok")
            pj_fm, pj_tm = sem("hg_fm"), sem("hg_tm")
            lb_d, lb_s, lb_o = sem("hg_lb_d"), sem("hg_lb_s"), sem("hg_lb_o")
            sig, gate, lnf, silu, cum = sem("hg_sig"), sem("hg_gate"), sem("hg_ln"), sem("hg_silu"), sem("hg_cum")
            d_k, d_q, l_e, l_k, l_q = sem("lv_dk"), sem("lv_dq"), sem("lv_exp"), sem("lv_k"), sem("lv_q")
            l_mm, l_s = sem("lv_mm"), sem("lv_s")
            o_h, o_l = sem("hg_o_h"), sem("hg_o_l")
            o_mm, o_sq, o_mean, o_rn, o_n, o_g = (sem("hg_o_mm"), sem("hg_o_sq"), sem("hg_o_mean"), sem("hg_o_rn"),
                                                  sem("hg_o_n"), sem("hg_o_g"))
            n0 = info["hgrn"]["c0"]
            st = info["hgrn"]["st"]
            blocks = [128, 64, 32, 16, 8, 4, 2, 1]
            groups = [("diag", 0, t, hh) for t in range(2) for hh in range(2)]
            groups += [("cross", 0, 1, hh) for hh in range(2)]
            groups += [("level", l, t, hh) for l in range(1, 8) for t in range(2) for hh in range(2)]
            by_level = [groups[0:4], groups[4:6]] + [groups[6 + 4 * l:10 + 4 * l] for l in range(7)]
            first_of = [0, 4] + [6 + 4 * l for l in range(7)]

            def level_pe(pe, l):
                if l == 0:
                    pe.wait_ge(silu, 4)
                    pe.wait_ge(gate, 16)
                else:
                    pe.wait_ge(l_k, l)
                    pe.wait_ge(l_q, l)
                for i, (kind, lv, t, hh) in enumerate(by_level[l]):
                    g = first_of[l] + i
                    if g >= 3:
                        pe.wait_ge(l_s, g - 2)
                    B = bank[4 + g % 3]
                    for k in range(4):
                        hd = 4 * hh + k
                        tt = slice(t * P, (t + 1) * P)
                        if kind == "diag":
                            lhs, rhs = KK[:, hd, tt], Q[:, hd, tt]
                        elif kind == "cross":
                            lhs, rhs = LV[0][:, hd, 0:P], LV[0][:, hd, P:T]
                        else:
                            lhs = rhs = LV[lv % 2][:, hd, tt]
                        last = nc.tensor.matmul(B[:, k * P:(k + 1) * P], lhs, rhs, start=True, stop=True)
                    last.then_inc(l_mm, 1)

            def pe_part(pe):
                done = 0
                for c in range(16):
                    if c == 2:
                        pe_stats(pe, "hgrn")
                    if c >= 4:
                        pe.wait_ge(pj_fm, min(c - 3, 12))
                    pe_chunk(pe, n0 + c, bank[c % 4], "tm" if c >= 12 else "fm",
                             first=first_xg("hgrn") if c == 0 else None)
                    if c >= 9 and done < 9:
                        level_pe(pe, done)
                        done += 1
                for l in range(done, 9):
                    level_pe(pe, l)
                pe.wait_ge(pj_tm, 4)
                pe.wait_ge(l_s, len(groups))
                pe.wait_ge(mean_ok, 1)
                for p in range(4):
                    for e in range(2):
                        hd = 2 * p + e
                        o = bank[p][:, e * T:(e + 1) * T]
                        nc.tensor.matmul(o, V[:, 0, hd * P:(hd + 1) * P], SA[:, hd, :], start=True, stop=False)
                        last = nc.tensor.matmul(o[:, P:T], V[:, 1, hd * P:(hd + 1) * P], SBt[:, hd, :], start=False,
                                                stop=True)
                    last.then_inc(o_mm, 1)
                for p in range(4):
                    pe.wait_ge(o_sq, p + 1)
                    nc.tensor.matmul(bank[4 + p][:, :], mean_e[:, :], OSQ[:, 2 * p:2 * p + 2, :], start=True,
                                     stop=True).then_inc(o_mean, 1)
                pe_residual(pe, "hgrn", n0 + 16, lambda k: pe.wait_ge(o_l, k // 2 + 1))

            def dve_part(dve):
                rs2 = rs_b[:, :].unsqueeze(1).broadcast_to([P, 2, T])
                nc.vector.memset(mean_e[:, :], 1.0 / P).then_inc(mean_ok, 1)

                def evac(c):
                    lo_until(dve, n0 + c + 2)
                    dve.wait_ge(chunk_mul, n0 + c + 1)
                    B = bank[c % 4][:, :].rearrange("p (e t) -> p e t", e=2)
                    dst = (FP, Q, GG)[c // 4][:, 2 * (c % 4):2 * (c % 4) + 2, :]
                    nc.vector.tensor_tensor(dst, B, rs2, ALU.mult).then_inc(pj_fm, 1)

                nc.vector.tensor_tensor(LB[:, :], vecs[:, ROW_LB:ROW_LB + 8], vecs[:, ROW_LB + 8:ROW_LB + 16],
                                        ALU.subtract).then_inc(lb_d, 1)
                dve.wait_ge(lb_s, 1)
                nc.vector.tensor_scalar(OML[:, :], LB[:, :], -1.0, 1.0, ALU.mult, ALU.add).then_inc(lb_o, 1)
                dve.wait_ge(lb_o, 1)
                for c in range(4):
                    evac(c)
                for hd in range(8):
                    dve.wait_ge(sig, 2 * (hd // 2) + 2)
                    nc.vector.tensor_scalar(SG[:, hd, :], SG[:, hd, :], OML[:, hd:hd + 1], LB[:, hd:hd + 1], ALU.mult,
                                            ALU.add).then_inc(gate, 1)
                    nc.vector.tensor_scalar(KK[:, hd, :], KK[:, hd, :], OML[:, hd:hd + 1], None,
                                            ALU.mult).then_inc(gate, 1)
                for c in range(4, 8):
                    evac(c)
                dve.wait_ge(lnf, 1)
                for hd in range(8):
                    nc.vector.tensor_tensor_scan(FP[:, hd, :], one_c[:, :].broadcast_to([P, T]), SG[:, hd, :], 0.0, ALU.mult,
                                                 ALU.add).then_inc(cum, 1)
                dve.wait_ge(cum, 8)
                evac(8)

                def diff(l):
                    b, buf = blocks[l], LV[l % 2]
                    if l >= 2:
                        dve.wait_ge(l_mm, first_of[l])
                    cv = FP[:, :, :].rearrange("p h (n two b) -> p (h n) two b", two=2, b=b)
                    lv = buf[:, :, :].rearrange("p h (n two b) -> p (h n) two b", two=2, b=b)
                    ref = cv[:, :, 1, 0:1].broadcast_to([P, 8 * T // (2 * b), b])
                    nc.vector.tensor_tensor(lv[:, :, 0, :], ref, cv[:, :, 0, :], ALU.subtract).then_inc(d_k, 1)

                def keys(l):
                    b, buf = blocks[l], LV[l % 2]
                    dve.wait_ge(l_e, l + 1)
                    kv = KK[:, :, :].rearrange("p h (n two b) -> p (h n) two b", two=2, b=b)
                    lv = buf[:, :, :].rearrange("p h (n two b) -> p (h n) two b", two=2, b=b)
                    nc.vector.tensor_tensor(lv[:, :, 0, :], lv[:, :, 0, :], kv[:, :, 0, :], ALU.mult).then_inc(l_k, 1)

                def take_out(l):
                    for i, (kind, lv, t, hh) in enumerate(by_level[l]):
                        g = first_of[l] + i
                        dve.wait_ge(l_mm, g + 1)
                        B = bank[4 + g % 3][:, :].rearrange("p (h t) -> p h t", h=4)
                        hs = slice(4 * hh, 4 * hh + 4)
                        dst = SBt[:, hs, :] if t and kind != "cross" else SA[:, hs, 0:P]
                        m = C["level"][:, lv * P:(lv + 1) * P]
                        if kind == "diag":
                            ins = nc.vector.tensor_tensor(dst, B, m.unsqueeze(1).broadcast_to([P, 4, P]), ALU.mult)
                        elif kind == "cross":
                            ins = nc.vector.tensor_copy(SA[:, hs, P:T], B)
                        else:
                            ins = nc.vector.copy_predicated(dst, m.bitcast(U32).unsqueeze(1).broadcast_to([P, 4, P]), B)
                        ins.then_inc(l_s, 1)

                more = [9, 10, 11]
                dve.wait_ge(const_in, 16)
                diff(0)
                for l in range(8):
                    keys(l)
                    if more:
                        evac(more.pop(0))
                    lo_until(dve, n0 + l + 11)
                    take_out(l)
                    if l + 1 < 8:
                        diff(l + 1)
                take_out(8)
                def outputs_low(p):
                    dve.wait_ge(o_h, p + 1)
                    two = slice(2 * p, 2 * p + 2)
                    nc.vector.tensor_tensor(xl[:, two, :], OT[:, two, :], xh[:, two, :].bitcast(F32),
                                            ALU.subtract).then_inc(o_l, 1)

                for p in range(4):
                    dve.wait_ge(o_rn, 5 + p)
                    dst = OT[:, 2 * p:2 * p + 2, :]
                    nc.vector.scalar_tensor_tensor(dst, bank[p][:, :].rearrange("p (e t) -> p e t", e=2),
                                                   vecs[:, ROW_OUT_GAIN:ROW_OUT_GAIN + 1], RN[:, 2 * p:2 * p + 2, :],
                                                   ALU.mult, ALU.mult).then_inc(o_n, 1)
                    dve.wait_ge(o_n, p + 1)
                    nc.vector.tensor_tensor(dst, dst, GG[:, 2 * p:2 * p + 2, :], ALU.mult).then_inc(o_g, 1)
                    if p >= 1:
                        outputs_low(p - 1)
                outputs_low(3)

            def act_part(act):
                act.dma_start(consts, A["consts_hgrn"]).then_inc(const_in, 16)
                hi_until(act, n0 + 2)
                act.wait_ge(lb_d, 1)
                nc.scalar.activation(LB[:, :], LB[:, :], ACT.Sigmoid).then_inc(lb_s, 1)
                for c in range(4):
                    hi_until(act, n0 + c + 3)
                    act.wait_ge(pj_fm, c + 1)
                    two = slice(2 * c, 2 * c + 2)
                    nc.scalar.activation(SG[:, two, :], FP[:, two, :], ACT.Sigmoid).then_inc(sig, 1)
                    nc.scalar.activation(KK[:, two, :], FP[:, two, :], ACT.Sigmoid, scale=-1.0).then_inc(sig, 1)
                act.wait_ge(gate, 15)
                nc.scalar.activation(SG[:, :, :], SG[:, :, :], ACT.Ln).then_inc(lnf, 1)
                for c in range(4):
                    hi_until(act, n0 + c + 7)
                    act.wait_ge(pj_fm, 5 + c)
                    nc.scalar.activation(Q[:, 2 * c:2 * c + 2, :], Q[:, 2 * c:2 * c + 2, :], ACT.Silu).then_inc(silu, 1)
                act.wait_ge(rs_new, st)

                def v_out(c):
                    act.wait_ge(chunk_mul, n0 + c + 1)
                    for t in range(2):
                        last = nc.scalar.activation(V[:, t, (c - 12) * CW:(c - 11) * CW],
                                                    bank[c % 4][:, t * CW:(t + 1) * CW], ACT.Copy, scale=rs_c[:, t:t + 1])
                    last.then_inc(pj_tm, 1)

                for l in range(8):
                    hi_until(act, n0 + l + 11)
                    act.wait_ge(d_k, l + 1)
                    act.wait_ge(d_q, l + 1)
                    nc.scalar.activation(LV[l % 2][:, :, :], LV[l % 2][:, :, :], ACT.Exp).then_inc(l_e, 1)
                    if 4 <= l:
                        v_out(12 + l - 4)
                act.wait_ge(pj_fm, 12)
                nc.scalar.activation(GG[:, :, :], GG[:, :, :], ACT.Silu).then_inc(silu, 1)
                for p in range(4):
                    act.wait_ge(o_mm, p + 1)
                    nc.scalar.activation(OSQ[:, 2 * p:2 * p + 2, :], bank[p][:, :].rearrange("p (e t) -> p e t", e=2),
                                         ACT.Square).then_inc(o_sq, 1)
                for p in range(4):
                    act.wait_ge(o_mean, p + 1)
                    nc.scalar.activation(RN[:, 2 * p:2 * p + 2, :], bank[4 + p][:, :].rearrange("p (e t) -> p e t", e=2),
                                         ACT.Ln, bias=eps_c[:, :]).then_inc(o_rn, 1)
                for p in range(4):
                    act.wait_ge(o_rn, p + 1)
                    nc.scalar.activation(RN[:, 2 * p:2 * p + 2, :], RN[:, 2 * p:2 * p + 2, :], ACT.Exp,
                                         scale=-0.5).then_inc(o_rn, 1)
                for p in range(4):
                    act.wait_ge(o_g, p + 1)
                    nc.scalar.activation(xh[:, 2 * p:2 * p + 2, :], OT[:, 2 * p:2 * p + 2, :], ACT.Copy).then_inc(o_h, 1)

            def pool_part(pool):
                for l in range(8):
                    b, buf = blocks[l], LV[l % 2]
                    cv = FP[:, :, :].rearrange("p h (n two b) -> p (h n) two b", two=2, b=b)
                    lv = buf[:, :, :].rearrange("p h (n two b) -> p (h n) two b", two=2, b=b)
                    qv = Q[:, :, :].rearrange("p h (n two b) -> p (h n) two b", two=2, b=b)
                    ref = cv[:, :, 1, 0:1].broadcast_to([P, 8 * T // (2 * b), b])
                    pool.wait_ge(cum, 8)
                    if l >= 2:
                        pool.wait_ge(l_mm, first_of[l])
                    nc.gpsimd.tensor_tensor(lv[:, :, 1, :], cv[:, :, 1, :], ref, ALU.subtract).then_inc(d_q, 1)
                    pool.wait_ge(silu, 4)
                    pool.wait_ge(l_e, l + 1)
                    nc.gpsimd.tensor_tensor(lv[:, :, 1, :], lv[:, :, 1, :], qv[:, :, 1, :], ALU.mult).then_inc(l_q, 1)

            return {"pe": pe_part, "dve": dve_part, "act": act_part, "pool": pool_part}

        def turned_round(v):
            return v.rearrange("p e (a b) -> p e a b", a=2)[:, :, :, ::-1]

        def make_head_norm(tag, dst, gain, tmp_sq, tmp_r, block_c, reverse=False):
            s = {k: sem(f"{tag}_{k}") for k in ("lin", "sqr", "mean", "log", "rec", "done")}
            n0, st = info[tag]["c0"], info[tag]["st"]
            consts, C, const_in = block_c

            def mean(pe, c):
                if c == 0:
                    pe.wait_ge(const_in, 16)
                pe.wait_ge(s["sqr"], c + 1)
                if c >= 2:
                    pe.wait_ge(s["log"], c - 1)
                nc.tensor.matmul(bank[4 + c % 2][:, :], C["block64"][:, :], tmp_sq[c % 2], start=True,
                                 stop=True).then_inc(s["mean"], 1)

            def pe_part(pe):
                for c in range(12):
                    if c == 1:
                        pe_stats(pe, tag)
                    if c >= 4:
                        pe.wait_ge(s["lin"], c - 3)
                    pe_chunk(pe, n0 + c, bank[c % 4], "fm", first=first_xg(tag) if c == 0 else None)
                    if c >= 1:
                        mean(pe, c - 1)

            def dve_norm(dve, k):
                for k in (k, k + 1):
                    dve.wait_ge(s["rec"], k + 1)
                    d2 = dst[:, 2 * k:2 * k + 2, :]
                    nc.vector.scalar_tensor_tensor(d2, d2, gain(k // 4), tmp_r[k % 2], ALU.mult,
                                                   ALU.mult).then_inc(s["done"], 1)

            def dve_part(dve):
                rs2 = rs_b[:, :].unsqueeze(1).broadcast_to([P, 2, T])
                for c in range(12):
                    lo_until(dve, n0 + c + 2)
                    dve.wait_ge(chunk_mul, n0 + c + 1)
                    B = bank[c % 4][:, :].rearrange("p (e t) -> p e t", e=2)
                    d2, r2 = dst[:, 2 * c:2 * c + 2, :], rs2
                    if reverse:
                        d2, B, r2 = turned_round(d2), *(v.rearrange("p e (a b) -> p e a b", a=2) for v in (B, rs2))
                    nc.vector.tensor_tensor(d2, B, r2, ALU.mult).then_inc(s["lin"], 1)
                    if c >= 3 and c % 2:
                        dve_norm(dve, c - 3)

            def act_norm(act, k0):
                for k in (k0, k0 + 1):
                    act.wait_ge(s["mean"], k + 1)
                    if k >= 2:
                        act.wait_ge(s["done"], k - 1)
                    nc.scalar.activation(tmp_r[k % 2], bank[4 + k % 2][:, :].rearrange("p (e t) -> p e t", e=2),
                                         ACT.Ln, bias=eps_c[:, :]).then_inc(s["log"], 1)
                for k in (k0, k0 + 1):
                    act.wait_ge(s["log"], k + 1)
                    nc.scalar.activation(tmp_r[k % 2], tmp_r[k % 2], ACT.Exp, scale=-0.5).then_inc(s["rec"], 1)

            def act_part(act):
                act.dma_start(consts, A["consts_" + tag]).then_inc(const_in, 16)
                for c in range(12):
                    hi_until(act, n0 + c + 2)
                    act.wait_ge(s["lin"], c + 1)
                    if c >= 2:
                        act.wait_ge(s["mean"], c - 1)
                    nc.scalar.activation(tmp_sq[c % 2], dst[:, 2 * c:2 * c + 2, :], ACT.Square).then_inc(s["sqr"], 1)
                    if c >= 2 and c % 2 == 0:
                        act_norm(act, c - 2)

            return s, mean, pe_part, dve_part, act_part, dve_norm, act_norm

        rel_rows = nc.dram_tensor("rel_rows", (16, 3 * 384), F32, kind="Internal").ap() if "kv" in plan else None
        rel_sent = sem("rel_sent") if "kv" in plan else None

        def make_kv():
            top[0] = F0
            tmp_sq, tmp_r = [take(2, T) for _ in range(2)], [take(2, T) for _ in range(2)]
            HOT, RM, RV, RB = take(3, 384), take(3, 384), take(3, 384), take(48)
            n0 = info["kv"]["c0"]
            s, mean, pe_n, dve_n, act_n, dve_norm, act_norm = make_head_norm(
                "kv", DK, lambda g: vecs[:, ROW_KG + g:ROW_KG + g + 1], tmp_sq, tmp_r, block_consts("kv"))
            small_in, rel_mm, rel_ok, v_ok = sem("kv_small_in"), sem("kv_rel_mm"), sem("kv_rel_ok"), sem("kv_v")

            def pe_part(pe):
                pe_n(pe)
                for c in range(12, 24):
                    if c < 16:
                        pe.wait_ge(s["lin"], c - 3)
                    else:
                        pe.wait_ge(v_ok, c - 15)
                    pe_chunk(pe, n0 + c, bank[c % 4], "tm")
                    if c == 12:
                        mean(pe, 11)
                    if 13 <= c < 16:
                        g = c - 13
                        if g == 0:
                            pe.wait_ge(small_in, 16 * 3)
                        if g == 2:
                            pe.wait_ge(rel_ok, 1)
                        nc.tensor.matmul(bank[6 + g % 2][0:16, 0:384], RB[0:32, 16 * g:16 * g + 16],
                                         HOT[0:32, g, :], start=True, stop=True).then_inc(rel_mm, 1)
                pe.wait_ge(v_ok, 12)
                pe.wait_ge(rel_ok, 3)

            def dve_part(dve):
                dve_n(dve)
                lo_until(dve, n0 + 14)
                dve_norm(dve, 10)
                dve.wait_ge(small_in, 16 * 3)
                for g in range(3):
                    lo_until(dve, n0 + 15 + g)
                    dve.wait_ge(rel_mm, g + 1)
                    nc.vector.tensor_tensor(RV[0:16, g, :], bank[6 + g % 2][0:16, 0:384], RM[0:16, g, :],
                                            ALU.add).then_inc(rel_ok, 1)
                lo_until(dve, n0 + 25)

            def act_part(act):
                act.dma_start(HOT[0:32, :, :], A["hot"].rearrange("b (g u) -> b g u", g=3)).then_inc(small_in, 16)
                act.dma_start(RM[0:16, :, :], A["rel_mask"].rearrange("b (g u) -> b g u", g=3)).then_inc(small_in, 16)
                act.dma_start(RB[0:32, :], A["rel_bias"]).then_inc(small_in, 16)
                act_n(act)
                hi_until(act, n0 + 14)
                act_norm(act, 10)
                act.wait_ge(rs_new, info["kv"]["st"])
                for c in range(12, 24):
                    hi_until(act, n0 + c + 2)
                    act.wait_ge(chunk_mul, n0 + c + 1)
                    for t in range(2):
                        last = nc.scalar.activation(DV[:, t, (c - 12) * CW:(c - 11) * CW],
                                                    bank[c % 4][:, t * CW:(t + 1) * CW], ACT.Copy, scale=rs_c[:, t:t + 1])
                    last.then_inc(v_ok, 1)
                    if c == 16:
                        act.wait_ge(rel_ok, 3)
                        act.dma_start(rel_rows.rearrange("h (g u) -> h g u", g=3), RV[0:16, :, :]).then_inc(rel_sent, 16)
                act.wait_ge(rel_sent, 16)

            return {"pe": pe_part, "dve": dve_part, "act": act_part}

        def make_dilated():
            top[0] = F0
            DQ = take(24, T)
            m0 = top[0]
            tmp_r = [take(2, T) for _ in range(2)]
            block_c = block_consts("dilated")
            m1 = m0 + 3 * 384
            top[0] = m1
            tmp_sq = [take(2, T) for _ in range(2)]
            top[0] = m0
            att2 = take(3, 384)
            pt = [take(384) for _ in range(3)]
            att = [take(3, 384), take(3, 384), att2]
            REL = [take(3, 384) for _ in range(2)]
            NM, RR, QG = take(4, 2), take(4, 4), take(3)

            def copies(p, y):
                h, l, y3 = xh[:, p:p + 1, :], xl[:, p:p + 1, :], y.unsqueeze(1)
                return turned_round(h)[:, 0], turned_round(l)[:, 0], y3.rearrange("p e (a b) -> p e a b", a=2)[:, 0]

            n0 = info["dilated"]["c0"]
            s, mean, pe_n, dve_n, act_n, dve_norm, act_norm = make_head_norm(
                "dilated", DQ, lambda g: QG[:, g:g + 1], tmp_sq, tmp_r, block_c, True)
            rel_in, qg_ok = [sem("dl_rel_in0"), sem("dl_rel_in1")], sem("dl_qg")
            units = []
            for h in range(16):
                pb = (h % 2) * DH
                units.append({"pair": h // 2, "pb": pb, "first": True, "last": True,
                              "ready": (s["done"], 9 + h // 4), "wait": (rel_in[h % 2], 32 * (h // 2 + 1)),
                              "subs": [{"q": DQ[pb:pb + DH, 8 * g + h // 2, :], "k": DK[pb:pb + DH, 8 * g + h // 2, :],
                                        "v": [DV[:, t, g * D + h * DH:g * D + (h + 1) * DH] for t in range(2)],
                                        "add": REL[h % 2][:, g, :]} for g in range(3)]})
            soft = Soft("dil", units, 3, att, pt, NM, RR, copies)

            def banks_free(pe):
                pe.wait_ge(s["lin"], 12)
                pe.wait_ge(s["log"], 12)

            def last_norm(dve):
                dve_norm(dve, 10)
                dve.wait_ge(s["done"], 12)

            soft.before["pe"] = {1: lambda pe: mean(pe, 11), 2: banks_free}
            soft.before["dve"] = {2: last_norm, 3: lambda dve: lo_until(dve, n0 + 14)}
            soft.before["act"] = {1: lambda act: act_norm(act, 10), 3: lambda act: hi_until(act, n0 + 14)}

            def pe_part(pe):
                pe_n(pe)
                pe.wait_ge(s["lin"], 11)
                soft_pe(pe, soft)
                pe_residual(pe, "dilated", n0 + 12, lambda k: pe.wait_ge(soft.o, k + 1))

            def dve_part(dve):
                nc.vector.tensor_scalar(QG[:, :], vecs[:, ROW_QG:ROW_QG + 3], DH ** -0.5, None, ALU.mult).then_inc(qg_ok, 1)
                dve.wait_ge(qg_ok, 1)
                dve_n(dve)
                soft_dve(dve, soft)

            def act_part(act):
                act_n(act)
                soft_act(act, soft)

            def pool_part(pool):
                pool.wait_ge(rel_sent, 16)
                pool.wait_ge(s["lin"], 1)
                for h in range(16):
                    if h >= 2:
                        pool.wait_ge(soft.masked, 3 * (h - 1))
                    for lo, n, u0 in ((0, T, 0), (T, P, P)):
                        src = bass.AP(tensor=rel_rows.tensor, offset=h * 1152 + u0, ap=[[1, P], [384, 3], [1, n]])
                        pool.dma_start(REL[h % 2][:, :, lo:lo + n], src).then_inc(rel_in[h % 2], 16)

            return {"pe": pe_part, "dve": dve_part, "act": act_part, "pool": pool_part}


        makers = {"even": make_even, "fox": make_fox, "hgrn": make_hgrn, "kv": make_kv, "dilated": make_dilated}
        parts = {b: makers[b]() for b in plan if b in makers}

        block = ctx.enter_context(nc.Block())

        @block.sync
        def _(sp):
            sp.dma_start(ident[:, :], A["ident"]).then_inc(first_in, 16)
            sp.dma_start(vec_in[0:VEC_ROWS, 0, :], A["vec_rows"]).then_inc(first_in, 16)
            for l in range(2):
                sp.dma_start(vec_in[0:CONV_ROWS, 1 + l, :], A["conv_rows"][l]).then_inc(first_in, 16)
            sp.dma_start(x_rows, A["x"].rearrange("(a p) d -> p a d", p=P)).then_inc(x_tok, 16)

            def free(n, it=None):
                if it is not None or n >= RING:
                    wait_split(sp, n - RING, it)

            def load_cols(n, w, c0, width, it=None):
                free(n, it)
                src = w.rearrange("(k p) n -> p k n", p=P)
                sp.dma_start(slot(n, width), src[:, :, bass.ds(c0, width)] if it is not None
                             else src[:, :, c0:c0 + width]).then_inc(chunk_in[n % RING], 16)

            def load_rows(n, w, j, it=None):
                free(n, it)
                src = w[bass.ds(j * CW, CW), :] if it is not None else w[j * CW:(j + 1) * CW, :]
                sp.dma_start(ring[n % RING][:, :].rearrange("p (k n) -> p k n", k=2),
                             src.rearrange("(k p) n -> p k n", p=P)).then_inc(chunk_in[n % RING], 16)

            for b in plan:
                n = info[b]["c0"]
                if b in ffn_in:
                    wi, wo = ffn_in[b], ffn_out[b]
                    load_cols(n, wi, 0, CW)
                    load_cols(n + 1, wi, DFF, CW)

                    def turn(i, m0, it):
                        for s in range(2):
                            m = m0 + 3 * s
                            load_cols(m, wi, i * (2 * CW) + CW * (1 + s), CW, it)
                            load_cols(m + 1, wi, i * (2 * CW) + (DFF + CW * (1 + s)), CW, it)
                            load_rows(m + 2, wo, i * 2 + s, it)

                    turn(0, n + 2, None)
                    with sp.Fori(1, LOOPED) as i:
                        turn(i, n + 2, i)
                    turn(LOOPED, n + 2 + CHUNKS_TURN * LOOPED, None)
                    load_rows(n + 3 * NJ - 1, wo, NJ - 1)
                else:
                    for c, (_, w, c0, width) in enumerate(streams[b]):
                        load_cols(n + c, W[w], c0, width)
            sp.wait_ge(out_sent, 16 * 2)

        @block.scalar
        def _(act):
            act.wait_ge(const_set, 1)
            act.wait_ge(vec_ok, 3)
            for b in plan:
                act_prep(act, b)
                if b in ffn_in:
                    ff_loop(act, lambda *a: act_ff_step(act, b, *a), b, done_hi)
                elif b in parts:
                    parts[b]["act"](act)
            act_prep(act, "end")
            for t in range(2):
                for h in range(2):
                    act.wait_ge(vec_t, 4 + 2 * t + h)
                    nc.scalar.activation(sq[:, 4 * t + 2 * h:4 * t + 2 * h + 2, :], bank[2 * t + h][:, :].rearrange(
                        "p (e t) -> p e t", e=2), ACT.Copy).then_inc(sq_new, 1)
                act.wait_ge(sq_new, info["end"]["prep"]["sq0"] + 2 * t + 2)
                act.dma_start(out[t * P:(t + 1) * P, :],
                              sq[:, 4 * t:4 * t + 4, :].rearrange("p k t -> p (k t)")).then_inc(out_sent, 16)

        @block.gpsimd
        def _(pool):
            for b in plan:
                n = info[b]["c0"]
                if b in ffn_in:
                    with pool.Fori(0, LOOPED) as i:
                        for s in range(2):
                            split_lo(pool, nc.gpsimd, n + 4 + 3 * s, i)
                    for c in range(n + 4 + CHUNKS_TURN * LOOPED, n + 3 * NJ):
                        if lo_by[c] == "P":
                            split_lo(pool, nc.gpsimd, c)
                elif b in parts:
                    for c in range(n, n + len(streams[b])):
                        if lo_by[c] == "P":
                            split_lo(pool, nc.gpsimd, c)
                    if "pool" in parts[b]:
                        parts[b]["pool"](pool)

        @block.tensor
        def _(pe):
            pe.wait_ge(first_in, 16 * 4)
            for l in range(3):
                rows = VEC_ROWS if l == 0 else CONV_ROWS
                last = nc.tensor.transpose(bank[l][:, 0:rows], vec_in[0:rows, l, :], ident[0:rows, 0:rows])
                last.then_inc(vec_t, 1)
            pe.wait_ge(x_tok, 16)
            for b in range(4):
                for e in range(2):
                    for t in range(2):
                        d = 2 * b + e
                        last = nc.tensor.transpose(bank[4 + b][:, e * T + t * P:e * T + (t + 1) * P],
                                                   x_rows[:, t, d * P:(d + 1) * P], ident[:, :])
                last.then_inc(y_bank, 1)
            pe.wait_ge(const_set, 3)
            for b in plan:
                if b in ffn_in:
                    pe_ffn(pe, b)
                elif b == "final":
                    pe_stats(pe, b)
                else:
                    parts[b]["pe"](pe)
            pe.wait_ge(x_new, info["end"]["prep"]["x0"] + 4)
            for t in range(2):
                for h in range(2):
                    for q in range(4):
                        d = 4 * h + q
                        last = nc.tensor.transpose(bank[2 * t + h][:, q * P:(q + 1) * P], x[:, d, t * P:(t + 1) * P],
                                                   ident[:, :])
                    last.then_inc(vec_t, 1)

        @block.vector
        def _(dve):
            nc.vector.memset(one_c[:, :], 1.0).then_inc(ff_read, 2)
            nc.vector.memset(eps_c[:, :], EPS).then_inc(const_set, 1)
            nc.vector.memset(mean_d[:, :], 1.0 / D).then_inc(const_set, 1)
            nc.vector.memset(zero16[:, :], 0.0).then_inc(const_set, 1)
            for l in range(3):
                rows = VEC_ROWS if l == 0 else CONV_ROWS
                dve.wait_ge(vec_t, l + 1)
                nc.vector.tensor_copy(vecs[:, :] if l == 0 else convv[:, l - 1, :],
                                      bank[l][:, 0:rows]).then_inc(vec_ok, 1)
            dve.wait_ge(vec_ok, 3)
            dve.wait_ge(const_set, 3)
            dve_prep(dve, plan[0], None)
            for pos, b in enumerate(plan):
                nxt = plan[pos + 1] if pos + 1 < len(plan) else "end"
                if info[b]["prep"]["kind"] != "regain":
                    dve_rs(dve, b)
                if b.startswith("conv"):
                    nc.vector.memset(ff_a[:, :, :, 0:2], 0.0)
                if b in ffn_in:
                    ff_loop(dve, lambda *a: dve_ff_step(dve, b, *a), b, done_lo)
                elif b in parts:
                    parts[b]["dve"](dve)
                dve_prep(dve, nxt, alpha(b))



ARENA = 25376


def lay_out(inputs):
    g = {k: np.asarray(v) for k, v in inputs.items()}
    arrays = {
        "x": g["x"].reshape(T, D),
        "ev_w_in": g["ev_w_in"][0], "ev_w_out": g["ev_w_out"][0], "od_w_in": g["od_w_in"][0],
        "od_w_out": g["od_w_out"][0], "a_w_in_2": g["a_w_in_2"][0], "a_w_out_2": g["a_w_out_2"][0],
        "w_kv_2": g["w_kv_2"], "b_w_q_2": g["b_w_q_2"][0], "b_w_o_2": g["b_w_o_2"][0],
        "ffn_w_in": g["ffn_w_in"], "ffn_w_out": g["ffn_w_out"], "ffn_w_in_2": g["ffn_w_in_2"],
        "ffn_w_out_2": g["ffn_w_out_2"], "cmp_w_k": g["ev_cmp_w_k"][0], "cmp_w_v": g["ev_cmp_w_v"][0],
        "cmp_pos": np.concatenate([g["ev_cmp_pos_k"][0]] * 2 + [g["ev_cmp_pos_v"][0]] * 2, 1),
        "b_f": g["od_b_f"].reshape(16, 1), "rel_bias": g["rel_bias_2"],
        "vec_rows": np.concatenate([
            g["attn_norm"].reshape(16, P), g["ffn_norm"].reshape(16, P), g["final_norm"].reshape(8, P),
            g["kv_norm_2"].reshape(8, P), g["norm_gain_2"].reshape(48, P), g["a_out_gain_2"].reshape(1, P),
            g["a_lb_logits_2"].reshape(16, P), np.concatenate([g["k_gain_2"]] * 2, 1),
            np.concatenate([g["b_q_gain_2"][0]] * 2, 1)], 0),
        "conv_rows": np.concatenate([g["ffn_conv_w"].reshape(2, 66, P), g["ffn_conv_b"].reshape(2, 22, P)], 1),
    }
    arrays.update(constants()[0])
    return {k: np.ascontiguousarray(v) for k, v in arrays.items()}


def kernel(**inputs):
    import concourse.bacc as _bacc
    from concourse.bass_utils import run_bass_kernel_spmd as _run

    nc = _bacc.Bacc("TRN2", target_bir_lowering=False, num_devices=1)
    arrays = {f"in_{k}": v for k, v in lay_out(inputs).items()}
    aps = {k[3:]: nc.dram_tensor(k, a.shape, mybir.dt.from_np(a.dtype), kind="ExternalInput").ap()
           for k, a in arrays.items()}
    out = nc.dram_tensor("out", (T, D), F32, kind="ExternalOutput").ap()
    build(nc, aps, out)
    r = _run(nc, [arrays], core_ids=[0])
    return r.results[0]["out"].reshape(1, T, D)
```
